# Optimizing a Trainium2 kernel written in Bass

```python
import jax, jax.numpy as jnp
from jax import lax
import numpy as np

D_MODEL = 1024
BATCH = 1
SEQ = 1024
DEPTH = 2
DEC_BATCH = 8
DEC_SEQ = 1
PAST_LEN = 256
PAGE_SIZE = 128

MLSTM_HEADS = 4
MLSTM_DV = D_MODEL // 2 // MLSTM_HEADS
MLSTM_DK = MLSTM_DV // 2
MLSTM_CHUNK = 128
FOX_HEADS = 8
FOX_DH = D_MODEL // 2 // FOX_HEADS
Q_BLOCK = 128
RWKV_DH = 64
RWKV_HEADS = D_MODEL // RWKV_DH
RWKV_DECAY_RANK = 64
RWKV_A_RANK = 64
RWKV_G_RANK = 128
FFN_HIDDEN = -(-8 * D_MODEL // (3 * 256)) * 256
EPS = 1e-6
GN_EPS = 64e-5
IN_SIZES = (MLSTM_HEADS * MLSTM_DK, MLSTM_HEADS * MLSTM_DK, MLSTM_HEADS * MLSTM_DV, MLSTM_HEADS * MLSTM_DV,
            MLSTM_HEADS, MLSTM_HEADS, FOX_HEADS * FOX_DH, FOX_HEADS * FOX_DH, FOX_HEADS * FOX_DH, FOX_HEADS)
IN_COLS = sum(IN_SIZES)
MIX_WIDTH = MLSTM_HEADS * MLSTM_DV + FOX_HEADS * FOX_DH

kernel_name = 'mlstm_fox_rwkv7_hybrid_step'

def rmsnorm(x, g):
    x32 = x.astype(jnp.float32)
    y = x32 * lax.rsqrt(jnp.mean(x32 * x32, axis=-1, keepdims=True) + EPS)
    return (y * g.astype(jnp.float32)).astype(x.dtype)

def swiglu(h, w_gate, w_up, w_down):
    return (jax.nn.silu(h @ w_gate) * (h @ w_up)) @ w_down

def mlstm_chunkwise(q, k, v, ig, lf, c0, n0, m0):
    B, T = q.shape[0], q.shape[1]
    L = min(MLSTM_CHUNK, T)
    nc = -(-T // L)
    pad = nc * L - T
    f32 = jnp.float32

    def blocks(a, fill):
        a = a.astype(f32)
        a = jnp.pad(a, [(0, 0), (0, pad)] + [(0, 0)] * (a.ndim - 2), constant_values=fill)
        a = a.reshape((B, nc, L) + a.shape[2:])
        return jnp.swapaxes(jnp.moveaxis(a, 1, 0), 2, 3)

    xs = (blocks(q, 0.0), blocks(k, 0.0), blocks(v, 0.0), blocks(ig, -jnp.inf), blocks(lf, 0.0))
    causal = jnp.tril(jnp.ones((L, L), dtype=bool))

    def step(carry, inp):
        c, n, m = carry
        qc, kc, vc, igc, lfc = inp
        b = jnp.cumsum(lfc, axis=-1)
        d = jnp.where(causal, b[..., :, None] - b[..., None, :] + igc[..., None, :], -jnp.inf)
        inter = b + m[..., None]
        m_t = jnp.maximum(inter, jnp.max(d, axis=-1))
        w_intra = jnp.exp(d - m_t[..., None])
        w_inter = jnp.exp(inter - m_t)
        s = jnp.einsum('bhtd,bhsd->bhts', qc, kc) * w_intra
        num = w_inter[..., None] * jnp.einsum('bhtd,bhde->bhte', qc, c) + jnp.einsum('bhts,bhse->bhte', s, vc)
        den = w_inter * jnp.einsum('bhtd,bhd->bht', qc, n) + jnp.sum(s, axis=-1)
        h = num / jnp.maximum(jnp.abs(den), jnp.exp(-m_t))[..., None]
        b_last = b[..., -1]
        g = b_last[..., None] - b + igc
        m_new = jnp.maximum(b_last + m, jnp.max(g, axis=-1))
        w_k = jnp.exp(g - m_new[..., None])
        decay = jnp.exp(b_last + m - m_new)
        c_new = decay[..., None, None] * c + jnp.einsum('bhs,bhsd,bhse->bhde', w_k, kc, vc)
        n_new = decay[..., None] * n + jnp.einsum('bhs,bhsd->bhd', w_k, kc)
        return (c_new, n_new, m_new), h

    (c, n, m), hs = lax.scan(step, (c0.astype(f32), n0.astype(f32), m0.astype(f32)), xs)
    hs = jnp.moveaxis(jnp.swapaxes(hs, 2, 3), 0, 1)
    hs = hs.reshape((B, nc * L) + hs.shape[3:])[:, :T]
    return hs, c, n, m

def fox_attention(q, k, v, fq, fk, q_pos):
    B, Tq, H, Dh = q.shape
    Tk = k.shape[1]
    qb = min(Q_BLOCK, Tq)
    nb = -(-Tq // qb)
    pad = nb * qb - Tq
    q = jnp.pad(q, ((0, 0), (0, pad), (0, 0), (0, 0)))
    fq = jnp.pad(fq, ((0, 0), (0, pad), (0, 0)))
    q_pos = jnp.pad(q_pos, (0, pad))
    qs = jnp.moveaxis(q.reshape(B, nb, qb, H, Dh), 1, 0)
    fqs = jnp.moveaxis(fq.reshape(B, nb, qb, H), 1, 0)
    ps = q_pos.reshape(nb, qb)
    fk_t = jnp.swapaxes(fk, 1, 2)
    key_pos = jnp.arange(Tk, dtype=jnp.int32)
    scale = Dh ** -0.5

    def block(args):
        qblk, fqblk, pblk = args
        s = jnp.einsum('bqhd,bkhd->bhqk', qblk, k).astype(jnp.float32) * scale
        s = s + jnp.swapaxes(fqblk, 1, 2)[..., None] - fk_t[:, :, None, :]
        s = jnp.where(key_pos[None, :] <= pblk[:, None], s, -jnp.inf)
        p = jax.nn.softmax(s, axis=-1)
        return jnp.einsum('bhqk,bkhd->bqhd', p.astype(v.dtype), v)

    out = lax.map(block, (qs, fqs, ps))
    return jnp.moveaxis(out, 0, 1).reshape(B, nb * qb, H, Dh)[:, :Tq]

def hybrid_mixer(h, w_in, i_bias, f_bias, out_g, fox_bias, w_out, c0, n0, m0, fox_past):
    B, T, _ = h.shape
    f32 = jnp.float32
    split_at = [int(i) for i in np.cumsum(IN_SIZES)[:-1]]
    mq, mk, mv, mo, mi, mf, fq, fk, fv, ff = jnp.split(h @ w_in, split_at, axis=-1)
    q = mq.reshape(B, T, MLSTM_HEADS, MLSTM_DK)
    k = mk.reshape(B, T, MLSTM_HEADS, MLSTM_DK) * (MLSTM_DK ** -0.5)
    v = mv.reshape(B, T, MLSTM_HEADS, MLSTM_DV)
    ig = mi.astype(f32) + i_bias.astype(f32)
    lf = jax.nn.log_sigmoid(mf.astype(f32) + f_bias.astype(f32))
    hm, c, n, m = mlstm_chunkwise(q, k, v, ig, lf, c0, n0, m0)
    hm = hm * lax.rsqrt(jnp.mean(hm * hm, axis=-1, keepdims=True) + EPS)
    hm = hm.reshape(B, T, MLSTM_HEADS * MLSTM_DV) * out_g.astype(f32) * jax.nn.sigmoid(mo.astype(f32))
    qf = fq.reshape(B, T, FOX_HEADS, FOX_DH)
    kf = fk.reshape(B, T, FOX_HEADS, FOX_DH)
    vf = fv.reshape(B, T, FOX_HEADS, FOX_DH)
    lff = jax.nn.log_sigmoid(ff.astype(f32) + fox_bias.astype(f32))
    if fox_past is None:
        k_all, v_all, lf_all, p0 = kf, vf, lff, 0
    else:
        kp, vp, lfp = fox_past
        k_all = jnp.concatenate([kp.astype(kf.dtype), kf], axis=1)
        v_all = jnp.concatenate([vp.astype(vf.dtype), vf], axis=1)
        lf_all = jnp.concatenate([lfp.astype(f32), lff], axis=1)
        p0 = kp.shape[1]
    cum = jnp.cumsum(lf_all, axis=1)
    hf = fox_attention(qf, k_all, v_all, cum[:, p0:], cum, p0 + jnp.arange(T, dtype=jnp.int32))
    mixed = jnp.concatenate([hm.astype(h.dtype), hf.reshape(B, T, FOX_HEADS * FOX_DH).astype(h.dtype)], axis=-1)
    dt = h.dtype
    return mixed @ w_out, (kf, vf, lff.astype(dt), c.astype(dt), n.astype(dt), m.astype(dt))

def wkv7_scan(r, w, k, v, a, b, s0):
    def step(S, inp):
        rt, wt, kt, vt, at, bt = inp
        S = (S * wt[:, :, None, :] + jnp.einsum('bhvk,bhk->bhv', S, at)[..., None] * bt[:, :, None, :]
             + vt[..., None] * kt[:, :, None, :])
        return S, jnp.einsum('bhvk,bhk->bhv', S, rt)

    xs = tuple(jnp.moveaxis(t.astype(jnp.float32), 1, 0) for t in (r, w, k, v, a, b))
    S, ys = lax.scan(step, s0.astype(jnp.float32), xs)
    return jnp.moveaxis(ys, 0, 1), S

def rwkv7_mixer(h, mix, w_r, w_k, w_v, w_o, w0, w1, w2, a0, a1, a2, g1, g2, k_k, k_a, r_k, ln_w, ln_b, s0, shift0):
    B, T, D = h.shape
    f32 = jnp.float32
    x_prev = jnp.concatenate([shift0[:, None, :].astype(h.dtype), h[:, :-1]], axis=1)
    xx = x_prev - h
    xr, xw, xk, xv, xa, xg = [h + xx * mix[i] for i in range(6)]
    r = xr @ w_r
    k = xk @ w_k
    v = xv @ w_v
    w_log = -jax.nn.softplus(-(w0 + jnp.tanh(xw @ w1) @ w2).astype(f32)) - 0.5
    decay = jnp.exp(-jnp.exp(w_log))
    a = jax.nn.sigmoid((a0 + (xa @ a1) @ a2).astype(f32))
    g = jax.nn.sigmoid(xg @ g1) @ g2
    heads = lambda t: t.reshape(B, T, RWKV_HEADS, RWKV_DH)
    kk = heads((k * k_k).astype(f32))
    kk = kk / jnp.maximum(jnp.sqrt(jnp.sum(kk * kk, axis=-1, keepdims=True)), 1e-12)
    k = k.astype(f32) * (1.0 + (a - 1.0) * k_a.astype(f32))
    rh, kh, vh, ah = heads(r.astype(f32)), heads(k), heads(v.astype(f32)), heads(a)
    y, s_new = wkv7_scan(rh, heads(decay), kh, vh, -kk, kk * ah, s0)
    mu = jnp.mean(y, axis=-1, keepdims=True)
    var = jnp.mean(jnp.square(y - mu), axis=-1, keepdims=True)
    y = ((y - mu) * lax.rsqrt(var + GN_EPS)).reshape(B, T, D) * ln_w.astype(f32) + ln_b.astype(f32)
    bonus = jnp.sum(rh * kh * r_k.astype(f32), axis=-1, keepdims=True) * vh
    y = (y + bonus.reshape(B, T, D)) * g.astype(f32)
    return y.astype(h.dtype) @ w_o, (s_new.astype(h.dtype), h[:, -1])

def setup_inputs(seed: int = 0) -> dict:
    key = jax.random.key(seed)
    ks = iter(jax.random.split(key, 64))
    nrm = lambda shape, scale: scale * jax.random.normal(next(ks), shape, jnp.float32)
    uni = lambda shape, lo, hi: jax.random.uniform(next(ks), shape, jnp.float32, lo, hi)
    n_even, n_odd = (DEPTH + 1) // 2, DEPTH // 2
    n_pages = PAST_LEN // PAGE_SIZE
    n_used = DEC_BATCH * n_pages
    n_phys = n_used + max(1, n_used // 4)
    D = D_MODEL
    page_table = jax.random.permutation(next(ks), n_phys)[:n_used].reshape(DEC_BATCH, n_pages).astype(jnp.int32)
    return {
        'x_prompt': nrm((BATCH, SEQ, D), 1.0),
        'x_sample': nrm((DEC_BATCH, DEC_SEQ, D), 1.0),
        'cache_fox_k': nrm((n_even, n_phys, PAGE_SIZE, FOX_HEADS, FOX_DH), 1.0),
        'cache_fox_v': nrm((n_even, n_phys, PAGE_SIZE, FOX_HEADS, FOX_DH), 1.0),
        'cache_fox_lf': jax.nn.log_sigmoid(3.0 + nrm((n_even, n_phys, PAGE_SIZE, FOX_HEADS), 1.0)),
        'state_mlstm_c': nrm((n_even, DEC_BATCH, MLSTM_HEADS, MLSTM_DK, MLSTM_DV), 0.5),
        'state_mlstm_n': nrm((n_even, DEC_BATCH, MLSTM_HEADS, MLSTM_DK), 0.5),
        'state_mlstm_m': nrm((n_even, DEC_BATCH, MLSTM_HEADS), 1.0),
        'state_rwkv_s': nrm((n_odd, DEC_BATCH, RWKV_HEADS, RWKV_DH, RWKV_DH), 0.3),
        'state_rwkv_shift': nrm((n_odd, DEC_BATCH, D), 1.0),
        'page_table': page_table,
        'norm_g': 1.0 + nrm((DEPTH, 4, D), 0.05),
        'hyb_w_in': nrm((n_even, D, IN_COLS), D ** -0.5),
        'mlstm_i_bias': nrm((n_even, MLSTM_HEADS), 0.1),
        'mlstm_f_bias': uni((n_even, MLSTM_HEADS), 3.0, 6.0),
        'mlstm_out_g': 1.0 + nrm((n_even, MLSTM_HEADS * MLSTM_DV), 0.05),
        'fox_f_bias': uni((n_even, FOX_HEADS), 2.0, 5.0),
        'hyb_w_out': nrm((n_even, MIX_WIDTH, D), MIX_WIDTH ** -0.5),
        'rwkv_mix': uni((n_odd, 6, D), 0.0, 1.0),
        'rwkv_w_r': nrm((n_odd, D, D), D ** -0.5),
        'rwkv_w_k': nrm((n_odd, D, D), D ** -0.5),
        'rwkv_w_v': nrm((n_odd, D, D), D ** -0.5),
        'rwkv_w_o': nrm((n_odd, D, D), D ** -0.5),
        'rwkv_w0': -1.5 + nrm((n_odd, D), 0.5),
        'rwkv_w1': nrm((n_odd, D, RWKV_DECAY_RANK), D ** -0.5),
        'rwkv_w2': nrm((n_odd, RWKV_DECAY_RANK, D), 0.1 * RWKV_DECAY_RANK ** -0.5),
        'rwkv_a0': nrm((n_odd, D), 0.1),
        'rwkv_a1': nrm((n_odd, D, RWKV_A_RANK), D ** -0.5),
        'rwkv_a2': nrm((n_odd, RWKV_A_RANK, D), 0.5 * RWKV_A_RANK ** -0.5),
        'rwkv_g1': nrm((n_odd, D, RWKV_G_RANK), D ** -0.5),
        'rwkv_g2': nrm((n_odd, RWKV_G_RANK, D), RWKV_G_RANK ** -0.5),
        'rwkv_k_k': 0.85 + nrm((n_odd, D), 0.05),
        'rwkv_k_a': 1.0 + nrm((n_odd, D), 0.05),
        'rwkv_r_k': nrm((n_odd, RWKV_HEADS, RWKV_DH), 0.1),
        'rwkv_ln_w': 1.0 + nrm((n_odd, D), 0.05),
        'rwkv_ln_b': nrm((n_odd, D), 0.02),
        'ffn_w_gate': nrm((DEPTH, D, FFN_HIDDEN), D ** -0.5),
        'ffn_w_up': nrm((DEPTH, D, FFN_HIDDEN), D ** -0.5),
        'ffn_w_down': nrm((DEPTH, FFN_HIDDEN, D), FFN_HIDDEN ** -0.5),
    }

def reference(x_prompt, x_sample, cache_fox_k, cache_fox_v, cache_fox_lf, state_mlstm_c, state_mlstm_n,
              state_mlstm_m, state_rwkv_s, state_rwkv_shift, page_table, norm_g, hyb_w_in, mlstm_i_bias,
              mlstm_f_bias, mlstm_out_g, fox_f_bias, hyb_w_out, rwkv_mix, rwkv_w_r, rwkv_w_k, rwkv_w_v, rwkv_w_o,
              rwkv_w0, rwkv_w1, rwkv_w2, rwkv_a0, rwkv_a1, rwkv_a2, rwkv_g1, rwkv_g2, rwkv_k_k, rwkv_k_a, rwkv_r_k,
              rwkv_ln_w, rwkv_ln_b, ffn_w_gate, ffn_w_up, ffn_w_down):
    n_even, n_odd = (DEPTH + 1) // 2, DEPTH // 2

    def trunk(x, even_init, odd_init, fox_pasts):
        even_new, odd_new = [], []
        for l in range(DEPTH):
            h = rmsnorm(x, norm_g[l, 0])
            if l % 2 == 0:
                e = l // 2
                c0, n0, m0 = even_init[e]
                out, st = hybrid_mixer(h, hyb_w_in[e], mlstm_i_bias[e], mlstm_f_bias[e], mlstm_out_g[e],
                                       fox_f_bias[e], hyb_w_out[e], c0, n0, m0, fox_pasts[e])
                even_new.append(st)
            else:
                o = l // 2
                s0, sh0 = odd_init[o]
                out, st = rwkv7_mixer(h, rwkv_mix[o], rwkv_w_r[o], rwkv_w_k[o], rwkv_w_v[o], rwkv_w_o[o],
                                      rwkv_w0[o], rwkv_w1[o], rwkv_w2[o], rwkv_a0[o], rwkv_a1[o], rwkv_a2[o],
                                      rwkv_g1[o], rwkv_g2[o], rwkv_k_k[o], rwkv_k_a[o], rwkv_r_k[o],
                                      rwkv_ln_w[o], rwkv_ln_b[o], s0, sh0)
                odd_new.append(st)
            x = x + rmsnorm(out, norm_g[l, 1])
            h = rmsnorm(x, norm_g[l, 2])
            x = x + rmsnorm(swiglu(h, ffn_w_gate[l], ffn_w_up[l], ffn_w_down[l]), norm_g[l, 3])
        return x, even_new, odd_new

    bp, dt = x_prompt.shape[0], x_prompt.dtype
    p_even_init = [(jnp.zeros((bp, MLSTM_HEADS, MLSTM_DK, MLSTM_DV), dt), jnp.zeros((bp, MLSTM_HEADS, MLSTM_DK), dt),
                    jnp.zeros((bp, MLSTM_HEADS), dt)) for _ in range(n_even)]
    p_odd_init = [(jnp.zeros((bp, RWKV_HEADS, RWKV_DH, RWKV_DH), dt), jnp.zeros((bp, D_MODEL), dt))
                  for _ in range(n_odd)]
    y_prompt, pe, po = trunk(x_prompt, p_even_init, p_odd_init, [None] * n_even)

    def gather(pool):
        g = pool[page_table]
        return g.reshape((g.shape[0], g.shape[1] * g.shape[2]) + g.shape[3:])

    fox_pasts = [(gather(cache_fox_k[e]), gather(cache_fox_v[e]), gather(cache_fox_lf[e])) for e in range(n_even)]
    s_even_init = [(state_mlstm_c[e], state_mlstm_n[e], state_mlstm_m[e]) for e in range(n_even)]
    s_odd_init = [(state_rwkv_s[o], state_rwkv_shift[o]) for o in range(n_odd)]
    y_sample, se, so = trunk(x_sample, s_even_init, s_odd_init, fox_pasts)

    stk = lambda lst, i: jnp.stack([s[i] for s in lst])
    return (y_prompt, y_sample,
            stk(pe, 0), stk(pe, 1), stk(pe, 2), stk(pe, 3), stk(pe, 4), stk(pe, 5), stk(po, 0), stk(po, 1),
            stk(se, 0), stk(se, 1), stk(se, 2), stk(se, 3), stk(se, 4), stk(se, 5), stk(so, 0), stk(so, 1))


_drawn_inputs = setup_inputs


def setup_inputs(seed=0):
    import zlib

    import numpy as np

    out = dict(_drawn_inputs(seed))
    spreads = {}
    factors = {'rwkv_w1': 4.2, 'rwkv_w2': 4.344, 'rwkv_k_k': 3.18, 'rwkv_ln_b': 5.391}
    for name, (base, spread) in spreads.items():
        noise = np.random.default_rng([zlib.crc32(name.encode()), seed]).standard_normal(out[name].shape)
        drawn = base * np.exp(spread * noise) if base else spread * noise
        out[name] = __import__('jax').numpy.asarray(drawn.astype(out[name].dtype))
    for name, factor in factors.items():
        out[name] = (out[name] * factor).astype(out[name].dtype)
    return out
```

```python
import math
from contextlib import ExitStack

import numpy as np

import concourse.bass as bass
from concourse import mybir

F32 = mybir.dt.float32
F32R = mybir.dt.float32r
I32 = mybir.dt.int32
ALU = mybir.AluOpType
ACT = mybir.ActivationFunctionType
AX = mybir.AxisListType

P = 128
D = 1024
TP = 1024
NS = 8
T = TP + NS
KT = D // P
NCH = 3
CH = T // NCH
NT = TP // P
EPS = 1e-6
GN_EPS = 64e-5
HID = 2816
HT = HID // P
HG = 4
HGROUPS = HT // HG
HREST = HT - HG * HGROUPS
MH, DK, DV = 4, 64, 128
FH, DH = 8, 64
RH = 16
NPAGES, PAGE = 2, 128
BIG = 1.0e30
LN2 = math.log(2.0)


class Steps:

    def __init__(self, sem, names):
        self.sem, self.names = sem, list(names)

    def __getitem__(self, name):
        return self.names.index(name) + 1

    def of(self, name, n):
        return n * len(self.names) + self[name]

    def chain(self, eng, ins, name, n=None):
        ins.then_inc(self.sem, 1)
        eng.wait_ge(self.sem, self[name] if n is None else self.of(name, n))


def decoder_step(nc, io):
    with ExitStack() as ctx:
        cursor = [(nc.sbuf_base + 31) // 32 * 32]

        def take(n_bytes):
            a = cursor[0]
            cursor[0] += (n_bytes + 31) // 32 * 32
            assert cursor[0] <= nc.sbuf_usable_end, ("SBUF is full", cursor[0])
            return a

        def sb(name, shape, dt=F32):
            return nc.alloc_sbuf_tensor_at(name, shape, dt, offset=take(4 * int(np.prod(shape[1:]))))

        def sem(name):
            return ctx.enter_context(nc.semaphore(name))

        def dram(name, shape):
            return nc.dram_tensor(name, shape, F32, kind="Internal").ap()

        ident = sb("ident", [P, P])
        ones = sb("ones", [P, P])
        xT = sb("xT", [P, KT, T])
        w_raw = sb("w_raw", [P, 2, KT, P])
        slots = {}
        slots["w_hi"] = take(2 * KT * P * 4)
        slots["w_lo"] = take(2 * KT * P * 4)
        w_hi, w_lo = (nc.alloc_sbuf_tensor_at(n, [P, 2, KT, P], F32R, offset=slots[n]) for n in ("w_hi", "w_lo"))
        vecs = sb("vecs", [P, 172])
        cst = sb("cst", [P, 4])
        EPS_C, ONE_C, SHIFT_C, GN_C = (cst[:, i:i + 1] for i in range(4))

        SIZE = {"hl": 2 * KT * T * 4, "o": KT * T * 4, "h": KT * T * 4, "s": 5 * T * 4}
        base = {r: take(n) for r, n in SIZE.items()}
        small = [take(544), 544]

        def at(region, name, shape, offset, dt=F32):
            n = 4 * int(np.prod(shape[1:]))
            assert offset % 32 == 0 and offset + n <= SIZE[region], (name, offset, n, SIZE[region])
            return nc.alloc_sbuf_tensor_at(name, shape, dt, offset=base[region] + offset)

        def tiny(name, shape, dt=F32):
            n = (4 * int(np.prod(shape[1:])) + 31) // 32 * 32
            assert n <= small[1], name
            small[0] += n
            small[1] -= n
            return nc.alloc_sbuf_tensor_at(name, shape, dt, offset=small[0] - n)

        VEC, column = {}, 0
        for name, n in (("norm_g", 64), ("rwkv_mix", 48), ("rwkv_w0", 8), ("rwkv_a0", 8), ("rwkv_k_k", 8),
                        ("rwkv_k_a", 8), ("rwkv_r_k", 8), ("rwkv_ln_w", 8), ("rwkv_ln_b", 8), ("mlstm_out_g", 4)):
            VEC[name] = column
            column += n
        gains = vecs[:, 0:64].rearrange("p (n k) -> p n k", k=KT)

        def vec(name, k):
            return vecs[:, VEC[name] + k:VEC[name] + k + 1]

        ROW = T * 4
        act_hi = at("hl", "act_hi", [P, KT, T], 0, F32R)
        act_lo = at("hl", "act_lo", [P, KT, T], KT * ROW, F32R)
        oT = at("o", "oT", [P, KT, T], 0)
        hid_hi = at("h", "hid_hi", [P, HG, T], 0, F32R)
        hid_lo = at("h", "hid_lo", [P, HG, T], HG * ROW, F32R)
        sq = at("s", "sq", [P, 2, T], 0)
        hf = at("s", "hf", [P, 2, T], 0)
        acc = at("s", "acc", [P, T], 2 * ROW)
        sg = at("s", "sg", [P, T], 2 * ROW)
        rstd = at("s", "rstd", [P, T], 3 * ROW)
        lnv = at("s", "lnv", [P, T], 4 * ROW)
        stage = at("s", "stage", [P, 2, T], 3 * ROW)
        PS = ctx.enter_context(nc.psum_tensor("PS", [P, 8, 512], F32))

        def chunks(ap):
            return ap.rearrange("p (c n) -> p c n", c=NCH)

        def banks(u):
            return PS[:, 3 * u:3 * u + 3, 0:CH]

        proj = dram("proj", [24 * P, T])

        w_loaded = [sem("w_loaded0"), sem("w_loaded1")]
        w_hi_done = sem("w_hi_done")
        w_turn = sem("w_turn")
        w_split = [sem("w_split0"), sem("w_split1")]
        psum_full = [sem("psum_full0"), sem("psum_full1")]
        psum_free = [sem("psum_free0"), sem("psum_free1")]
        act_ready = sem("act_ready")
        hf_ready, hi_ready = sem("hf_ready"), sem("hi_ready")
        sq_ready, sq_used, ss_ready, ln_ready, rstd_ready = (
            sem(s) for s in ("sq_ready", "sq_used", "ss_ready", "ln_ready", "rstd_ready"))
        x_ready = sem("x_ready")
        o_ready = sem("o_ready")
        stored = [sem("stored0"), sem("stored1")]
        setup_done, gain_in = sem("setup_done"), sem("gain_in")
        hid_hi_ready, hid_ready = sem("hid_hi_ready"), sem("hid_ready")
        sg_ready = sem("sg_ready")
        o_zero = sem("o_zero")
        const_in = sem("const_in")

        used = [0, 0]
        plan = {}

        def step(name, n0, n1):
            plan[name] = tuple(used)
            used[0] += n0
            used[1] += n1

        step("gates", 1, 0)
        step("in_a", 4, 4)
        step("in_o", 2, 2)
        step("in_b", 6, 6)
        step("out0", 4, 4)
        step("ffn0", 8 * HGROUPS + HREST + 4, 8 * HGROUPS + HREST + 4)

        for m in "wag":
            step(f"a_{m}", 1, 0)
        for m in "rkv":
            step(f"a_{m}", 4, 4)
        step("out1", 4, 4)
        step("ffn1", 8 * HGROUPS + HREST + 4, 8 * HGROUPS + HREST + 4)
        step("end", 0, 0)

        w_in = io["hyb_w_in"][0].rearrange("(k p) n -> p k n", p=P)
        w_out = io["hyb_w_out"][0].rearrange("(k p) n -> p k n", p=P)
        C_MI, C_MF, C_FQ, C_FF = 1536, 1540, 1544, 3080

        def setup_gpsimd(pool):
            pool.memset(w_raw[:, :, :, :], 0.0).then_inc(setup_done, 1)
            pool.memset(ident[:, :], 0.0).then_inc(setup_done, 1)
            pool.memset(ones[:, :], 1.0).then_inc(setup_done, 1)
            for col, value in ((EPS_C, EPS), (ONE_C, 1.0), (SHIFT_C, 10 * LN2), (GN_C, GN_EPS)):
                pool.memset(col, value).then_inc(setup_done, 1)
            pool.wait_ge(setup_done, 7)
            pool.affine_select(out=ident[:, :], in_=ident[:, :], compare_op=ALU.not_equal, fill=1.0,
                               base=0, pattern=[[-1, P]], channel_multiplier=1).then_inc(setup_done, 1)

        x_in = at("o", "x_in", [P, NT, D], 0)
        xs_in = at("s", "xs_in", [NS, D], 0)
        vec_in = at("s", "vec_in", [P, 2, P], ROW)
        vec_loaded, vec_full = sem("vec_loaded"), sem("vec_full")
        x_loaded = [sem("x_loaded0"), sem("x_loaded1")]
        xt_full, xt_free = [sem("xt_full0"), sem("xt_full1")], [sem("xt_free0"), sem("xt_free1")]

        def load_x_sync(sp):
            xp = io["x_prompt"][0].rearrange("(t p) d -> p t d", p=P)
            for half in range(2):
                sp.dma_start(x_in[:, 4 * half:4 * half + 4, :], xp[:, 4 * half:4 * half + 4, :]).then_inc(x_loaded[half], 16)
            sp.dma_start(xs_in[:, :], io["x_sample"][:, 0, :]).then_inc(x_loaded[1], 16)
            for name, shape in (("norm_g", "l i (k p) -> (l i k) p"), ("rwkv_mix", "o i (k p) -> (o i k) p"),
                                ("rwkv_w0", ""), ("rwkv_a0", ""), ("rwkv_k_k", ""), ("rwkv_k_a", ""),
                                ("rwkv_r_k", "o (k h) d -> (o k) (h d)"), ("rwkv_ln_w", ""), ("rwkv_ln_b", ""),
                                ("mlstm_out_g", "")):
                src = io[name].rearrange(shape or "o (k p) -> (o k) p", **({"h": 2} if "h d" in shape else {"p": P}))
                c, n = VEC[name], src.shape[0]
                sp.dma_start(vec_in[c % P:c % P + n, c // P, :], src).then_inc(vec_loaded, 16)

        def load_x_tensor(pe):
            pe.wait_ge(setup_done, 8)
            pe.wait_ge(vec_loaded, 160)
            nc.tensor.transpose(PS[:, 2, 0:P], vec_in[:, 0, :], ident[:, :])
            nc.tensor.transpose(PS[:, 2, P:172], vec_in[0:44, 1, :], ident[0:44, 0:44]).then_inc(vec_full, 1)
            for t in range(NT):
                pe.wait_ge(x_loaded[t // 4], 16 if t < 4 else 32)
                for half in range(2):
                    if t >= 1:
                        pe.wait_ge(xt_free[half], t)
                    for k in range(4):
                        mm = nc.tensor.transpose(PS[:, half, P * k:P * k + P],
                                                 x_in[:, t, P * (4 * half + k):P * (4 * half + k) + P], ident[:, :])
                    mm.then_inc(xt_full[half], 1)
            pe.wait_ge(xt_free[0], NT)
            for k in range(KT):
                mm = nc.tensor.transpose(PS[:, 0, NS * k:NS * k + NS], xs_in[:, P * k:P * k + P], ident[0:NS, 0:NS])
            mm.then_inc(xt_full[0], 1)

        def x_copy(eng_copy, half, t):
            src = PS[:, half, :].rearrange("p (k n) -> p k n", k=4)
            return eng_copy(xT[:, 4 * half:4 * half + 4, P * t:P * t + P], src)

        def load_x_scalar(act):
            for t in range(NT):
                act.wait_ge(xt_full[0], t + 1)
                x_copy(nc.scalar.copy, 0, t).then_inc(xt_free[0], 1)
            act.wait_ge(xt_full[0], NT + 1)
            nc.scalar.copy(xT[:, :, TP:T], PS[:, 0, 0:KT * NS].rearrange("p (k n) -> p k n", k=KT)).then_inc(xt_free[0], 1)

        def load_x_vector(dve):
            dve.wait_ge(vec_full, 1)
            nc.vector.tensor_copy(vecs[:, :], PS[:, 2, 0:172]).then_inc(gain_in, 1)
            for t in range(NT):
                dve.wait_ge(xt_full[1], t + 1)
                x_copy(nc.vector.tensor_copy, 1, t).then_inc(xt_free[1], 1)

        def stats_scalar(act, n, src, wait_source):
            wait_source(act)
            for k in range(KT):
                g = KT * n + k
                if g >= 2:
                    act.wait_ge(sq_used, g - 1)
                nc.scalar.activation(sq[:, k % 2, :], src[:, k, :], ACT.Square).then_inc(sq_ready, 1)
            if n == 0:
                act.wait_ge(gain_in, 1)
            act.wait_ge(ss_ready, n + 1)
            nc.scalar.activation(chunks(lnv[:, :]), banks(0), ACT.Ln, bias=EPS_C, scale=1.0 / D).then_inc(ln_ready, 1)
            act.wait_ge(ln_ready, n + 1)
            nc.scalar.activation(rstd[:, :], lnv[:, :], ACT.Exp, scale=-0.5).then_inc(rstd_ready, 1)

        def stats_vector(dve, n):
            for k in range(KT):
                g = KT * n + k
                dve.wait_ge(sq_ready, g + 1)
                if k == 0:
                    nc.vector.tensor_copy(acc[:, :], sq[:, k % 2, :]).then_inc(sq_used, 1)
                else:
                    dve.wait_ge(sq_used, g)
                    nc.vector.tensor_tensor(acc[:, :], acc[:, :], sq[:, k % 2, :], ALU.add).then_inc(sq_used, 1)

        def stats_tensor(pe, n):
            pe.wait_ge(sq_used, KT * (n + 1))
            for c in range(NCH):
                mm = nc.tensor.matmul(PS[:, c, 0:CH], ones[:, :], acc[:, CH * c:CH * c + CH], start=True, stop=True)
            mm.then_inc(ss_ready, 1)

        def split_vector(dve, r, make):
            for k in range(KT + 1):
                if k < KT:
                    if k >= 2:
                        dve.wait_ge(act_ready, KT * r + k - 1)
                    make(k).then_inc(hf_ready, 1)
                if k >= 1:
                    dve.wait_ge(hf_ready, KT * r + k)
                    dve.wait_ge(hi_ready, KT * r + k)
                    nc.vector.tensor_tensor(act_lo[:, k - 1, :], hf[:, (k - 1) % 2, :],
                                            act_hi[:, k - 1, :].bitcast(F32), ALU.subtract).then_inc(act_ready, 1)

        def split_scalar(act, r):
            for k in range(KT):
                act.wait_ge(hf_ready, KT * r + k + 1)
                nc.scalar.copy(act_hi[:, k, :], hf[:, k % 2, :]).then_inc(hi_ready, 1)

        def normed(dve, n):
            dve.wait_ge(rstd_ready, n + 1)
            dve.wait_ge(gain_in, 1)
            return lambda k: nc.vector.scalar_tensor_tensor(hf[:, k % 2, :], xT[:, k, :], gains[:, n, k:k + 1],
                                                            rstd[:, :], ALU.mult, ALU.mult)

        add_t = sem("add_t")

        def add_normed_vector(dve, n, m):
            dve.wait_ge(rstd_ready, n + 1)
            for k in range(KT + 1):
                if k < KT:
                    if k >= 2:
                        dve.wait_ge(x_ready, KT * m + k - 1)
                    nc.vector.scalar_tensor_tensor(hf[:, k % 2, :], oT[:, k, :], gains[:, n, k:k + 1], rstd[:, :],
                                                   ALU.mult, ALU.mult).then_inc(add_t, 1)
                if k >= 1:
                    dve.wait_ge(add_t, KT * m + k)
                    nc.vector.tensor_tensor(xT[:, k - 1, :], xT[:, k - 1, :], hf[:, (k - 1) % 2, :],
                                            ALU.add).then_inc(x_ready, 1)

        def load_w(sp, u, k, src, dst=None):
            sp.wait_ge(w_split[u], k)
            sp.dma_start(w_raw[:, u, 0:src.shape[1], :] if dst is None else dst, src).then_inc(w_loaded[u], 16)

        def split_w(pool, u, k, kts, hi_count):
            pool.wait_ge(w_loaded[u], 16 * (k + 1))
            pool.wait_ge(psum_full[u], k)
            pool.sem_inc(w_turn, 1)
            nc.gpsimd.tensor_copy(w_hi[:, u, 0:kts, :], w_raw[:, u, 0:kts, :]).then_inc(w_hi_done, 1)
            pool.wait_ge(w_hi_done, hi_count)
            nc.gpsimd.tensor_tensor(w_lo[:, u, 0:kts, :], w_raw[:, u, 0:kts, :],
                                    w_hi[:, u, 0:kts, :].bitcast(F32), ALU.subtract).then_inc(w_split[u], 1)

        def split_pairs(pool, name, pairs, kts, k_off=0):
            k0, k1 = plan[name][0] + k_off, plan[name][1] + k_off
            with pool.Fori(0, pairs) as i:
                split_w(pool, 0, k0 + i, kts, k0 + k1 + 2 * i + 1)
                split_w(pool, 1, k1 + i, kts, k0 + k1 + 2 * i + 2)

        def tile_products(pe, u, k, hi, lo, kts, ready, ready_base):
            pe.wait_ge(w_split[u], k + 1)
            pe.wait_ge(psum_free[u], k)
            for kt in range(kts):
                pe.wait_ge(ready, ready_base + kt + 1)
                for part, (w, x) in enumerate(((w_hi, hi), (w_hi, lo), (w_lo, hi))):
                    for c in range(NCH):
                        mm = nc.tensor.matmul(PS[:, 3 * u + c, 0:CH], w[:, u, kt, :], x[:, kt, CH * c:CH * c + CH],
                                              start=(kt == 0 and part == 0), stop=(kt == kts - 1 and part == 2))
            mm.then_inc(psum_full[u], 1)

        def gemm_tensor(pe, name, pairs, r, k_off=0):
            k0, k1 = plan[name][0] + k_off, plan[name][1] + k_off
            with pe.Fori(0, pairs) as i:
                tile_products(pe, 0, k0 + i, act_hi, act_lo, KT, act_ready, KT * r)
                tile_products(pe, 1, k1 + i, act_hi, act_lo, KT, act_ready, KT * r)

        def load_pairs(sp, name, pairs, w, c0=0, k_off=0):
            k0, k1 = plan[name][0] + k_off, plan[name][1] + k_off
            with sp.Fori(0, pairs) as i:
                load_w(sp, 0, k0 + i, w[:, :, bass.ds(i * (2 * P) + c0, P)])
                load_w(sp, 1, k1 + i, w[:, :, bass.ds(i * (2 * P) + (c0 + P), P)])

        def store_scalar(act, name, pairs, dst, row0, s0, func=ACT.Copy, k_off=0):
            k0, k1 = plan[name][0] + k_off, plan[name][1] + k_off
            with act.Fori(0, pairs) as i:
                for u, k in ((0, k0), (1, k1)):
                    act.wait_ge(psum_full[u], k + i + 1)
                    act.wait_ge(stored[u], (i + s0) * 16)
                    nc.scalar.activation(chunks(stage[:, u, :]), banks(u), func).then_inc(psum_free[u], 1)
                    act.wait_ge(psum_free[u], k + i + 1)
                    act.dma_start(dst[bass.ds(i * (2 * P) + (row0 + P * u), P), :], stage[:, u, :]).then_inc(stored[u], 16)

        def keep_scalar(act, name):
            k0, k1 = plan[name]
            with act.Fori(0, KT // 2) as i:
                for u, k in ((0, k0), (1, k1)):
                    act.wait_ge(psum_full[u], k + i + 1)
                    nc.scalar.copy(oT[:, bass.ds(2 * i + u, 1), :].rearrange("p o (c n) -> p (o c) n", c=NCH), banks(u)).then_inc(psum_free[u], 1)

        def ffn_weights(l):
            wg, wu = (io[n][l].rearrange("(k p) n -> p k n", p=P) for n in ("ffn_w_gate", "ffn_w_up"))
            return wg, wu, io["ffn_w_down"][l].rearrange("(k p) n -> p k n", p=P)

        def ffn_groups(eng, body):
            with eng.Fori(0, HGROUPS) as g:
                body(g, HG)
            body(HGROUPS, HREST)

        def ffn_sync(sp, l):
            name = f"ffn{l}"
            k0, k1 = plan[name]
            wg, wu, wd = ffn_weights(l)

            def body(g, n):
                with sp.Fori(0, n) as i:
                    load_w(sp, 0, g * 8 + (i + k0), wg[:, :, bass.ds(g * (HG * P) + i * P, P)])
                    load_w(sp, 1, g * 8 + (i + k1), wu[:, :, bass.ds(g * (HG * P) + i * P, P)])
                with sp.Fori(0, KT // 2) as i:
                    for u, k in ((0, k0), (1, k1)):
                        load_w(sp, u, g * 8 + (i + (k + n)), wd[:, bass.ds(g * HG, n), bass.ds(i * (2 * P) + P * u, P)])
            ffn_groups(sp, body)

        def ffn_gpsimd(pool, l):
            k0, k1 = plan[f"ffn{l}"]

            def body(g, n):
                for count, kts, off in ((n, KT, 0), (KT // 2, n, n)):
                    with pool.Fori(0, count) as i:
                        for u, k in ((0, k0), (1, k1)):
                            split_w(pool, u, g * 8 + (i + (k + off)), kts, g * 16 + (2 * i + (k0 + k1 + 2 * off + u + 1)))
            ffn_groups(pool, body)

        def ffn_tensor(pe, l, r):
            k0, k1 = plan[f"ffn{l}"]

            def body(g, n):
                with pe.Fori(0, n) as i:
                    for u, k in ((0, k0), (1, k1)):
                        tile_products(pe, u, g * 8 + (i + k), act_hi, act_lo, KT, act_ready, KT * r)
                with pe.Fori(0, KT // 2) as i:
                    for u, k in ((0, k0), (1, k1)):
                        tile_products(pe, u, g * 8 + (i + (k + n)), hid_hi, hid_lo, n, hid_ready, g * HG + l * HT)
            ffn_groups(pe, body)

        def ffn_scalar(act, l):
            k0, k1 = plan[f"ffn{l}"]
            h0 = l * HT

            def body(g, n):
                with act.Fori(0, n) as i:
                    act.wait_ge(psum_full[0], g * 8 + (i + (k0 + 1)))
                    act.wait_ge(hid_ready, g * HG + (i + h0))
                    nc.scalar.activation(chunks(sg[:, :]), banks(0), ACT.Silu).then_inc(psum_free[0], 1)
                    act.wait_ge(psum_free[1], g * 8 + (i + (k1 + 1)))
                    nc.scalar.copy(hid_hi[:, bass.ds(i, 1), :], hf[:, 0:1, :]).then_inc(hid_hi_ready, 1)
            ffn_groups(act, body)

        def ffn_vector(dve, l, m):
            k0, k1 = plan[f"ffn{l}"]
            h0 = l * HT
            dve.wait_ge(act_ready, KT * (m + 1))
            nc.vector.memset(oT[:, :, :], 0.0).then_inc(o_zero, 1)
            dve.wait_ge(o_zero, l + 1)

            def body(g, n):
                with dve.Fori(0, n) as i:
                    dve.wait_ge(psum_free[0], g * 8 + (i + (k0 + 1)))
                    dve.wait_ge(psum_full[1], g * 8 + (i + (k1 + 1)))
                    nc.vector.tensor_tensor(chunks(hf[:, 0, :]), banks(1), chunks(sg[:, :]), ALU.mult).then_inc(psum_free[1], 1)
                    dve.wait_ge(hid_hi_ready, g * HG + (i + (h0 + 1)))
                    nc.vector.tensor_tensor(hid_lo[:, bass.ds(i, 1), :], hf[:, 0:1, :],
                                            hid_hi[:, bass.ds(i, 1), :].bitcast(F32), ALU.subtract).then_inc(hid_ready, 1)
                with dve.Fori(0, KT // 2) as i:
                    for u, k in ((0, k0), (1, k1)):
                        dve.wait_ge(psum_full[u], g * 8 + (i + (k + n + 1)))
                        tile = oT[:, bass.ds(2 * i + u, 1), :].rearrange("p o (c n) -> p (o c) n", c=NCH)
                        nc.vector.tensor_tensor(tile, banks(u), tile, ALU.add).then_inc(psum_free[u], 1)
            ffn_groups(dve, body)

        mix = dram("mix", [D, T])
        mrow = dram("mrow", [2, MH, TP])
        frow = dram("frow", [FH, TP])
        lfs = dram("lfs", [2, MH, NS])
        g_ig, g_lf, g_ff, g_t0, g_t1, g_b, g_M, g_wi = (
            at("h", n, [FH, T], i * ROW) for i, n in enumerate(("g_ig", "g_lf", "g_ff", "g_t0", "g_t1", "g_b", "g_M", "g_wi")))
        pack = at("o", "pack", [96, TP], 0)
        cols = at("o", "cols", [P, NT, 96], 4096)
        fresh = at("o", "fresh", [FH, TP], 7168)
        mask_st = at("o", "mask_st", [P, P], 11264)
        mask_ts = at("o", "mask_ts", [P, P], 11776)
        bias_i, bias_f, bias_x = tiny("bias_i", [MH, 1]), tiny("bias_f", [MH, 1]), tiny("bias_x", [FH, 1])
        m_in = tiny("m_in", [MH, NT + 1])
        lf_tok = at("o", "lf_tok", [P, NT, FH], 12288)
        lf_sam = at("o", "lf_sam", [NS, FH], 12544)
        gate_w_in, bias_in = sem("gate_w_in"), sem("bias_in")
        gp = sem("gp")
        GA = Steps(sem("ga"), "ig mf fx fabs fexp fln xx xabs xexp xln wi wk em".split())
        GV = Steps(sem("gv"), "fresh minit lf lff F starts b g".split()
                   + [f"{x}{c}" for c in range(NT) for x in ("M", "m")] + "wi wk bM".split())
        rows_out, cols_full, cols_done = sem("rows_out"), sem("cols_full"), sem("cols_done")

        def gates_sync(sp):
            sp.wait_ge(setup_done, 8)
            sp.dma_start(w_raw[:, 0, :, 0:4], w_in[:, :, C_MI:C_MI + 4], allow_slow_non_contiguous=True).then_inc(gate_w_in, 16)
            sp.dma_start(w_raw[:, 0, :, 32:36], w_in[:, :, C_MF:C_MF + 4], allow_slow_non_contiguous=True).then_inc(gate_w_in, 16)
            sp.dma_start(w_raw[:, 0, :, 64:72], w_in[:, :, C_FF:C_FF + 8], allow_slow_non_contiguous=True).then_inc(w_loaded[0], 16)
            for dst, name in ((bias_i, "mlstm_i_bias"), (bias_f, "mlstm_f_bias"), (bias_x, "fox_f_bias")):
                sp.dma_start(dst[:, :], io[name].rearrange("o h -> h o")).then_inc(bias_in, 16)

        def gates_out_sync(sp):
            sp.wait_ge(GA.sem, GA["em"])
            sp.wait_ge(GV.sem, GV["bM"])
            sp.dma_start(mrow[0], g_M[0:MH, 0:TP]).then_inc(rows_out, 16)
            sp.dma_start(mrow[1], g_wi[0:MH, 0:TP]).then_inc(rows_out, 16)
            sp.dma_start(frow, g_t1[:, 0:TP]).then_inc(rows_out, 16)
            sp.dma_start(lfs[0], g_ig[0:MH, TP:T]).then_inc(rows_out, 16)
            sp.dma_start(lfs[1], g_lf[0:MH, TP:T]).then_inc(rows_out, 16)
            sp.dma_start(io["p_mlstm_m"].rearrange("o b h -> (o h) b"), m_in[:, NT:NT + 1]).then_inc(rows_out, 16)
            sp.wait_ge(cols_done, 3)
            sp.dma_start(io["p_fox_lf"][0, 0].rearrange("(c p) h -> p c h", p=P), lf_tok[:, :, :]).then_inc(rows_out, 16)
            sp.dma_start(io["s_fox_lf"][0, :, 0, :], lf_sam[:, :]).then_inc(rows_out, 16)

        def gates_gpsimd(pool):
            pool.wait_ge(gate_w_in, 32)
            split_w(pool, 0, 0, KT, 1)
            pool.wait_ge(xt_full[0], NT + 1)
            pool.memset(pack[:, :], 0.0).then_inc(gp, 1)
            pool.memset(mask_st[:, :], 0.0).then_inc(gp, 1)
            pool.memset(mask_ts[:, :], 0.0).then_inc(gp, 1)
            pool.wait_ge(gp, 3)
            pool.affine_select(out=mask_st[:, :], in_=mask_st[:, :], compare_op=ALU.is_ge, fill=BIG,
                               base=0, pattern=[[1, P]], channel_multiplier=-1).then_inc(gp, 1)
            pool.affine_select(out=mask_ts[:, :], in_=mask_ts[:, :], compare_op=ALU.is_ge, fill=-BIG,
                               base=0, pattern=[[-1, P]], channel_multiplier=1).then_inc(gp, 1)

        def gates_tensor(pe, r):
            tile_products(pe, 0, 0, act_hi, act_lo, KT, act_ready, KT * r)

        def gates_cols_tensor(pe):
            pe.wait_ge(GA.sem, GA["em"])
            pe.wait_ge(GV.sem, GV["bM"])
            pe.wait_ge(psum_free[0], plan["out0"][0])
            pe.wait_ge(psum_free[1], plan["out0"][1])
            for c in range(NT):
                nc.tensor.transpose(PS[:, c // 4, P * (c % 4):P * (c % 4) + 96], pack[:, P * c:P * c + P], ident[0:96, 0:96])
            for c in range(NT):
                nc.tensor.transpose(PS[:, 2, FH * c:FH * c + FH], g_ff[:, P * c:P * c + P], ident[0:FH, 0:FH])
            nc.tensor.transpose(PS[0:NS, 2, P:P + FH], g_ff[:, TP:T], ident[0:FH, 0:FH]).then_inc(cols_full, 1)

        def gates_scalar(act):
            row = lambda ap: ap.rearrange("p (c n) -> p c n", c=NCH)
            act.wait_ge(bias_in, 48)
            act.wait_ge(psum_full[0], 1)
            GA.chain(act, nc.scalar.activation(row(g_ig[0:MH, :]), PS[0:MH, 0:3, 0:CH], ACT.Identity, bias=bias_i[:, :]), "ig")
            GA.chain(act, nc.scalar.copy(row(g_t0[0:MH, :]), PS[32:32 + MH, 0:3, 0:CH]), "mf")
            nc.scalar.copy(row(g_ff[:, :]), PS[64:64 + FH, 0:3, 0:CH]).then_inc(psum_free[0], 1)
            act.wait_ge(psum_free[0], 1)
            for s, x, dst, n, bias in (("f", g_t0, g_t1, MH, bias_f), ("x", g_ff, g_M, FH, bias_x)):
                GA.chain(act, nc.scalar.activation(x[0:n, :], x[0:n, :], ACT.Identity, bias=bias[:, :]), s + "x")
                GA.chain(act, nc.scalar.activation(dst[0:n, :], x[0:n, :], ACT.Abs), s + "abs")
                GA.chain(act, nc.scalar.activation(dst[0:n, :], dst[0:n, :], ACT.Exp, scale=-1.0), s + "exp")
                GA.chain(act, nc.scalar.activation(dst[0:n, :], dst[0:n, :], ACT.Ln, bias=ONE_C[0:n, :]), s + "ln")

        def gates_exp_scalar(act):
            act.wait_ge(gp, 1)
            act.wait_ge(GV.sem, GV["bM"])
            nc.scalar.activation(g_wi[0:MH, 0:TP], g_wi[0:MH, 0:TP], ACT.Exp).then_inc(GA.sem, 1)
            nc.scalar.activation(pack[32:32 + MH, :], g_t0[0:MH, 0:TP], ACT.Exp).then_inc(GA.sem, 1)
            nc.scalar.activation(pack[64:64 + MH, :], g_b[0:MH, 0:TP], ACT.Exp, scale=-1.0).then_inc(GA.sem, 1)

        def gates_vector(dve):
            by_chunk = lambda ap: ap.rearrange("p (c n) -> p c n", c=NT)
            last = lambda ap, c: ap[0:MH, P * c + P - 1:P * c + P]
            dve.wait_ge(xt_full[0], NT + 1)
            GV.chain(dve, nc.vector.memset(fresh[:, :], 1.0), "fresh")
            GV.chain(dve, nc.vector.memset(m_in[:, :], 0.0), "minit")
            dve.wait_ge(GA.sem, GA["fln"])
            GV.chain(dve, nc.vector.scalar_tensor_tensor(g_lf[0:MH, :], g_t0[0:MH, :], 0.0, g_t1[0:MH, :], ALU.min, ALU.subtract), "lf")
            dve.wait_ge(GA.sem, GA["xln"])
            GV.chain(dve, nc.vector.scalar_tensor_tensor(g_ff[:, :], g_ff[:, :], 0.0, g_M[:, :], ALU.min, ALU.subtract), "lff")
            GV.chain(dve, nc.vector.tensor_tensor_scan(g_t1[:, 0:TP], fresh[:, :], g_ff[:, 0:TP], 0.0, ALU.mult, ALU.subtract), "F")
            GV.chain(dve, nc.vector.memset(by_chunk(fresh[:, :])[:, :, 0:1], 0.0), "starts")
            GV.chain(dve, nc.vector.tensor_tensor_scan(g_b[0:MH, 0:TP], fresh[0:MH, :], g_lf[0:MH, 0:TP], 0.0, ALU.mult, ALU.add), "b")
            dve.wait_ge(gp, 1)
            GV.chain(dve, nc.vector.tensor_tensor(pack[0:MH, :], g_ig[0:MH, 0:TP], g_b[0:MH, 0:TP], ALU.subtract), "g")
            for c in range(NT):
                s = slice(P * c, P * c + P)
                GV.chain(dve, nc.vector.tensor_tensor_scan(g_M[0:MH, s], pack[0:MH, s], pack[0:MH, s], m_in[:, c:c + 1], ALU.max, ALU.max), f"M{c}")
                GV.chain(dve, nc.vector.tensor_tensor(m_in[:, c + 1:c + 2], last(g_b, c), last(g_M, c), ALU.add), f"m{c}")
            M3 = by_chunk(g_M[0:MH, 0:TP])
            m3 = m_in[:, 0:NT].rearrange("p (c o) -> p c o", o=1).broadcast_to([MH, NT, P])
            GV.chain(dve, nc.vector.tensor_tensor(by_chunk(g_wi[0:MH, 0:TP]), m3, M3, ALU.subtract), "wi")
            GV.chain(dve, nc.vector.tensor_tensor(by_chunk(g_t0[0:MH, 0:TP]), by_chunk(pack[0:MH, :]),
                                                  M3[:, :, P - 1:P].broadcast_to([MH, NT, P]), ALU.subtract), "wk")
            GV.chain(dve, nc.vector.tensor_tensor(g_b[0:MH, 0:TP], g_b[0:MH, 0:TP], g_M[0:MH, 0:TP], ALU.add), "bM")

        def gates_cols_vector(dve):
            dve.wait_ge(cols_full, 1)
            nc.vector.tensor_copy(cols[:, :, :].rearrange("p (b c) n -> p b c n", b=2),
                                  PS[:, 0:2, :].rearrange("p b (c n) -> p b c n", c=4)[:, :, :, 0:96]).then_inc(cols_done, 1)
            nc.vector.tensor_copy(lf_tok[:, :, :], PS[:, 2, 0:NT * FH].rearrange("p (c h) -> p c h", h=FH)).then_inc(cols_done, 1)
            nc.vector.tensor_copy(lf_sam[:, :], PS[0:NS, 2, P:P + FH]).then_inc(cols_done, 1)

        HB = 4 * ROW + 2 * 4096
        ml_q, ml_k, ml_v, ml_o, ml_M, ml_wi = ([at("hl", f"{n}{e}", [p, w], e * HB + off) for e in range(2)] for n, p, w, off in (
            ("ml_q", DK, T, 0), ("ml_k", DK, T, ROW), ("ml_v", P, T, 2 * ROW), ("ml_o", P, T, 3 * ROW),
            ("ml_M", P, TP, 4 * ROW), ("ml_wi", DK, TP, 4 * ROW + 4096)))
        AV = DV + 1
        ml_va = at("o", "ml_va", [P, NT, 132], 12608)
        ml_se = at("o", "ml_se", [P, NT, P], 16832)
        ml_qw = at("o", "ml_qw", [DK, TP], 20928)
        ml_num = at("o", "ml_num", [P, NT, AV], 25024)
        ml_kw = at("s", "ml_kw", [P, NT, DK], 0)
        ml_e = at("s", "ml_e", [P, NT, P], 2048)
        ml_hn = at("s", "ml_hn", [P, NT, P], 2048)
        ml_c = at("s", "ml_c", [DK, NT + 1, 132], 6144)
        ml_sq = at("s", "ml_sq", [P, NT, P], 10912)
        ml_out = at("s", "ml_out", [P, TP], 15008)
        ml_den, ml_r, ml_r2, ml_ss, ml_t, ml_ln, ml_rs, ml_fac, ml_abs = (
            at("s", n, [P, NT], 19104 + 32 * i) for i, n in enumerate("ml_den ml_r ml_r2 ml_ss ml_t ml_ln ml_rs ml_fac ml_abs".split()))
        ml_in = [sem("ml_in0"), sem("ml_in1")]
        MT = Steps(sem("ml_pe"), "tr st kv num ht".split())
        MA = Steps(sem("ml_act"), "va e num sq abs ln rs".split())
        MV = Steps(sem("ml_dve"), "kw zg se".split() + [f"c{c}" for c in range(NT)] + "den r r2 ss t fac hn out".split())
        MP = Steps(sem("ml_pool"), "z qw".split())
        ml_ones, ml_stored = sem("ml_ones"), sem("ml_stored")
        bank3 = lambda c: PS[:, 5 + c // 3, AV * (c % 3):AV * (c % 3) + AV]

        def heads_of(eng, body):
            with eng.Fori(0, MH // 2) as i:
                for e in range(2):
                    body(2 * i + e, e, i)

        def mlstm_sync(sp):
            sp.wait_ge(stored[0], 16 * plan["out0"][0] - 16)
            sp.wait_ge(stored[1], 16 * plan["out0"][1])
            sp.wait_ge(rows_out, 16 * 8)

            def body(n, e, i):
                sp.wait_ge(MV.sem, i * (2 * len(MV.names)) + (e - 1) * len(MV.names) if e == 1 else i * (2 * len(MV.names)))
                src = lambda row, p: proj[bass.ds(n * p + row, p), :]
                sp.dma_start(ml_q[e][:, :], src(0, DK)).then_inc(ml_in[e], 16)
                sp.dma_start(ml_k[e][:, :], src(256, DK)).then_inc(ml_in[e], 16)
                sp.dma_start(ml_v[e][:, :], src(512, P)).then_inc(ml_in[e], 16)
                sp.dma_start(ml_o[e][:, :], src(1024, P)).then_inc(ml_in[e], 16)
                sp.dma_start(ml_M[e][:, :], mrow[0, bass.ds(n, 1), :].broadcast_to([P, TP])).then_inc(ml_in[e], 16)
                sp.dma_start(ml_wi[e][:, :], mrow[1, bass.ds(n, 1), :].broadcast_to([DK, TP])).then_inc(ml_in[e], 16)
            heads_of(sp, body)

        def mlstm_store_scalar(act, n, e, i):
            act.wait_ge(MV.sem, MV.of("out", n))
            act.dma_start(mix[bass.ds(n * P, P), 0:TP], ml_out[:, :]).then_inc(ml_stored, 16)
            act.dma_start(io["p_mlstm_c"][0, 0, bass.ds(n, 1)].rearrange("o k v -> (o k) v"), ml_c[:, NT, 0:DV]).then_inc(ml_stored, 16)
            act.dma_start(io["p_mlstm_n"][0, 0, bass.ds(n, 1)].rearrange("o (k x) -> (o k) x", x=1), ml_c[:, NT, DV:AV], allow_slow_non_contiguous=True).then_inc(ml_stored, 16)

        def mlstm_tensor(pe):
            pe.wait_ge(cols_done, 3)

            def body(n, e, i):
                pe.wait_ge(ml_in[e], i * 96 + 96)
                for c in range(NT):
                    nc.tensor.transpose(PS[:, 1 + c // 4, P * (c % 4):P * (c % 4) + P], ml_v[e][:, P * c:P * c + P], ident[:, :])
                for c in range(NT):
                    mm = nc.tensor.transpose(PS[:, 0, DK * c:DK * c + DK], ml_k[e][:, P * c:P * c + P], ident[0:DK, 0:DK])
                mm.then_inc(MT.sem, 1)
                pe.wait_ge(MV.sem, n * len(MV.names))
                for c in range(NT):
                    s = slice(P * c, P * c + P)
                    mm = nc.tensor.matmul(PS[:, 3 + c // 4, P * (c % 4):P * (c % 4) + P], ml_k[e][:, s], ml_q[e][:, s], start=True, stop=True)
                mm.then_inc(MT.sem, 1)
                pe.wait_ge(MV.sem, MV.of("kw", n))
                pe.wait_ge(MA.sem, MA.of("va", n))
                for c in range(NT):
                    mm = nc.tensor.matmul(bank3(c)[0:DK], ml_kw[:, c, :], ml_va[:, c, 0:AV], start=True, stop=True)
                mm.then_inc(MT.sem, 1)
                pe.wait_ge(MP.sem, MP.of("qw", n))
                pe.wait_ge(MV.sem, MV.of("c7", n))
                for c in range(NT):
                    nc.tensor.matmul(bank3(c), ml_se[:, c, :], ml_va[:, c, 0:AV], start=True, stop=False)
                    mm = nc.tensor.matmul(bank3(c), ml_qw[:, P * c:P * c + P], ml_c[:, c, 0:AV], start=False, stop=True)
                mm.then_inc(MT.sem, 1)
                pe.wait_ge(MV.sem, MV.of("hn", n))
                for c in range(NT):
                    mm = nc.tensor.transpose(PS[:, 3 + c // 4, P * (c % 4):P * (c % 4) + P], ml_hn[:, c, :], ident[:, :])
                mm.then_inc(MT.sem, 1)
            heads_of(pe, body)

        def mlstm_scalar(act):
            def body(n, e, i):
                act.wait_ge(MT.sem, MT.of("tr", n))
                nc.scalar.copy(ml_va[:, :, 0:DV].rearrange("p (b c) n -> p b c n", b=2),
                               PS[:, 1:3, :].rearrange("p b (c n) -> p b c n", c=4)).then_inc(MA.sem, 1)
                act.wait_ge(MV.sem, MV.of("zg", n))
                nc.scalar.activation(ml_e[:, :, :], ml_e[:, :, :], ACT.Exp, scale=-1.0).then_inc(MA.sem, 1)
                act.wait_ge(MT.sem, MT.of("num", n))
                nc.scalar.copy(ml_num[:, 0:6, :].rearrange("p (b c) n -> p b (c n)", b=2), PS[:, 5:7, 0:3 * AV])
                nc.scalar.copy(ml_num[:, 6:8, :].rearrange("p c n -> p (c n)"), PS[:, 7, 0:2 * AV]).then_inc(MA.sem, 1)
                act.wait_ge(MA.sem, MA.of("num", n))
                nc.scalar.activation(ml_sq[:, :, :], ml_num[:, :, 0:DV], ACT.Square).then_inc(MA.sem, 1)
                nc.scalar.activation(ml_abs[:, :].rearrange("p (c o) -> p c o", o=1), ml_num[:, :, DV:AV], ACT.Abs).then_inc(MA.sem, 1)
                act.wait_ge(MV.sem, MV.of("t", n))
                nc.scalar.activation(ml_ln[:, :], ml_t[:, :], ACT.Ln, bias=EPS_C, scale=1.0 / DV).then_inc(MA.sem, 1)
                act.wait_ge(MA.sem, MA.of("ln", n))
                nc.scalar.activation(ml_rs[:, :], ml_ln[:, :], ACT.Exp, scale=-0.5).then_inc(MA.sem, 1)
                mlstm_store_scalar(act, n, e, i)
            heads_of(act, body)

        def mlstm_gpsimd(pool):
            def body(n, e, i):
                pool.wait_ge(ml_in[e], i * 96 + 96)
                pool.wait_ge(MV.sem, n * len(MV.names))
                by = lambda ap: ap.rearrange("p (c n) -> p c n", c=NT)
                nc.gpsimd.tensor_tensor(ml_e[:, :, :], by(ml_M[e][:, :]), mask_st[:, :].rearrange("p (o n) -> p o n", o=1).broadcast_to([P, NT, P]),
                                        ALU.add).then_inc(MP.sem, 1)
                nc.gpsimd.tensor_tensor(ml_qw[:, :], ml_q[e][:, 0:TP], ml_wi[e][:, :], ALU.mult).then_inc(MP.sem, 1)
            pool.memset(ml_va[:, :, DV:AV], 1.0).then_inc(ml_ones, 1)
            pool.memset(ml_c[:, 0, :], 0.0).then_inc(ml_ones, 1)
            pool.wait_ge(rows_out, 128)
            heads_of(pool, body)

        def mlstm_vector(dve):
            dve.wait_ge(ml_ones, 2)
            b4 = lambda ap: ap.rearrange("p (b c) n -> p b c n", b=2)

            def column(row, n):
                return cols[:, :, bass.ds(n + row, 1)]

            def body(n, e, i):
                N = len(MV.names)
                dve.wait_ge(MT.sem, MT.of("tr", n))
                nc.vector.scalar_tensor_tensor(ml_kw[:, :, :], PS[:, 0, :].rearrange("p (c k) -> p c k", c=NT), DK ** -0.5,
                                               column(32, n).broadcast_to([P, NT, DK]), ALU.mult, ALU.mult).then_inc(MV.sem, 1)
                dve.wait_ge(MP.sem, MP.of("z", n))
                nc.vector.tensor_tensor(ml_e[:, :, :], ml_e[:, :, :], column(0, n).broadcast_to([P, NT, P]), ALU.subtract).then_inc(MV.sem, 1)
                dve.wait_ge(MA.sem, MA.of("e", n))
                dve.wait_ge(MT.sem, MT.of("st", n))
                nc.vector.scalar_tensor_tensor(b4(ml_se[:, :, :]), PS[:, 3:5, :].rearrange("p b (c n) -> p b c n", c=4), DK ** -0.5,
                                               b4(ml_e[:, :, :]), ALU.mult, ALU.mult).then_inc(MV.sem, 1)
                dve.wait_ge(MT.sem, MT.of("kv", n))
                dve.wait_ge(ml_stored, n * 48)
                for c in range(NT):
                    dst = ml_c[:, c + 1, 0:AV]
                    if c:
                        dve.wait_ge(MV.sem, MV.of(f"c{c - 1}", n))
                    nc.vector.scalar_tensor_tensor(dst, ml_c[:, c, 0:AV], ml_wi[e][:, P * c + P - 1:P * c + P], bank3(c)[0:DK],
                                                   ALU.mult, ALU.add).then_inc(MV.sem, 1)
                dve.wait_ge(MA.sem, MA.of("abs", n))
                den = ml_den[:, :].rearrange("p (c o) -> p c o", o=1)
                MV.chain(dve, nc.vector.tensor_tensor(den, ml_abs[:, :].rearrange("p (c o) -> p c o", o=1), column(64, n), ALU.max), "den", n)
                MV.chain(dve, nc.vector.reciprocal(ml_r[:, :], ml_den[:, :]), "r", n)
                MV.chain(dve, nc.vector.tensor_tensor(ml_r2[:, :], ml_r[:, :], ml_r[:, :], ALU.mult), "r2", n)
                MV.chain(dve, nc.vector.tensor_reduce(ml_ss[:, :], ml_sq[:, :, :], AX.X, ALU.add), "ss", n)
                MV.chain(dve, nc.vector.tensor_tensor(ml_t[:, :], ml_ss[:, :], ml_r2[:, :], ALU.mult), "t", n)
                dve.wait_ge(MA.sem, MA.of("rs", n))
                MV.chain(dve, nc.vector.tensor_tensor(ml_fac[:, :], ml_r[:, :], ml_rs[:, :], ALU.mult), "fac", n)
                MV.chain(dve, nc.vector.tensor_tensor(ml_hn[:, :, :], ml_num[:, :, 0:DV],
                                                      ml_fac[:, :].rearrange("p (c o) -> p c o", o=1).broadcast_to([P, NT, DV]), ALU.mult), "hn", n)
                dve.wait_ge(MT.sem, MT.of("ht", n))
                out_g = vecs[:, bass.ds(n + VEC["mlstm_out_g"], 1)]
                nc.vector.scalar_tensor_tensor(ml_out[:, :].rearrange("p (b n) -> p b n", b=2), PS[:, 3:5, :], out_g,
                                               ml_o[e][:, 0:TP].rearrange("p (b n) -> p b n", b=2), ALU.mult, ALU.mult).then_inc(MV.sem, 1)
            heads_of(dve, body)

        FB = 3 * ROW + 4096
        fx_q, fx_k, fx_v, fx_F = ([at("hl", f"{n}{e}", [p, w], e * FB + off) for e in range(2)] for n, p, w, off in (
            ("fx_q", DH, T, 0), ("fx_k", DH, T, ROW), ("fx_v", DH, T, 2 * ROW), ("fx_F", P, TP, 3 * ROW)))
        fx_s = [at("hl", f"fx_s{e}", [P, TP], 2 * FB + 4096 * e) for e in range(2)]
        fx_p = [at("hl", f"fx_p{e}", [P, TP], 2 * FB + 8192 + 4096 * e) for e in range(2)]
        fx_pt = [at("o", f"fx_pt{e}", [P, NT, P], 12608 + 4096 * e) for e in range(2)]
        fx_Fd = at("o", "fx_Fd", [P, NT, P], 20800)
        fx_qs = at("o", "fx_qs", [DH, TP], 24896)
        fx_on = at("s", "fx_on", [P, NT, DH], 0)
        fx_vt = at("s", "fx_vt", [P, NT, DH], 2048)
        fx_kt = at("s", "fx_kt", [P, NT, DH], 4096)
        fx_of = at("s", "fx_of", [DH, TP], 6144)
        fx_mx = at("s", "fx_mx", [P, 2, NT], 10240)
        fx_nm, fx_rs, fx_ri = (at("s", n, [P, NT], 10304 + 32 * i) for i, n in enumerate(("fx_nm", "fx_rs", "fx_ri")))
        fx_in = [sem("fx_in0"), sem("fx_in1")]
        FQ, FT, FV, FO = sem("fx_scores"), sem("fx_turned"), sem("fx_pv"), sem("fx_out_turned")
        fx_kv_turned = sem("fx_kv_turned")
        fx_kv_kept = sem("fx_kv_kept")
        fx_scaled, fx_prob = sem("fx_scaled"), sem("fx_prob")
        fx_part, fx_max, fx_neg = sem("fx_part"), sem("fx_max"), sem("fx_neg")
        fx_ptk = sem("fx_ptk")
        fx_inv, fx_norm = sem("fx_inv"), sem("fx_norm")
        fx_diag = sem("fx_diag")
        fx_kept = sem("fx_kept")
        fx_stored, fx_turn = sem("fx_stored"), sem("fx_turn")

        def fox_heads(eng, body):
            with eng.Fori(0, FH // 2) as i:
                for e in range(2):
                    body(2 * i + e, e, i)

        def fox_sync(sp):
            sp.wait_ge(ml_stored, 48 * MH)
            sp.wait_ge(stored[0], 16 * plan["out0"][0] - 16)

            def body(n, e, i):
                sp.wait_ge(fx_norm, (i * 2 + e) * NT - (NT if e else 0) if e else i * (2 * NT))
                src = lambda row: proj[bass.ds(n * DH + row, DH), :]
                sp.dma_start(fx_q[e][:, :], src(1536)).then_inc(fx_in[e], 16)
                sp.dma_start(fx_k[e][:, :], src(2048)).then_inc(fx_in[e], 16)
                sp.dma_start(fx_v[e][:, :], src(2560)).then_inc(fx_in[e], 16)
                sp.dma_start(fx_F[e][:, :], frow[bass.ds(n, 1), :].broadcast_to([P, TP])).then_inc(fx_in[e], 16)
            fox_heads(sp, body)

        def fox_end(sp):
            sp.wait_ge(fx_stored, 48 * FH)

        def fox_gpsimd(pool):
            def body(n, e, i):
                pool.wait_ge(fx_in[e], i * 64 + 64)
                pool.wait_ge(fx_max, n * NT)
                nc.gpsimd.tensor_tensor(fx_Fd[:, :, :], fx_F[e][:, :].rearrange("p (c n) -> p c n", c=NT),
                                        mask_ts[:, :].rearrange("p (o n) -> p o n", o=1).broadcast_to([P, NT, P]), ALU.add).then_inc(fx_diag, 1)
            fox_heads(pool, body)

        def fox_tensor(pe):
            pe.wait_ge(MV.sem, MV.of("out", MH - 1))

            def scores(n, e, b):
                j = b % 2
                w = P * (b + 1)
                if b >= 2:
                    pe.wait_ge(fx_max, n * NT + (b - 1))
                else:
                    pe.wait_ge(fx_max, n * NT)
                for x in range(0, w, 512):
                    m = min(512, w - x)
                    mm = nc.tensor.matmul(PS[:, 2 * j + x // 512, 0:m], fx_qs[:, P * b:P * b + P], fx_k[e][:, x:x + m], start=True, stop=True)
                mm.then_inc(FQ, 1)

            def weights(n, b):
                pe.wait_ge(fx_prob, n * NT + (b + 1))
                pe.wait_ge(fx_ptk, n * NT + b)
                for c in range(b + 1):
                    mm = nc.tensor.transpose(PS[:, 4 + c // 4, P * (c % 4):P * (c % 4) + P], fx_p[b % 2][:, P * c:P * c + P], ident[:, :])
                mm.then_inc(FT, 1)

            def product(n, b):
                pe.wait_ge(fx_ptk, n * NT + (b + 1))
                pe.wait_ge(fx_norm, n * NT + b)
                for c in range(b + 1):
                    mm = nc.tensor.matmul(PS[:, 6, 0:DH], fx_pt[b % 2][:, c, :], fx_vt[:, c, :], start=(c == 0), stop=(c == b))
                mm.then_inc(FV, 1)

            def body(n, e, i):
                pe.wait_ge(fx_in[e], i * 64 + 64)
                pe.wait_ge(fx_kept, n)
                for r, src in enumerate((fx_v[e], fx_k[e])):
                    if r:
                        pe.wait_ge(fx_kv_kept, n * 2 + 1)
                    pe.sem_inc(fx_turn, 1)
                    for c in range(NT):
                        mm = nc.tensor.transpose(PS[:, 7, DH * c:DH * c + DH], src[:, P * c:P * c + P], ident[0:DH, 0:DH])
                    mm.then_inc(fx_kv_turned, 1)
                pe.wait_ge(fx_scaled, n + 1)
                pe.wait_ge(fx_kv_kept, n * 2 + 2)
                scores(n, e, 0)
                for b in range(NT):
                    if b + 1 < NT:
                        scores(n, e, b + 1)
                    weights(n, b)
                    product(n, b)
                pe.wait_ge(fx_norm, n * NT + NT)
                pe.sem_inc(fx_turn, 1)
                for c in range(NT):
                    mm = nc.tensor.transpose(PS[0:DH, 6 + c // 4, P * (c % 4):P * (c % 4) + P], fx_on[:, c, :], ident[:, :])
                mm.then_inc(FO, 1)
            fox_heads(pe, body)

        def fox_scalar(act):
            def body(n, e, i):
                act.wait_ge(fx_in[e], i * 64 + 64)
                act.wait_ge(FQ, n * NT)
                nc.scalar.mul(fx_qs[:, :], fx_q[e][:, 0:TP], DH ** -0.5).then_inc(fx_scaled, 1)
                act.wait_ge(FV, n * NT)
                act.wait_ge(fx_stored, n * 48)
                for r, dst in enumerate((fx_vt, fx_kt)):
                    act.wait_ge(fx_kv_turned, n * 2 + (r + 1))
                    nc.scalar.copy(dst[:, :, :].rearrange("p c d -> p (c d)"), PS[:, 7, :]).then_inc(fx_kv_kept, 1)
                for r, (src, name) in enumerate(((fx_vt, "p_fox_v"), (fx_kt, "p_fox_k"))):
                    act.wait_ge(fx_kv_kept, n * 2 + 2)
                    act.dma_start(io[name][0, 0, :, bass.ds(n, 1), :].rearrange("(c p) o d -> p c (o d)", p=P), src[:, :, :]).then_inc(fx_stored, 16)
                for b in range(NT):
                    act.wait_ge(fx_neg, n * NT + (b + 1))
                    act.wait_ge(FT, n * NT + b - 1 if b >= 1 else n * NT)
                    nc.scalar.activation(fx_p[b % 2][:, 0:P * (b + 1)], fx_s[b % 2][:, 0:P * (b + 1)], ACT.Exp,
                                         bias=fx_nm[:, b:b + 1], accum_out=fx_rs[:, b:b + 1]).then_inc(fx_prob, 1)
                act.wait_ge(FO, n + 1)
                nc.scalar.copy(fx_of[:, :].rearrange("p (b n) -> p b n", b=2), PS[0:DH, 6:8, :]).then_inc(fx_kept, 1)
                act.wait_ge(fx_kept, n + 1)
                act.dma_start(mix[bass.ds(n * DH + 512, DH), 0:TP], fx_of[:, :]).then_inc(fx_stored, 16)
            fox_heads(act, body)

        def fox_vector(dve):
            def soft(n, e, b):
                j = b % 2
                dve.wait_ge(FQ, n * NT + (b + 1))
                if b >= 1:
                    dve.wait_ge(fx_prob, n * NT + b - 1)
                else:
                    dve.wait_ge(fx_prob, n * NT)
                both = PS[:, 2 * j:2 * j + 2, :].rearrange("p b n -> p (b n)")
                dve.sem_inc(fx_turn, 1)
                first = -3.0e38
                if b:
                    nc.vector.tensor_tensor_reduce(fx_s[j][:, 0:P * b], both[:, 0:P * b], fx_F[e][:, 0:P * b], 1.0, -3.0e38,
                                                   ALU.add, ALU.max, fx_mx[:, 0, b:b + 1]).then_inc(fx_part, 1)
                    dve.wait_ge(fx_part, n * (NT - 1) + b)
                    dve.sem_inc(fx_turn, 1)
                    first = fx_mx[:, 0, b:b + 1]
                nc.vector.tensor_tensor_reduce(fx_s[j][:, P * b:P * b + P], both[:, P * b:P * b + P], fx_Fd[:, b, :], 1.0, first,
                                               ALU.add, ALU.max, fx_mx[:, 1, b:b + 1]).then_inc(fx_max, 1)
                dve.wait_ge(fx_max, n * NT + (b + 1))
                nc.vector.tensor_scalar(fx_nm[:, b:b + 1], fx_mx[:, 1, b:b + 1], -1.0, None, ALU.mult).then_inc(fx_neg, 1)

            def turned(n, b):
                dve.wait_ge(FT, n * NT + (b + 1))
                dve.wait_ge(FV, n * NT + b - 1 if b >= 1 else n * NT)
                k = min(4, b + 1)
                m = b + 1 - k
                if m:
                    nc.vector.tensor_copy(fx_pt[b % 2][:, 0:4, :].rearrange("p c n -> p (c n)"), PS[:, 4, :])
                    nc.vector.tensor_copy(fx_pt[b % 2][:, 4:4 + m, :].rearrange("p c n -> p (c n)"), PS[:, 5, 0:P * m]).then_inc(fx_ptk, 1)
                else:
                    nc.vector.tensor_copy(fx_pt[b % 2][:, 0:k, :].rearrange("p c n -> p (c n)"), PS[:, 4, 0:P * k]).then_inc(fx_ptk, 1)

            def out(n, b):
                nc.vector.reciprocal(fx_ri[:, b:b + 1], fx_rs[:, b:b + 1]).then_inc(fx_inv, 1)
                dve.wait_ge(fx_inv, n * NT + (b + 1))
                dve.wait_ge(FV, n * NT + (b + 1))
                nc.vector.tensor_scalar(fx_on[:, b, :], PS[:, 6, 0:DH], fx_ri[:, b:b + 1], None, ALU.mult).then_inc(fx_norm, 1)

            def body(n, e, i):
                dve.wait_ge(fx_diag, n + 1)
                dve.wait_ge(FO, n)
                soft(n, e, 0)
                for b in range(NT):
                    if b + 1 < NT:
                        soft(n, e, b + 1)
                    turned(n, b)
                    out(n, b)
            fox_heads(dve, body)

        def packer(region, start=0):
            off = [start]

            def put(name, shape, dt=F32):
                a = off[0]
                off[0] += (4 * int(np.prod(shape[1:])) + 31) // 32 * 32
                return at(region, name, shape, a, dt)
            return put

        BH = NS * MH
        BF = NS * FH
        NP = NS * NPAGES
        R4 = 4
        put = packer("hl")
        d_v = put("d_v", [P, NP, FH * DH])
        d_k = [put(f"d_k{e}", [P, FH * DH]) for e in range(2)]
        d_qb = [put(f"d_qb{e}", [P, FH * DH]) for e in range(2)]
        d_kq = put("d_kq", [P, FH * DH])
        d_C = put("d_C", [P, DK // R4, DV])
        d_Ct = put("d_Ct", [P, DK // R4, DV])
        put = packer("o")
        d_fm = put("d_fm", [P, 24, NS])
        d_tm = put("d_tm", [NS, 24 * P])
        d_sc = put("d_sc", [P, NPAGES, BF])
        d_lf = put("d_lf", [P, NPAGES, BF])
        d_st = put("d_st", [BF, 2 * PAGE + 1])
        d_pr = put("d_pr", [BF, 2 * PAGE + 1])
        d_pt = put("d_pt", [P, NPAGES, BF])
        d_self, d_wself = put("d_self", [NS, FH]), put("d_wself", [NS, FH])
        d_w2 = put("d_w2", [NS, 4, NS, 2])
        d_qk = put("d_qk", [NS, FH * DH])
        d_ld = put("d_ld", [FH, NS, FH])
        d_tri = put("d_tri", [P, P])
        d_of = put("d_of", [P, 4, NS])
        put = packer("s")
        d_spread = put("d_spread", [BH, P])
        d_gather = put("d_gather", [P, BH])
        d_row = put("d_row", [BH, DV + 3])
        d_rep = put("d_rep", [P, DV + 3])
        d_q4, d_k4, d_n4, d_t4 = (put(n, [P, DK // R4]) for n in ("d_q4", "d_k4", "d_n4", "d_t4"))
        d_par = put("d_par", [P, DV + 3])
        d_sum = put("d_sum", [BH, DV + 3])
        d_h, d_hn = put("d_h", [BH, DV]), put("d_hn", [BH, DV])
        d_sq = put("d_sq", [BH, DV])
        d_hm = put("d_hm", [P, MH, NS])
        d_c = put("d_c", [P, 16])
        d_max, d_sumw, d_inv = (put(n, [BF, 1]) for n in ("d_max", "d_sumw", "d_inv"))
        d_pg = put("d_pg", [1, NP], I32)
        sam = dram("sam", [NS, 24 * P])
        d_fm_in, d_state_in, d_rows_in, d_lf_in, d_pg_in, d_self_in, d_wself_in, d_out, d_sam_out = (
            sem(s) for s in ("d_fm_in", "d_state_in", "d_rows_in", "d_lf_in", "d_pg_in", "d_self_in", "d_wself_in", "d_out", "d_sam_out"))
        d_k_in, d_v_in, d_q_in = [sem("d_k_in0"), sem("d_k_in1")], sem("d_v_in"), [sem("d_q_in0"), sem("d_q_in1")]
        d_kq_done, d_sc_done = sem("d_kq_done"), sem("d_sc_done")
        EP = Steps(sem("d_pool"), "z1 z2 tri s1 s2 g1 g2".split())
        ET = Steps(sem("d_pe"), "turn rep bias st pt pv sum hm".split())
        EA = Steps(sem("d_act"), "tm rep winter wintra em exp pt of0 of1 sq ln rs".split())
        EV = Steps(sem("d_dve"), ("lfm m di da kw nt n ct c cq cs nq ns e4 m4 qk self ld bias st self8 max neg inv pr "
                                  "w0 w1 w2 w3 dsum dneg dabs dmax dinv h hn hm0 hm1 hm2 hm3").split())

        def dec0_sync(sp):
            sp.wait_ge(fx_stored, 48 * FH)
            sp.wait_ge(stored[0], 16 * (plan["out0"][0] - 1))
            sp.wait_ge(stored[1], 16 * plan["out0"][1])
            sp.wait_ge(rows_out, 128)
            sp.dma_start(d_fm[:, :, :], proj.rearrange("(k p) t -> p k t", p=P)[:, :, TP:T]).then_inc(d_fm_in, 16)
            sp.dma_start(d_C[:, :, :], io["state_mlstm_c"][0].rearrange("b h (r d) v -> (b h r) d v", r=R4)).then_inc(d_state_in, 16)
            sp.dma_start(d_n4[:, :], io["state_mlstm_n"][0].rearrange("b h (r d) -> (b h r) d", r=R4)).then_inc(d_state_in, 16)
            sp.dma_start(d_row[:, DV + 2:DV + 3], io["state_mlstm_m"][0].rearrange("b (h o) -> (b h) o", o=1), allow_slow_non_contiguous=True).then_inc(d_rows_in, 16)
            for j in range(2):
                for h in range(MH):
                    sp.dma_start(d_row[h:BH:MH, DV + j:DV + j + 1], lfs[j, h:h + 1, :].rearrange("h b -> b h"), allow_slow_non_contiguous=True).then_inc(d_rows_in, 16)
            sp.dma_start(d_pg[:, :], io["page_table"].rearrange("(o b) n -> o (b n)", o=1)).then_inc(d_pg_in, 16)
            sp.wait_ge(EA.sem, EA["tm"])
            sp.dma_start(sam, d_tm[:, :]).then_inc(d_sam_out, 16)
            sp.dma_start(io["s_fox_k"][0].rearrange("b o h d -> b (o h d)"), d_tm[:, 2048:2560]).then_inc(d_out, 16)
            sp.dma_start(io["s_fox_v"][0].rearrange("b o h d -> b (o h d)"), d_tm[:, 2560:3072]).then_inc(d_out, 16)
            sp.dma_start(d_q4[:, :], d_tm[:, 0:256]).then_inc(d_state_in, 16)
            sp.dma_start(d_k4[:, :], d_tm[:, 256:512]).then_inc(d_state_in, 16)
            sp.dma_start(d_row[:, 0:DV], d_tm[:, 512:1024]).then_inc(d_rows_in, 16)
            sp.wait_ge(d_sam_out, 16)
            sp.wait_ge(d_pg_in, 16)
            for b in range(NS):
                if b >= 2:
                    sp.wait_ge(d_kq_done, 2 * b - 2)
                sp.dma_start(d_qb[b % 2][:, :], sam[b:b + 1, 1536:2048].broadcast_to([P, FH * DH])).then_inc(d_q_in[b % 2], 16)
                for p in range(NPAGES):
                    i = NPAGES * b + p
                    page = sp.value_load(d_pg[0:1, i:i + 1], min_val=0, max_val=io["cache_fox_k"].shape[1] - 1)
                    if i >= 2:
                        sp.wait_ge(d_kq_done, i - 1)
                    sp.dma_start(d_k[i % 2][:, :], io["cache_fox_k"][0, bass.ds(page, 1)].rearrange("o t h d -> (o t) (h d)")).then_inc(d_k_in[i % 2], 16)
                    sp.dma_start(d_v[:, i, :], io["cache_fox_v"][0, bass.ds(page, 1)].rearrange("o t h d -> (o t) (h d)")).then_inc(d_v_in, 16)
                    sp.dma_start(d_lf[:, p, FH * b:FH * b + FH], io["cache_fox_lf"][0, bass.ds(page, 1)].rearrange("o t h -> (o t) h")).then_inc(d_lf_in, 16)
            sp.wait_ge(EV.sem, EV["c"])
            sp.dma_start(io["s_mlstm_c"][0].rearrange("b h (r d) v -> (b h r) d v", r=R4), d_C[:, :, :]).then_inc(d_out, 16)
            sp.dma_start(io["s_mlstm_n"][0].rearrange("b h (r d) -> (b h r) d", r=R4), d_n4[:, :]).then_inc(d_out, 16)
            sp.wait_ge(EV.sem, EV["self"])
            sp.dma_start(d_st[:, 2 * PAGE:2 * PAGE + 1], d_self[:, :], allow_slow_non_contiguous=True).then_inc(d_self_in, 16)
            sp.wait_ge(EV.sem, EV["pr"])
            sp.dma_start(d_wself[:, :], d_pr[:, 2 * PAGE:2 * PAGE + 1], allow_slow_non_contiguous=True).then_inc(d_wself_in, 16)
            sp.wait_ge(EA.sem, EA["of1"])
            sp.dma_start(mix[512:1024, TP:T].rearrange("(j p) t -> p j t", p=P), d_of[:, :, :]).then_inc(d_out, 16)
            sp.wait_ge(EV.sem, EV["hm3"])
            sp.dma_start(io["s_mlstm_m"][0].rearrange("b (h o) -> (b h) o", o=1), d_sum[:, DV + 2:DV + 3], allow_slow_non_contiguous=True).then_inc(d_out, 16)
            sp.dma_start(mix[0:512, TP:T].rearrange("(j p) t -> p j t", p=P), d_hm[:, :, :]).then_inc(d_out, 16)

        def dec0_end(sp):
            sp.wait_ge(d_out, 16 * 7)

        def dec0_gpsimd(pool):
            pool.wait_ge(fx_stored, 48 * FH)
            EP.chain(pool, pool.memset(d_spread[:, :], 1.0), "z1")
            EP.chain(pool, pool.memset(d_gather[:, :], 1.0), "z2")
            EP.chain(pool, pool.affine_select(out=d_tri[:, :], in_=ones[:, :], compare_op=ALU.is_ge, fill=0.0,
                                              base=-1, pattern=[[-1, P]], channel_multiplier=1), "tri")
            for name, base, m in (("s1", 0, 1), ("s2", R4 - 1, -1)):
                EP.chain(pool, pool.affine_select(out=d_spread[:, :], in_=d_spread[:, :], compare_op=ALU.is_ge, fill=0.0,
                                                  base=base, pattern=[[m, P]], channel_multiplier=-m * R4), name)
            for name, base, m in (("g1", 0, 1), ("g2", R4 - 1, -1)):
                EP.chain(pool, pool.affine_select(out=d_gather[:, :], in_=d_gather[:, :], compare_op=ALU.is_ge, fill=0.0,
                                                  base=base, pattern=[[-m * R4, BH]], channel_multiplier=m), name)

        def dec0_tensor(pe):
            pe.wait_ge(fx_kept, FH)
            pe.wait_ge(d_fm_in, 16)
            for k in range(24):
                mm = nc.tensor.transpose(PS[0:NS, k // 4, P * (k % 4):P * (k % 4) + P], d_fm[:, k, :], ident[:, :])
            mm.then_inc(ET.sem, 1)
            pe.wait_ge(EP.sem, EP["g2"])
            pe.wait_ge(d_rows_in, 16 * (2 + 2 * MH))
            nc.tensor.matmul(PS[:, 6, 0:DV + 3], d_spread[:, :], d_row[:, :], start=True, stop=True).then_inc(ET.sem, 1)
            pe.wait_ge(d_lf_in, 16 * NP)
            pe.wait_ge(EV.sem, EV["ld"])
            nc.tensor.matmul(PS[:, 7, BF:2 * BF], d_tri[:, :], d_lf[:, 1, :], start=True, stop=False)
            nc.tensor.matmul(PS[:, 7, BF:2 * BF], ones[0:FH, :], d_ld[:, :, :].rearrange("p b h -> p (b h)"), start=False, stop=True)
            nc.tensor.matmul(PS[:, 7, 0:BF], d_tri[:, :], d_lf[:, 0, :], start=True, stop=False)
            nc.tensor.matmul(PS[:, 7, 0:BF], ones[:, :], d_lf[:, 1, :], start=False, stop=False)
            nc.tensor.matmul(PS[:, 7, 0:BF], ones[0:FH, :], d_ld[:, :, :].rearrange("p b h -> p (b h)"), start=False, stop=True).then_inc(ET.sem, 1)
            pe.wait_ge(EV.sem, EV["bias"])
            pe.wait_ge(EA.sem, EA["tm"])
            for p in range(NPAGES):
                mm = nc.tensor.transpose(PS[0:BF, 0, P * p:P * p + P], d_sc[:, p, :], ident[:, :])
            mm.then_inc(ET.sem, 1)
            pe.wait_ge(EV.sem, EV["pr"])
            for p in range(NPAGES):
                mm = nc.tensor.transpose(PS[:, 1, BF * p:BF * p + BF], d_pr[:, P * p:P * p + P], ident[0:BF, 0:BF])
            mm.then_inc(ET.sem, 1)
            pe.wait_ge(d_v_in, 16 * NP)
            pe.wait_ge(EV.sem, EV["w3"])
            pe.wait_ge(EA.sem, EA["pt"])
            for j in range(4):
                out = lambda b: PS[:, 2, 2 * (NS * j + b):2 * (NS * j + b) + 2]
                nc.tensor.matmul(PS[:, 2, 2 * NS * j:2 * NS * (j + 1)], d_tm[:, 2560 + P * j:2560 + P * j + P],
                                 d_w2[:, j, :, :].rearrange("p b e -> p (b e)"), start=True, stop=False, skip_group_check=True)
                for i in range(NP):
                    b, p = i // NPAGES, i % NPAGES
                    mm = nc.tensor.matmul(out(b), d_v[:, i, P * j:P * j + P], d_pt[:, p, FH * b + 2 * j:FH * b + 2 * j + 2],
                                          start=False, stop=(i == NP - 1), skip_group_check=True)
            mm.then_inc(ET.sem, 1)
            pe.wait_ge(EV.sem, EV["m4"])
            nc.tensor.matmul(PS[0:BH, 3, 0:DV + 3], d_gather[:, :], d_par[:, :], start=True, stop=True).then_inc(ET.sem, 1)
            pe.wait_ge(EV.sem, EV["hn"])
            nc.tensor.transpose(PS[:, 4, 0:BH], d_hn[:, :], ident[0:BH, 0:BH]).then_inc(ET.sem, 1)

        d_col = lambda i: d_c[:, i:i + 1]
        LFM, MN, DI, DA, WI, WA = (d_col(i) for i in range(6))
        DN, DX, RI, LN_, RS, SS = (d_c[0:BH, 6 + i:7 + i] for i in range(6))

        def dec0_scalar(act):
            act.wait_ge(ET.sem, ET["turn"])
            EA.chain(act, nc.scalar.copy(d_tm[:, :].rearrange("p (b n) -> p b n", b=6), PS[0:NS, 0:6, :]), "tm")
            act.wait_ge(ET.sem, ET["rep"])
            EA.chain(act, nc.scalar.copy(d_rep[:, :], PS[:, 6, 0:DV + 3]), "rep")
            act.wait_ge(EV.sem, EV["da"])
            EA.chain(act, nc.scalar.activation(WI, DI, ACT.Exp), "winter")
            EA.chain(act, nc.scalar.activation(WA, DA, ACT.Exp), "wintra")
            EA.chain(act, nc.scalar.activation(d_par[:, DV + 1:DV + 2], MN, ACT.Exp, scale=-1.0), "em")
            act.wait_ge(EV.sem, EV["neg"])
            EA.chain(act, nc.scalar.activation(d_pr[:, :], d_st[:, :], ACT.Exp, bias=d_max[:, :], accum_out=d_sumw[:, :]), "exp")
            act.wait_ge(ET.sem, ET["pt"])
            EA.chain(act, nc.scalar.copy(d_pt[:, :, :].rearrange("p n b -> p (n b)"), PS[:, 1, 0:2 * BF]), "pt")
            act.wait_ge(ET.sem, ET["pv"])
            out = PS[:, 2, 0:2 * NS * 4].rearrange("p (j b e) -> p j b e", j=4, e=2)
            for e in range(2):
                EA.chain(act, nc.scalar.copy(d_of[64 * e:64 * e + 64, :, :], out[64 * e:64 * e + 64, :, :, e]), f"of{e}")
            act.wait_ge(EV.sem, EV["h"])
            EA.chain(act, nc.scalar.activation(d_sq[:, :], d_h[:, :], ACT.Square, accum_out=SS), "sq")
            EA.chain(act, nc.scalar.activation(LN_, SS, ACT.Ln, bias=EPS_C[0:BH, :], scale=1.0 / DV), "ln")
            EA.chain(act, nc.scalar.activation(RS, LN_, ACT.Exp, scale=-0.5), "rs")

        def dec0_vector(dve):
            c = lambda ins, name: EV.chain(dve, ins, name)
            tt, ts, stt = nc.vector.tensor_tensor, nc.vector.tensor_scalar, nc.vector.scalar_tensor_tensor
            IG, LF, M0 = (d_rep[:, DV + j:DV + j + 1] for j in range(3))
            cut = lambda ap, o: ap.rearrange("p (d o) -> p d o", o=1).broadcast_to([P, DK // R4, DV])
            dve.wait_ge(EA.sem, EA["rep"])
            c(tt(LFM, LF, M0, ALU.add), "lfm")
            c(tt(MN, LFM, IG, ALU.max), "m")
            c(tt(DI, LFM, MN, ALU.subtract), "di")
            c(tt(DA, IG, MN, ALU.subtract), "da")
            dve.wait_ge(EA.sem, EA["wintra"])
            dve.wait_ge(d_state_in, 64)
            c(ts(d_k4[:, :], d_k4[:, :], WA, DK ** -0.5, ALU.mult, ALU.mult), "kw")
            c(ts(d_n4[:, :], d_n4[:, :], WI, None, ALU.mult), "nt")
            c(tt(d_n4[:, :], d_n4[:, :], d_k4[:, :], ALU.add), "n")
            vrep = d_rep[:, 0:DV].rearrange("p (o v) -> p o v", o=1).broadcast_to([P, DK // R4, DV])
            c(tt(d_Ct[:, :, :], cut(d_k4[:, :], 1), vrep, ALU.mult), "ct")
            c(stt(d_C[:, :, :], d_C[:, :, :], WI, d_Ct[:, :, :], ALU.mult, ALU.add), "c")
            c(tt(d_Ct[:, :, :], d_C[:, :, :], cut(d_q4[:, :], 1), ALU.mult), "cq")
            c(nc.vector.tensor_reduce(d_par[:, 0:DV], d_Ct[:, :, :].rearrange("p d v -> p v d"), AX.X, ALU.add), "cs")
            c(tt(d_t4[:, :], d_n4[:, :], d_q4[:, :], ALU.mult), "nq")
            c(nc.vector.tensor_reduce(d_par[:, DV:DV + 1], d_t4[:, :], AX.X, ALU.add), "ns")
            dve.wait_ge(EA.sem, EA["em"])
            c(ts(d_par[:, DV + 1:DV + 2], d_par[:, DV + 1:DV + 2], 1.0 / R4, None, ALU.mult), "e4")
            c(ts(d_par[:, DV + 2:DV + 3], MN, 1.0 / R4, None, ALU.mult), "m4")
            c(tt(d_qk[:, :], d_tm[:, 1536:2048], d_tm[:, 2048:2560], ALU.mult), "qk")
            c(nc.vector.tensor_reduce(d_self[:, :], d_qk[:, :].rearrange("p (h d) -> p h d", h=FH), AX.X, ALU.add), "self")
            c(tt(d_ld[:, :, :], ident[0:FH, 0:FH].rearrange("p (o h) -> p o h", o=1).broadcast_to([FH, NS, FH]),
                 g_ff[:, TP:T].rearrange("p (b o) -> p b o", o=1).broadcast_to([FH, NS, FH]), ALU.mult), "ld")
            for i in range(NP):
                b, p = i // NPAGES, i % NPAGES
                dve.wait_ge(d_q_in[b % 2], 16 * (b // 2 + 1))
                dve.wait_ge(d_k_in[i % 2], 16 * (i // 2 + 1))
                if i:
                    dve.wait_ge(d_sc_done, i)
                tt(d_kq[:, :], d_k[i % 2][:, :], d_qb[b % 2][:, :], ALU.mult).then_inc(d_kq_done, 1)
                dve.wait_ge(d_kq_done, i + 1)
                nc.vector.tensor_reduce(d_sc[:, p, FH * b:FH * b + FH], d_kq[:, :].rearrange("p (h d) -> p h d", h=FH), AX.X, ALU.add).then_inc(d_sc_done, 1)
            dve.wait_ge(d_sc_done, NP)
            dve.wait_ge(ET.sem, ET["bias"])
            c(stt(d_sc[:, :, :], d_sc[:, :, :], DH ** -0.5, PS[:, 7, 0:2 * BF].rearrange("p (n b) -> p n b", n=NPAGES), ALU.mult, ALU.add), "bias")
            dve.wait_ge(ET.sem, ET["st"])
            dve.wait_ge(d_self_in, 16)
            c(nc.vector.tensor_copy(d_st[:, 0:2 * PAGE], PS[0:BF, 0, 0:2 * PAGE]), "st")
            c(ts(d_st[:, 2 * PAGE:2 * PAGE + 1], d_st[:, 2 * PAGE:2 * PAGE + 1], DH ** -0.5, None, ALU.mult), "self8")
            c(nc.vector.tensor_reduce(d_inv[:, :], d_st[:, :], AX.X, ALU.max), "max")
            c(ts(d_max[:, :], d_inv[:, :], -1.0, None, ALU.mult), "neg")
            dve.wait_ge(EA.sem, EA["exp"])
            c(nc.vector.reciprocal(d_inv[:, :], d_sumw[:, :]), "inv")
            c(ts(d_pr[:, :], d_pr[:, :], d_inv[:, :], None, ALU.mult), "pr")
            dve.wait_ge(d_wself_in, 16)
            for j in range(4):
                c(tt(d_w2[:, j, :, :], ident[0:NS, 0:NS].rearrange("p (b o) -> p b o", o=1).broadcast_to([NS, NS, 2]),
                     d_wself[:, 2 * j:2 * j + 2].rearrange("p (o e) -> p o e", o=1).broadcast_to([NS, NS, 2]), ALU.mult), f"w{j}")
            dve.wait_ge(ET.sem, ET["sum"])
            c(nc.vector.tensor_copy(d_sum[:, :], PS[0:BH, 3, 0:DV + 3]), "dsum")
            c(ts(DN, d_sum[:, DV:DV + 1], -1.0, None, ALU.mult), "dneg")
            c(tt(DN, DN, d_sum[:, DV:DV + 1], ALU.max), "dabs")
            c(tt(DX, DN, d_sum[:, DV + 1:DV + 2], ALU.max), "dmax")
            c(nc.vector.reciprocal(RI, DX), "dinv")
            c(ts(d_h[:, :], d_sum[:, 0:DV], RI, None, ALU.mult), "h")
            dve.wait_ge(EA.sem, EA["rs"])
            c(ts(d_hn[:, :], d_h[:, :], RS, None, ALU.mult), "hn")
            dve.wait_ge(ET.sem, ET["hm"])
            for h in range(MH):
                c(stt(d_hm[:, h, :], PS[:, 4, 0:BH].rearrange("p (b h) -> p b h", h=MH)[:, :, h], vec("mlstm_out_g", h),
                      d_fm[:, 8 + h, :], ALU.mult, ALU.mult), f"hm{h}")

        mix_in = [sem("mix_in0"), sem("mix_in1")]

        def mix_sync(sp, n, src):
            for half in range(2):
                sp.dma_start(oT[:, 4 * half:4 * half + 4, :], src.rearrange("(k p) t -> p k t", p=P)[:, 4 * half:4 * half + 4, :]).then_inc(mix_in[half], 16)

        def mix_split_vector(dve, r, n):
            def make(k):
                if k % 4 == 0:
                    dve.wait_ge(mix_in[k // 4], 16 * n + 16)
                return nc.vector.tensor_copy(hf[:, k % 2, :], oT[:, k, :])
            split_vector(dve, r, make)

        def after(name):
            return lambda eng: [eng.wait_ge(psum_free[u], plan[name][u]) for u in range(2)]

        xx = at("h", "xx", [P, KT, T], 0)
        sh_in = at("hl", "sh_in", [NS, D], 0)
        sh_out = at("s", "sh_out", [NS + 1, D], 2 * ROW)
        lora = at("s", "lora", [P, T], 2 * ROW)
        rw = dram("rw", [6 * D, T])
        RW = {n: i * D for i, n in enumerate("rkvsag")}
        mix2 = dram("mix2", [D, T])
        sh_loaded, sh_turned, h_ready, xx_ready, sh_full, sh_kept, sh_stored = (
            sem(s) for s in ("sh_loaded", "sh_turned", "h_ready", "xx_ready", "sh_full", "sh_kept", "sh_stored"))
        w2_loaded, lora_ready = sem("w2_loaded"), sem("lora_ready")
        z_full, z_free = [sem("z_full0"), sem("z_full1")], [sem("z_free0"), sem("z_free1")]
        w2_in = at("s", "w2_in", [P, D], 0)
        MIXES = (("w", 1), ("a", 4), ("g", 5), ("r", 0), ("k", 2), ("v", 3))
        LORA = {"w": ("rwkv_w1", "rwkv_w2", 64, ACT.Tanh, "s"), "a": ("rwkv_a1", "rwkv_a2", 64, ACT.Copy, "a"),
                "g": ("rwkv_g1", "rwkv_g2", 128, ACT.Sigmoid, "g")}
        R0 = 3
        S0 = 12
        kt_of = lambda name: io[name][0].rearrange("(k p) n -> p k n", p=P)

        def shift_sync(sp):
            sp.wait_ge(psum_full[1], plan["a_w"][1])
            sp.dma_start(sh_in[:, :], io["state_rwkv_shift"][0]).then_inc(sh_loaded, 16)

        def shift_tensor(pe):
            pe.wait_ge(sh_loaded, 16)
            for k in range(KT):
                mm = nc.tensor.transpose(PS[:, 6, NS * k:NS * k + NS], sh_in[:, P * k:P * k + P], ident[0:NS, 0:NS])
            mm.then_inc(sh_turned, 1)
            pe.wait_ge(xx_ready, 3)
            for k in range(KT):
                mm = nc.tensor.transpose(PS[0:NS + 1, 6 + k // 4, P * (k % 4):P * (k % 4) + P], oT[:, k, TP - 1:T], ident[:, :])
            mm.then_inc(sh_full, 1)

        def shift_vector(dve):
            dve.wait_ge(rstd_ready, 5)
            for k in range(KT):
                mm = nc.vector.scalar_tensor_tensor(oT[:, k, :], xT[:, k, :], gains[:, 4, k:k + 1], rstd[:, :], ALU.mult, ALU.mult)
                mm.then_inc(h_ready, 1)
            dve.wait_ge(h_ready, KT)
            dve.wait_ge(psum_free[1], plan["a_w"][1])
            nc.vector.tensor_tensor(xx[:, :, 1:TP], oT[:, :, 0:TP - 1], oT[:, :, 1:TP], ALU.subtract).then_inc(xx_ready, 1)
            nc.vector.tensor_scalar(xx[:, :, 0:1], oT[:, :, 0:1], -1.0, None, ALU.mult).then_inc(xx_ready, 1)
            dve.wait_ge(sh_turned, 1)
            nc.vector.tensor_tensor(xx[:, :, TP:T], PS[:, 6, 0:KT * NS].rearrange("p (k n) -> p k n", k=KT),
                                    oT[:, :, TP:T], ALU.subtract).then_inc(xx_ready, 1)
            dve.wait_ge(xx_ready, 3)

        def shift_scalar(act):
            act.wait_ge(sh_full, 1)
            act.wait_ge(sq_used, KT * 5)
            act.wait_ge(ss_ready, 5)
            nc.scalar.copy(sh_out[:, :].rearrange("p (b n) -> p b n", b=2), PS[0:NS + 1, 6:8, :]).then_inc(sh_kept, 1)
            act.wait_ge(sh_kept, 1)
            act.dma_start(io["p_rwkv_shift"][0], sh_out[0:1, :]).then_inc(sh_stored, 16)
            act.dma_start(io["s_rwkv_shift"][0], sh_out[1:NS + 1, :]).then_inc(sh_stored, 16)

        def mixes_sync(sp):
            nl = 0
            for n, (m, _) in enumerate(MIXES):
                if m in LORA:
                    w1, w2, rank = LORA[m][:3]
                    load_w(sp, 0, plan[f"a_{m}"][0], kt_of(w1), w_raw[:, 0, :, 0:rank])
                    sp.wait_ge(act_ready, KT * (R0 + n + 1))
                    sp.dma_start(w2_in[0:rank, :], io[w2][0]).then_inc(w2_loaded, 16)
                else:
                    load_pairs(sp, f"a_{m}", 4, kt_of("rwkv_w_" + m))

        def mixes_gpsimd(pool):
            for m, _ in MIXES:
                k0, k1 = plan[f"a_{m}"]
                if m in LORA:
                    split_w(pool, 0, k0, KT, k0 + k1 + 1)
                else:
                    split_pairs(pool, f"a_{m}", 4, KT)

        def mixes_tensor(pe):
            for n, (m, _) in enumerate(MIXES):
                r = R0 + n
                if m not in LORA:
                    gemm_tensor(pe, f"a_{m}", 4, r)
                    continue
                rank = LORA[m][2]
                tile_products(pe, 0, plan[f"a_{m}"][0], act_hi, act_lo, KT, act_ready, KT * r)
                pe.wait_ge(lora_ready, n + 1)
                pe.wait_ge(w2_loaded, 16 * n + 16)
                for j in range(KT):
                    u = j % 2
                    if 4 * n + j // 2:
                        pe.wait_ge(z_free[u], 4 * n + j // 2)
                    for c in range(NCH):
                        mm = nc.tensor.matmul(PS[:, 3 * u + c, 0:CH], w2_in[0:rank, P * j:P * j + P], lora[0:rank, CH * c:CH * c + CH],
                                              start=True, stop=True)
                    mm.then_inc(z_full[u], 1)
                for u in range(2):
                    pe.wait_ge(z_free[u], 4 * n + 4)

        def mixes_scalar(act):
            stores = S0
            for n, (m, _) in enumerate(MIXES):
                r = R0 + n
                if n:
                    for u in range(2):
                        act.wait_ge(psum_full[u], plan[f"a_{m}"][u])
                split_scalar(act, r)
                if m not in LORA:
                    store_scalar(act, f"a_{m}", 4, rw, RW[m], stores)
                    stores += 4
                    continue
                _, _, rank, func, out = LORA[m]
                k0 = plan[f"a_{m}"][0]
                act.wait_ge(psum_full[0], k0 + 1)
                if n == 0:
                    act.wait_ge(sh_stored, 32)
                else:
                    act.wait_ge(z_full[1], 4 * n)
                nc.scalar.activation(chunks(lora[:, :])[0:rank], PS[0:rank, 0:3, 0:CH], func).then_inc(psum_free[0], 1)
                act.wait_ge(psum_free[0], k0 + 1)
                act.sem_inc(lora_ready, 1)
                for j in range(KT):
                    u = j % 2
                    act.wait_ge(z_full[u], 4 * n + j // 2 + 1)
                    act.wait_ge(stored[u], 16 * (stores + j // 2))
                    dst = chunks(stage[:, u, :])
                    if m == "g":
                        ins = nc.scalar.copy(dst, banks(u))
                    else:
                        ins = nc.scalar.activation(dst, banks(u), ACT.Sigmoid, bias=vec(f"rwkv_{m}0", j))
                    ins.then_inc(z_free[u], 1)
                    act.wait_ge(z_free[u], 4 * n + j // 2 + 1)
                    act.dma_start(rw[RW[out] + P * j:RW[out] + P * j + P, :], stage[:, u, :]).then_inc(stored[u], 16)
                stores += 4

        def mixes_vector(dve):
            for n, (m, i) in enumerate(MIXES):
                if n:
                    for u in range(2):
                        dve.wait_ge(psum_full[u], plan[f"a_{m}"][u])
                    if n <= 3:
                        dve.wait_ge(z_full[0], 4 * n)
                        dve.wait_ge(z_full[1], 4 * n)
                split_vector(dve, R0 + n, lambda k: nc.vector.scalar_tensor_tensor(
                    hf[:, k % 2, :], xx[:, k, :], vec("rwkv_mix", KT * i + k), oT[:, k, :], ALU.mult, ALU.add))

        C0 = math.exp(-0.5)
        PAIRS = RH // 2
        L2 = 2 * P
        put = packer("hl")
        b_in = {n: put(f"b_{n}", [P, T]) for n in "rksavg"}
        b_AR = put("b_AR", [P, NT, L2])
        b_B, b_K = put("b_B", [P, TP]), put("b_K", [P, TP])
        b_bv = put("b_bv", [P, T])
        b_cs, b_P, b_iP, b_Pm = (put(n, [P, T]) for n in ("b_cs", "b_P", "b_iP", "b_Pm"))
        b_kkn = put("b_kkn", [P, T])
        put = packer("o")
        b_kp, b_b = put("b_kp", [P, T]), put("b_b", [P, T])
        b_y = put("b_y", [P, NT, P])
        b_ysq = put("b_ysq", [P, NT, P])
        b_Z, b_CZ, b_W = (put(n, [P, 8, P]) for n in ("b_Z", "b_CZ", "b_W"))
        b_GT = put("b_GT", [DH, 8, P])
        put = packer("h")
        tm = {n: put(f"tm_{n}", [P, NT, P]) for n in "VABK"}
        b_ab = [put(f"b_ab{l}", [P, 4, L2]) for l in range(2)]
        b_ak = [put(f"b_ak{l}", [P, 4, L2]) for l in range(2)]
        put = packer("s")
        b_X, b_XTc, b_T1 = ([put(f"{n}{l}", [P, 4, 32]) for l in range(2)] for n in ("b_X", "b_XTc", "b_T1"))
        b_XT = [put(f"b_XT{l}", [P, 4, P]) for l in range(2)]
        b_AV = [put(f"b_AV{l}", [P, 4, DH]) for l in range(2)]
        b_T = put("b_T", [DH, NT + 1, 2, DH])
        b_MT = put("b_MT", [DH, 8, DH])
        b_so = put("b_so", [DH, 2, DH])
        b_pc, b_mid, b_dm, b_dx = (put(n, [P, 8]) for n in ("b_pc", "b_mid", "b_dm", "b_dx"))
        b_D = put("b_D", [DH, 2, NT])
        b_gm, b_gv, b_gl, b_gr = (put(n, [P, 16]) for n in ("b_gm", "b_gv", "b_gl", "b_gr"))
        over = lambda buf, name, shape, off: nc.alloc_sbuf_tensor_at(name, shape, F32, offset=slots[buf] + off)
        LEVELS = (1, 2, 4, 8, 16, 32, 64)
        b_C = [over("w_hi", f"b_C{k}", [P, 8, P], 4096 * k) for k in range(2)]
        b_lev = {m: over("w_lo", f"b_lev{m}", [P, P], 512 * i) for i, m in enumerate(LEVELS)}
        b_bd32, b_bd64 = over("w_lo", "b_bd32", [P, P], 3584), over("w_lo", "b_bd64", [P, P], 4096)
        b_mask = over("w_lo", "b_mask", [P, L2], 4608)
        b_ic = over("w_lo", "b_ic", [P, 32], 5632)
        bd_tmp = {m: at("h", f"bd_tmp{m}", [P, P], 512 * i) for i, m in enumerate((2, 4, 8, 16))}
        bd_tmp[32], bd_tmp[64] = b_bd32, b_bd64
        bd_tmp[1], bd_tmp[128] = ident, ones
        rsam = dram("rsam", [4, D, NS])
        rk_in, rv_in, b_in_free, b_stored, b_turn = (sem(s) for s in ("rk_in", "rv_in", "b_in_free", "b_stored", "b_turn"))
        pe_names, act_names, dve_names, pool_names = "ss tV tA tB tK bon dcol".split(), "P iP Pm dx sq ln rs eV eA eB eK eD".split(), \
            "pc cs mid cc dm dl ccm kk0 ssm kkn b k1 kp A B K R rk bv".split(), []
        for h in range(2):
            two = lambda n: [f"{n}_{h}{l}" for l in range(2)]
            pe_names += two("s") + two("AV") + two("T1") + [x for m in LEVELS[1:6] for x in two(f"T{m}") + two(f"X{m}")]
            pe_names += two("Z") + two("CZ") + two("XZ") + two("G") + two("M")
            pe_names += [x for c in range(4 * h, 4 * h + 4) for x in (f"c{c}", f"y{c}")]
            act_names += two("av") + [x for m in LEVELS[1:5] for x in two(f"t{m}")] + two("zc") + two("cz") + two("gc")
            act_names += [f"yc{c}" for c in range(4 * h, 4 * h + 4)]
            dve_names += two("mak") + two("mab") + [f"{x}{m}_{h}{l}" for m in LEVELS[0:5] for l in range(2) for x in ("xa", "xt", "xb")]
            dve_names += two("t32") + [f"{x}_{h}{l}" for l in range(2) for x in ("xp", "xq")] + two("w") + two("mt")
            dve_names += [f"ch{c}" for c in range(4 * h, 4 * h + 4)]
            pool_names += [x for m in LEVELS for x in two(f"cm{m}")]
        pe_names += ["yt"]
        act_names += "gsq gln grs so".split()
        dve_names += "g1 g2 g3 g4 g5 o1 o2 o3".split()
        BP, BA, BV, BG = Steps(sem("b_pe"), pe_names), Steps(sem("b_act"), act_names), Steps(sem("b_dve"), dve_names), Steps(sem("b_pool"), pool_names)
        GM = Steps(sem("b_masks"), [f"bd{m}{x}" for m in (2, 4, 8, 16, 32, 64) for x in "ab"] + [f"lev{m}" for m in LEVELS] + "m0 m1".split())
        VM = Steps(sem("b_ic_done"), "0 1 2 3".split())

        def rwb_sync(sp):
            sp.wait_ge(BG_ready, 1)
            with sp.Fori(0, PAIRS) as j:
                sp.wait_ge(b_in_free, j)
                for n in "rksa":
                    sp.dma_start(b_in[n][:, :], rw[bass.ds(j * P + RW[n], P), :]).then_inc(rk_in, 16)
                sp.wait_ge(BV.sem, j * len(BV.names))
                for n in "vg":
                    sp.dma_start(b_in[n][:, :], rw[bass.ds(j * P + RW[n], P), :]).then_inc(rv_in, 16)

        BG_ready = sem("b_region_free")

        def rwb_gpsimd(pool):
            for u in range(2):
                pool.wait_ge(psum_free[u], plan["out1"][u])
                pool.wait_ge(stored[u], 16 * 36)
            pool.sem_inc(BG_ready, 1)
            for m in (2, 4, 8, 16, 32, 64):
                view = bd_tmp[m][:, :].rearrange("p (q i) -> p q i", i=m)
                GM.chain(pool, pool.affine_select(out=view, in_=ones[:, :].rearrange("p (q i) -> p q i", i=m), compare_op=ALU.is_ge, fill=0.0,
                                                  base=0, pattern=[[-m, P // m], [0, m]], channel_multiplier=1), f"bd{m}a")
                GM.chain(pool, pool.affine_select(out=view, in_=view, compare_op=ALU.is_ge, fill=0.0,
                                                  base=m - 1, pattern=[[m, P // m], [0, m]], channel_multiplier=-1), f"bd{m}b")
            for m in LEVELS:
                GM.chain(pool, nc.gpsimd.tensor_tensor(b_lev[m][:, :], bd_tmp[2 * m][:, :], bd_tmp[m][:, :], ALU.subtract), f"lev{m}")
            GM.chain(pool, pool.affine_select(out=b_mask[:, 0:P], in_=ones[:, :], compare_op=ALU.is_ge, fill=0.0,
                                              base=-1, pattern=[[1, P]], channel_multiplier=-1), "m0")
            GM.chain(pool, pool.affine_select(out=b_mask[:, P:L2], in_=ones[:, :], compare_op=ALU.is_ge, fill=0.0,
                                              base=0, pattern=[[1, P]], channel_multiplier=-1), "m1")
            with pool.Fori(0, PAIRS) as j:
                for h in range(2):
                    for i, m in enumerate(LEVELS):
                        for l in range(2):
                            pool.wait_ge(BV.sem, BV.of(f"mab_{h}{l}", j))
                            if i >= 2:
                                pool.wait_ge(BP.sem, BP.of(f"T{LEVELS[i - 2]}_{h}{l}", j))
                            elif h:
                                pool.wait_ge(BP.sem, BP.of(f"{'T32' if i else 'CZ'}_0{l}", j))
                            pool.sem_inc(b_turn_pool, 1)
                            nc.gpsimd.tensor_tensor(b_C[i % 2][:, 4 * l:4 * l + 4, :], b_ab[l][:, :, 0:P],
                                                    b_lev[m][:, :].rearrange("p (o n) -> p o n", o=1).broadcast_to([P, 4, P]), ALU.mult).then_inc(BG.sem, 1)
            pool.wait_ge(BP.sem, PAIRS * len(BP.names))

        b_turn_pool = sem("b_turn_pool")

        def rwb_tensor(pe):
            heads = lambda e: slice(DH * e, DH * e + DH)
            def done(mm):
                mm.then_inc(BP.sem, 1)

            def body(j):
                v = lambda n: pe.wait_ge(BV.sem, BV.of(n, j))
                a = lambda n: pe.wait_ge(BA.sem, BA.of(n, j))
                g = lambda n: pe.wait_ge(BG.sem, BG.of(n, j))

                def go():
                    pe.sem_inc(b_turn, 1)
                a("sq")
                go()
                for c in range(NCH):
                    mm = nc.tensor.matmul(PS[:, c, 0:CH], b_bd64[:, :], b_b[:, CH * c:CH * c + CH], start=True, stop=True)
                done(mm)

                def turn(src, bank):
                    go()
                    for c in range(NT):
                        mm = nc.tensor.transpose(PS[:, bank + c // 4, P * (c % 4):P * (c % 4) + P], src(c), ident[:, :])
                    done(mm)
                pe.wait_ge(rv_in, j * 32 + 32)
                turn(lambda c: b_in["v"][:, P * c:P * c + P], 6)
                v("A")
                turn(lambda c: b_AR[:, c, 0:P], 0)
                v("B")
                a("eV")
                turn(lambda c: b_B[:, P * c:P * c + P], 6)
                v("K")
                a("eA")
                turn(lambda c: b_K[:, P * c:P * c + P], 0)
                v("rk")
                go()
                for c in range(NCH):
                    mm = nc.tensor.matmul(PS[:, 3 + c, 0:CH], b_bd64[:, :], b_cs[:, CH * c:CH * c + CH], start=True, stop=True)
                done(mm)
                for e in range(2):
                    mm = nc.tensor.matmul(PS[0:DH, 2, NT * e:NT * e + NT], ident[:, heads(e)], b_dx[:, :], start=True, stop=True)
                done(mm)
                a("eD")
                v("bv")
                for h in range(2):
                    us = lambda l: [(u, 4 * h + 2 * l + u % 2, u // 2) for u in range(4)]
                    for l in range(2):
                        if h:
                            v("ch3")
                            a("yc3")
                        go()
                        for u, c, e in us(l):
                            for x, (lhs, bank) in enumerate(((b_B, 4 * l), (b_K, 4 * l + 2))):
                                mm = nc.tensor.matmul(PS[:, bank + u // 2, L2 * (u % 2):L2 * (u % 2) + L2], lhs[heads(e), P * c:P * c + P],
                                                      b_AR[heads(e), c, :], start=True, stop=True)
                        done(mm)
                    for l in range(2):
                        v(f"mak_{h}{l}")
                        go()
                        for u, c, e in us(l):
                            mm = nc.tensor.matmul(PS[:, 4 * l + 2, DH * u:DH * u + DH], b_ak[l][:, u, 0:P], tm["V"][:, c, heads(e)], start=True, stop=True)
                        done(mm)
                    small = lambda l, bank, u: PS[:, 4 * l + bank, 32 * u:32 * u + 32]
                    for i, m in enumerate(LEVELS[0:6]):
                        for l in range(2):
                            g(f"cm{m}_{h}{l}")
                            if i:
                                v(f"xb{m // 2}_{h}{l}")
                            go()
                            for u in range(4):
                                mm = nc.tensor.matmul(small(l, 0, u), b_C[i % 2][:, 4 * l + u, :], b_ic[:, :] if i == 0 else b_X[l][:, u, :], start=True, stop=True)
                            done(mm)
                        if i == 0:
                            continue
                        for l in range(2):
                            if m < 32:
                                a(f"t{m}_{h}{l}")
                            else:
                                v(f"t32_{h}{l}")
                            go()
                            for u in range(4):
                                lhs, rhs = (b_XT[l][:, u, :], b_T1[l][:, u, :]) if m < 32 else (b_Z[:, 4 * l + u, :], b_XTc[l][:, u, :])
                                mm = nc.tensor.matmul(small(l, 1, u), lhs, rhs, start=True, stop=True)
                            done(mm)
                    full = lambda l, bank, u: PS[:, 4 * l + bank, P * u:P * u + P]
                    for l in range(2):
                        v(f"xq_{h}{l}")
                        a(f"av_{h}{l}")
                        go()
                        for u, c, e in us(l):
                            nc.tensor.matmul(full(l, 3, u)[:, 0:DH], b_XT[l][:, u, :], tm["A"][:, c, heads(e)], start=True, stop=True)
                            mm = nc.tensor.matmul(full(l, 3, u)[:, DH:P], b_XT[l][:, u, :], b_AV[l][:, u, :], start=True, stop=True)
                        done(mm)
                    for l in range(2):
                        g(f"cm64_{h}{l}")
                        a(f"zc_{h}{l}")
                        go()
                        for u in range(4):
                            mm = nc.tensor.matmul(full(l, 0, u), b_C[0][:, 4 * l + u, :], b_Z[:, 4 * l + u, :], start=True, stop=True)
                        done(mm)
                    for l in range(2):
                        a(f"cz_{h}{l}")
                        go()
                        for u in range(4):
                            mm = nc.tensor.matmul(full(l, 1, u), b_XT[l][:, u, :], b_CZ[:, 4 * l + u, :], start=True, stop=True)
                        done(mm)
                    for l in range(2):
                        v(f"w_{h}{l}")
                        go()
                        for u, c, e in us(l):
                            out = PS[0:DH, 4 * l + 2, P * u:P * u + P]
                            nc.tensor.matmul(out, b_W[:, 4 * l + u, 0:DH], b_ab[l][:, u, P:L2], start=True, stop=False)
                            mm = nc.tensor.matmul(out, ident[:, heads(e)], b_AR[:, c, P:L2], start=False, stop=True)
                        done(mm)
                    for l in range(2):
                        go()
                        for u, c, e in us(l):
                            mm = nc.tensor.matmul(PS[0:DH, 4 * l + 3, DH * u:DH * u + DH], b_W[:, 4 * l + u, 0:DH], tm["B"][:, c, heads(e)], start=True, stop=True)
                        done(mm)
                    for c in range(4 * h, 4 * h + 4):
                        l = (c % 4) // 2
                        at_ = lambda bank, p, e: PS[0:p, 4 * l + bank + 2 * (c % 2), DH * e:DH * e + DH]
                        v(f"ch{c - 1}" if c % 4 else f"mt_{h}1")
                        go()
                        for e in range(2):
                            u = 2 * e + c % 2
                            nc.tensor.matmul(at_(0, DH, e), tm["B"][:, c, heads(e)], b_W[:, 4 * l + u, DH:P], start=True, stop=False)
                            mm = nc.tensor.matmul(at_(0, DH, e), tm["K"][:, c, heads(e)], tm["V"][:, c, heads(e)], start=False, stop=(c == 0))
                            if c:
                                mm = nc.tensor.matmul(at_(0, DH, e), b_MT[:, 4 * l + u, :], b_T[:, c, e, :], start=False, stop=True)
                        done(mm)
                        a(f"gc_{h}{l}")
                        go()
                        for e in range(2):
                            u = 2 * e + c % 2
                            nc.tensor.matmul(at_(1, P, e), b_ab[l][:, u, P:L2], b_W[:, 4 * l + u, DH:P], start=True, stop=False)
                            mm = nc.tensor.matmul(at_(1, P, e), b_ak[l][:, u, P:L2], tm["V"][:, c, heads(e)], start=False, stop=(c == 0))
                            if c:
                                mm = nc.tensor.matmul(at_(1, P, e), b_GT[:, 4 * l + u, :], b_T[:, c, e, :], start=False, stop=True)
                        done(mm)
                v("g5")
                go()
                for c in range(NT):
                    nc.tensor.transpose(PS[:, c // 4, P * (c % 4):P * (c % 4) + P], b_y[:, c, :], ident[:, :])
                for e in range(2):
                    mm = nc.tensor.transpose(PS[0:DH, 2, DH * e:DH * e + DH], b_T[:, NT, e, :], ident[0:DH, 0:DH])
                done(mm)
            with pe.Fori(0, PAIRS) as j:
                body(j)

        def rwb_scalar(act):
            def body(j):
                v = lambda n: act.wait_ge(BV.sem, BV.of(n, j))
                p = lambda n: act.wait_ge(BP.sem, BP.of(n, j))
                done = lambda ins: ins.then_inc(BA.sem, 1)
                own = lambda n: act.wait_ge(BA.sem, BA.of(n, j))
                v("cc")
                done(nc.scalar.activation(b_P[:, 0:TP], b_cs[:, 0:TP], ACT.Exp, scale=-C0))
                done(nc.scalar.activation(b_iP[:, 0:TP], b_cs[:, 0:TP], ACT.Exp, scale=C0))
                v("ccm")
                done(nc.scalar.activation(b_Pm[:, 0:TP], b_Pm[:, 0:TP], ACT.Exp, scale=-C0))
                done(nc.scalar.activation(b_dx[:, :], b_dm[:, :], ACT.Exp, scale=-C0))
                v("kk0")
                act.wait_ge(b_stored, j * (16 * 6))
                done(nc.scalar.activation(b_b[:, :], b_kkn[:, :], ACT.Square))
                v("ssm")
                done(nc.scalar.activation(b_b[:, :], b_b[:, :], ACT.Ln, scale=2.0 ** 20))
                own("ln")
                done(nc.scalar.activation(b_b[:, :], b_b[:, :], ACT.Exp, scale=-0.5, bias=SHIFT_C))
                for n, bank in (("V", 6), ("A", 0), ("B", 6), ("K", 0)):
                    p(f"t{n}")
                    done(nc.scalar.copy(tm[n][:, :, :].rearrange("p (b c) n -> p b (c n)", b=2), PS[:, bank:bank + 2, :]))
                p("dcol")
                done(nc.scalar.copy(b_D[:, :, :].rearrange("p e c -> p (e c)"), PS[0:DH, 2, 0:2 * NT]))
                v("bv")
                for i, src in enumerate((b_kp, b_kkn, b_b, b_bv)):
                    act.dma_start(rsam[i, bass.ds(j * P, P), :], src[:, TP:T]).then_inc(b_stored, 16)
                for h in range(2):
                    flat = lambda ap: ap.rearrange("p u n -> p (u n)")
                    for l in range(2):
                        p(f"AV_{h}{l}")
                        done(nc.scalar.copy(flat(b_AV[l][:, :, :]), PS[:, 4 * l + 2, 0:4 * DH]))
                    for m in LEVELS[1:5]:
                        for l in range(2):
                            p(f"T{m}_{h}{l}")
                            done(nc.scalar.copy(flat(b_T1[l][:, :, :]), PS[:, 4 * l, 0:P]))
                    for l in range(2):
                        p(f"Z_{h}{l}")
                        done(nc.scalar.copy(flat(b_Z[:, 4 * l:4 * l + 4, :]), PS[:, 4 * l + 3, :]))
                    for l in range(2):
                        p(f"CZ_{h}{l}")
                        done(nc.scalar.copy(flat(b_CZ[:, 4 * l:4 * l + 4, :]), PS[:, 4 * l, :]))
                    for l in range(2):
                        p(f"G_{h}{l}")
                        done(nc.scalar.copy(flat(b_GT[:, 4 * l:4 * l + 4, :]), PS[0:DH, 4 * l + 2, :]))
                    for c in range(4 * h, 4 * h + 4):
                        l = (c % 4) // 2
                        p(f"y{c}")
                        done(nc.scalar.copy(b_y[:, c, :], PS[:, 4 * l + 1 + 2 * (c % 2), 0:P]))
                v("g3")
                done(nc.scalar.activation(b_ysq[:, :, :], b_y[:, :, :], ACT.Square))
                v("g4")
                done(nc.scalar.activation(b_gl[:, :], b_gv[:, :], ACT.Ln, scale=1.0 / DH, bias=GN_C))
                own("gln")
                done(nc.scalar.activation(b_gr[:, :], b_gl[:, :], ACT.Exp, scale=-0.5))
                p("yt")
                done(nc.scalar.copy(b_so[:, :, :].rearrange("p e n -> p (e n)"), PS[0:DH, 2, 0:P]))
                own("so")
                act.dma_start(io["p_rwkv_s"][0, 0, bass.ds(2 * j, 2)].rearrange("e v k -> v e k"), b_so[:, :, :]).then_inc(b_stored, 16)
                v("o3")
                act.dma_start(mix2[bass.ds(j * P, P), 0:TP], b_kp[:, 0:TP]).then_inc(b_stored, 16)
            with act.Fori(0, PAIRS) as j:
                body(j)

        def rwb_vector(dve):
            tt, ts, stt = nc.vector.tensor_tensor, nc.vector.tensor_scalar, nc.vector.scalar_tensor_tensor
            dve.wait_ge(BG_ready, 1)
            for i in range(4):
                VM.chain(dve, nc.vector.tensor_copy(b_ic[32 * i:32 * i + 32, :], ident[32 * i:32 * i + 32, 32 * i:32 * i + 32]), str(i))
            dve.wait_ge(GM.sem, len(GM.names))
            by = lambda ap: ap.rearrange("p (c n) -> p c n", c=NT)
            spread = lambda ap, n: ap.rearrange("p (o n) -> p o n", o=1).broadcast_to([P, n, ap.shape[1]])

            def body(j):
                def done(ins, name):
                    BV.chain(dve, ins, name, j)
                p = lambda n: dve.wait_ge(BP.sem, BP.of(n, j))
                a = lambda n: dve.wait_ge(BA.sem, BA.of(n, j))
                col = lambda i: b_pc[:, i:i + 1]
                r, k, s, aa, vv, gg = (b_in[n] for n in "rksavg")
                pars = vecs[:, VEC["rwkv_k_k"]:VEC["rwkv_k_k"] + 40].rearrange("p (n k) -> p n k", k=KT)
                done(nc.vector.tensor_copy(b_pc[:, 0:5].rearrange("p (n o) -> p n o", o=1), pars[:, :, bass.ds(j, 1)]), "pc")
                dve.wait_ge(rk_in, j * 64 + 64)
                dve.sem_inc(b_turn_dve, 1)
                for c in range(NT):
                    x = slice(P * c, P * c + P)
                    ins = nc.vector.tensor_tensor_scan(b_cs[:, x], ones[:, :], s[:, x], 0.0, ALU.mult, ALU.add)
                done(ins, "cs")
                done(ts(b_mid[:, :].rearrange("p (c o) -> p c o", o=1), by(b_cs[:, 0:TP])[:, :, P - 1:P], 0.5, None, ALU.mult), "mid")
                done(tt(by(b_cs[:, 0:TP]), by(b_cs[:, 0:TP]), b_mid[:, :].rearrange("p (c o) -> p c o", o=1).broadcast_to([P, NT, P]), ALU.subtract), "cc")
                done(tt(b_dm[:, 0:NT - 1], b_mid[:, 0:NT - 1], b_mid[:, 1:NT], ALU.add), "dm")
                done(nc.vector.tensor_copy(b_dm[:, NT - 1:NT], b_mid[:, NT - 1:NT]), "dl")
                done(tt(b_Pm[:, 0:TP], b_cs[:, 0:TP], s[:, 0:TP], ALU.subtract), "ccm")
                dve.wait_ge(b_stored, j * (16 * 6))
                dve.sem_inc(b_turn_dve, 1)
                done(ts(b_kkn[:, :], k[:, :], col(0), None, ALU.mult), "kk0")
                p("ss")
                done(ts(chunks(b_b[:, :]), banks(0), 1e-24, None, ALU.max), "ssm")
                a("rs")
                done(tt(b_kkn[:, :], b_kkn[:, :], b_b[:, :], ALU.mult), "kkn")
                done(tt(b_b[:, :], b_kkn[:, :], aa[:, :], ALU.mult), "b")
                done(ts(b_kp[:, :], aa[:, :], 1.0, col(1), ALU.subtract, ALU.mult), "k1")
                done(stt(b_kp[:, :], b_kp[:, :], 1.0, k[:, :], ALU.add, ALU.mult), "kp")
                done(stt(b_AR[:, :, 0:P], by(b_kkn[:, 0:TP]), -1.0, by(b_Pm[:, 0:TP]), ALU.mult, ALU.mult), "A")
                done(tt(b_B[:, :], b_b[:, 0:TP], b_iP[:, 0:TP], ALU.mult), "B")
                done(tt(b_K[:, :], b_kp[:, 0:TP], b_iP[:, 0:TP], ALU.mult), "K")
                done(tt(b_AR[:, :, P:L2], by(r[:, 0:TP]), by(b_P[:, 0:TP]), ALU.mult), "R")
                done(stt(b_cs[:, :], r[:, :], col(2), b_kp[:, :], ALU.mult, ALU.mult), "rk")
                dve.sem_inc(b_in_free, 1)
                p("bon")
                done(tt(chunks(b_bv[:, :]), banks(1), chunks(vv[:, :]), ALU.mult), "bv")
                for h in range(2):
                    two = lambda l, bank: PS[:, 4 * l + bank:4 * l + bank + 2, :].rearrange("p b (u n) -> p (b u) n", u=2)
                    for dst, bank, name in ((b_ak, 2, "mak"), (b_ab, 0, "mab")):
                        for l in range(2):
                            p(f"s_{h}{l}")
                            done(tt(dst[l][:, :, :], two(l, bank), spread(b_mask[:, :], 4), ALU.mult), f"{name}_{h}{l}")
                    small = lambda l, bank: PS[:, 4 * l + bank, 0:P].rearrange("p (u n) -> p u n", u=4)
                    blocks = lambda ap: ap.rearrange("p u (o n) -> p u o n", o=1).broadcast_to([P, 4, 4, 32])
                    wide = lambda ap: ap.rearrange("p u (q n) -> p u q n", q=4)
                    bmask = lambda m: m[:, :].rearrange("p (o q n) -> p o q n", o=1, q=4).broadcast_to([P, 4, 4, 32])

                    def widen(dst, src, mask, name):
                        done(tt(wide(dst), blocks(src), bmask(mask), ALU.mult), name)
                    for m in LEVELS[0:5]:
                        for l in range(2):
                            if m == 1:
                                p(f"T1_{h}{l}")
                                done(tt(b_X[l][:, :, :], small(l, 0), spread(b_ic[:, :], 4), ALU.add), f"xa1_{h}{l}")
                            else:
                                p(f"X{m}_{h}{l}")
                                done(tt(b_X[l][:, :, :], small(l, 1), b_X[l][:, :, :], ALU.add), f"xa{m}_{h}{l}")
                            done(nc.vector.transpose(b_XTc[l][:, :, :].rearrange("p u n -> p (u n)"), b_X[l][:, :, :].rearrange("p u n -> p (u n)")), f"xt{m}_{h}{l}")
                            widen(b_XT[l][:, :, :], b_XTc[l][:, :, :], b_bd32, f"xb{m}_{h}{l}")
                    for l in range(2):
                        p(f"T32_{h}{l}")
                        widen(b_Z[:, 4 * l:4 * l + 4, :], small(l, 0), b_lev[32], f"t32_{h}{l}")
                    for l in range(2):
                        p(f"X32_{h}{l}")
                        widen(b_Z[:, 4 * l:4 * l + 4, :], small(l, 1), b_lev[32], f"xp_{h}{l}")
                        done(tt(b_XT[l][:, :, :], b_XT[l][:, :, :], b_Z[:, 4 * l:4 * l + 4, :], ALU.add), f"xq_{h}{l}")
                    for l in range(2):
                        p(f"XZ_{h}{l}")
                        done(tt(b_W[:, 4 * l:4 * l + 4, :], b_Z[:, 4 * l:4 * l + 4, :], PS[:, 4 * l + 1, :].rearrange("p (u n) -> p u n", u=4), ALU.add), f"w_{h}{l}")
                    for l in range(2):
                        p(f"M_{h}{l}")
                        done(tt(b_MT[:, 4 * l:4 * l + 4, :], PS[0:DH, 4 * l + 3, 0:4 * DH].rearrange("p (u n) -> p u n", u=4),
                                ident[0:DH, 0:DH].rearrange("p (o n) -> p o n", o=1).broadcast_to([DH, 4, DH]), ALU.add), f"mt_{h}{l}")
                    for c in range(4 * h, 4 * h + 4):
                        l = (c % 4) // 2
                        p(f"c{c}")
                        done(tt(b_T[:, c + 1, :, :], PS[0:DH, 4 * l + 2 * (c % 2), 0:P].rearrange("p (e n) -> p e n", e=2),
                                b_D[:, :, c:c + 1].broadcast_to([DH, 2, DH]), ALU.mult), f"ch{c}")
                groups = lambda ap: ap.rearrange("p c (e n) -> p (c e) n", e=2)
                each = lambda ap: ap.rearrange("p (g o) -> p g o", o=1).broadcast_to([P, 16, DH])
                a("yc7")
                done(nc.vector.tensor_reduce(b_gm[:, :], groups(b_y[:, :, :]), AX.X, ALU.add), "g1")
                done(ts(b_gm[:, :], b_gm[:, :], 1.0 / DH, None, ALU.mult), "g2")
                done(tt(groups(b_y[:, :, :]), groups(b_y[:, :, :]), each(b_gm[:, :]), ALU.subtract), "g3")
                a("gsq")
                done(nc.vector.tensor_reduce(b_gv[:, :], groups(b_ysq[:, :, :]), AX.X, ALU.add), "g4")
                a("grs")
                done(tt(groups(b_y[:, :, :]), groups(b_y[:, :, :]), each(b_gr[:, :]), ALU.mult), "g5")
                p("yt")
                yo = b_kp[:, 0:TP]
                done(ts(yo.rearrange("p (b n) -> p b n", b=2), PS[:, 0:2, :], col(3), col(4), ALU.mult, ALU.add), "o1")
                done(tt(yo, yo, b_bv[:, 0:TP], ALU.add), "o2")
                done(tt(yo, yo, gg[:, 0:TP], ALU.mult), "o3")
            with dve.Fori(0, PAIRS) as j:
                body(j)

        b_turn_dve = sem("b_turn_dve")

        QN = "srvgpkbe"
        HD = RH * NS
        put = packer("h")
        e_S, e_t = put("e_S", [HD, DH, DH]), put("e_t", [HD, DH, DH])
        put = packer("hl")
        e_fm = put("e_fm", [P, 8, KT, NS])
        e_tm = put("e_tm", [NS, 8, D])
        e_rows = {n: put(f"e_{n}", [HD, DH]) for n in QN}
        e_w, e_sa, e_y, e_sq, e_lnw, e_lnb = (put(n, [HD, DH]) for n in ("e_w", "e_sa", "e_y", "e_sq", "e_lnw", "e_lnb"))
        e_mu, e_var, e_ln, e_rs = (put(n, [HD, 1]) for n in ("e_mu", "e_var", "e_ln", "e_rs"))
        e_yT = put("e_yT", [DH, RH, NS])
        e_fm_in, e_S_in, e_par_in, e_rows_in, e_out = (sem(s) for s in ("e_fm_in", "e_S_in", "e_par_in", "e_rows_in", "e_out"))
        QT = Steps(sem("e_pe"), "t0 t1 yt".split())
        QA = Steps(sem("e_act"), "k0 k1 w sq ln rs yk".split())
        QV = Steps(sem("e_dve"), "ta sa sw sb s1 vk s2 tr y mu1 mu2 yc yw yb ye yg".split())

        def rwd_sync(sp):
            sp.wait_ge(b_stored, 16 * 6 * PAIRS)
            sp.wait_ge(BV.sem, PAIRS * len(BV.names))
            tile = lambda ap: ap.rearrange("(k p) t -> p k t", p=P)
            for i, n in enumerate(QN[0:4]):
                sp.dma_start(e_fm[:, i, :, :], tile(rw[RW[n]:RW[n] + D, TP:T])).then_inc(e_fm_in, 16)
            for i in range(4):
                sp.dma_start(e_fm[:, 4 + i, :, :], tile(rsam[i])).then_inc(e_fm_in, 16)
            sp.dma_start(e_S[:, :, :], io["state_rwkv_s"][0].rearrange("b h v k -> (b h) v k")).then_inc(e_S_in, 16)
            for dst, name in ((e_lnw, "rwkv_ln_w"), (e_lnb, "rwkv_ln_b")):
                for b in range(NS):
                    sp.dma_start(dst[RH * b:RH * b + RH, :], io[name].rearrange("o (h d) -> (o h) d", d=DH)).then_inc(e_par_in, 16)
            for r in range(2):
                sp.wait_ge(QA.sem, QA[f"k{r}"])
                for i, n in enumerate(QN[4 * r:4 * r + 4]):
                    sp.dma_start(e_rows[n][:, :], e_tm[:, 4 * r + i, :]).then_inc(e_rows_in, 16)
            sp.wait_ge(QV.sem, QV["s2"])
            sp.dma_start(io["s_rwkv_s"][0].rearrange("b h v k -> (b h) v k"), e_S[:, :, :]).then_inc(e_out, 16)
            sp.wait_ge(QA.sem, QA["yk"])
            sp.dma_start(mix2[:, TP:T].rearrange("(h d) t -> d h t", d=DH), e_yT[:, :, :]).then_inc(e_out, 16)
            sp.wait_ge(e_out, 32)

        def rwd_tensor(pe):
            for r in range(2):
                if r:
                    pe.wait_ge(QA.sem, QA["k0"])
                pe.wait_ge(e_fm_in, 16 * 8)
                for i in range(4 * KT):
                    mm = nc.tensor.transpose(PS[0:NS, i // 4, P * (i % 4):P * (i % 4) + P], e_fm[:, 4 * r + i // KT, i % KT, :], ident[:, :])
                mm.then_inc(QT.sem, 1)
            pe.wait_ge(QV.sem, QV["yg"])
            pe.wait_ge(QA.sem, QA["k1"])
            nc.tensor.transpose(PS[0:DH, 0, 0:HD], e_y[:, :], ident[:, :]).then_inc(QT.sem, 1)

        def rwd_scalar(act):
            for r in range(2):
                act.wait_ge(QT.sem, QT[f"t{r}"])
                QA.chain(act, nc.scalar.copy(e_tm[:, 4 * r:4 * r + 4, :].rearrange("p i n -> p (i n)"), PS[0:NS, :, :].rearrange("p b n -> p (b n)")), f"k{r}")
            act.wait_ge(e_rows_in, 16 * 8)
            QA.chain(act, nc.scalar.activation(e_w[:, :], e_rows["s"][:, :], ACT.Exp, scale=-C0), "w")
            act.wait_ge(QV.sem, QV["yc"])
            QA.chain(act, nc.scalar.activation(e_sq[:, :], e_y[:, :], ACT.Square, accum_out=e_var[:, :]), "sq")
            QA.chain(act, nc.scalar.activation(e_ln[:, :], e_var[:, :], ACT.Ln, scale=1.0 / DH, bias=GN_C), "ln")
            QA.chain(act, nc.scalar.activation(e_rs[:, :], e_ln[:, :], ACT.Exp, scale=-0.5), "rs")
            act.wait_ge(QT.sem, QT["yt"])
            QA.chain(act, nc.scalar.copy(e_yT[:, :, :], PS[0:DH, 0, 0:HD].rearrange("p (b h) -> p h b", b=NS)), "yk")

        def rwd_vector(dve):
            tt, ts, stt = nc.vector.tensor_tensor, nc.vector.tensor_scalar, nc.vector.scalar_tensor_tensor
            c = lambda ins, name: QV.chain(dve, ins, name)
            by_k = lambda ap: ap[:, :].rearrange("p (o k) -> p o k", o=1).broadcast_to([HD, DH, DH])
            by_v = lambda ap: ap[:, :].rearrange("p (v o) -> p v o", o=1).broadcast_to([HD, DH, DH])
            R = e_rows
            S, t = e_S[:, :, :], e_t[:, :, :]
            dve.wait_ge(e_S_in, 16)
            dve.wait_ge(e_rows_in, 16 * 8)
            c(tt(t, S, by_k(R["k"]), ALU.mult), "ta")
            c(nc.vector.tensor_reduce(e_sa[:, :], t, AX.X, ALU.add), "sa")
            dve.wait_ge(QA.sem, QA["w"])
            c(tt(S, S, by_k(e_w), ALU.mult), "sw")
            c(tt(t, by_v(e_sa), by_k(R["b"]), ALU.mult), "sb")
            c(tt(S, S, t, ALU.subtract), "s1")
            c(tt(t, by_v(R["v"]), by_k(R["p"]), ALU.mult), "vk")
            c(tt(S, S, t, ALU.add), "s2")
            c(tt(t, S, by_k(R["r"]), ALU.mult), "tr")
            c(nc.vector.tensor_reduce(e_y[:, :], t, AX.X, ALU.add), "y")
            c(nc.vector.tensor_reduce(e_mu[:, :], e_y[:, :], AX.X, ALU.add), "mu1")
            c(ts(e_mu[:, :], e_mu[:, :], 1.0 / DH, None, ALU.mult), "mu2")
            c(ts(e_y[:, :], e_y[:, :], e_mu[:, :], None, ALU.subtract), "yc")
            dve.wait_ge(QA.sem, QA["sq"])
            dve.wait_ge(e_par_in, 16 * 2 * NS)
            c(tt(e_y[:, :], e_y[:, :], e_lnw[:, :], ALU.mult), "yw")
            dve.wait_ge(QA.sem, QA["rs"])
            c(stt(e_y[:, :], e_y[:, :], e_rs[:, :], e_lnb[:, :], ALU.mult, ALU.add), "yb")
            c(tt(e_y[:, :], e_y[:, :], R["e"][:, :], ALU.add), "ye")
            c(tt(e_y[:, :], e_y[:, :], R["g"][:, :], ALU.mult), "yg")

        y_out = at("h", "y_out", [P, NT, D], 0)
        ys_out = at("s", "ys_out", [NS, D], 0)
        y_full, y_free = [sem("y_full0"), sem("y_full1")], [sem("y_free0"), sem("y_free1")]
        y_stored = sem("y_stored")

        def y_tensor(pe):
            pe.wait_ge(x_ready, 4 * KT)
            for t in range(NT + 1):
                for half in range(2):
                    if t >= 1:
                        pe.wait_ge(y_free[half], t)
                    n = P if t < NT else NS
                    for k in range(4):
                        mm = nc.tensor.transpose(PS[0:n, half, P * k:P * k + P], xT[:, 4 * half + k, P * t:P * t + n], ident[:, :])
                    mm.then_inc(y_full[half], 1)

        def y_copy(eng, half, copy):
            eng.wait_ge(x_ready, 4 * KT)
            for t in range(NT + 1):
                eng.wait_ge(y_full[half], t + 1)
                if t < NT:
                    copy(y_out[:, t, 512 * half:512 * half + 512], PS[:, half, :]).then_inc(y_free[half], 1)
                else:
                    copy(ys_out[:, 512 * half:512 * half + 512], PS[0:NS, half, :]).then_inc(y_free[half], 1)

        def y_sync(sp):
            for t in range(NT + 1):
                for half in range(2):
                    sp.wait_ge(y_free[half], t + 1)
                if t < NT:
                    sp.dma_start(io["y_prompt"][0, P * t:P * t + P, :], y_out[:, t, :]).then_inc(y_stored, 16)
                else:
                    sp.dma_start(io["y_sample"][:, 0, :], ys_out[:, :]).then_inc(y_stored, 16)
            sp.wait_ge(y_stored, 16 * (NT + 1))
            sp.wait_ge(sh_stored, 32)

        block = ctx.enter_context(nc.Block())



        x_sem = lambda eng: [eng.wait_ge(s, NT + (1 if i == 0 else 0)) for i, s in enumerate(xt_free)]

        @block.sync
        def _(sp):
            load_x_sync(sp)
            gates_sync(sp)
            load_pairs(sp, "in_a", 4, w_in)
            load_pairs(sp, "in_o", 2, w_in, c0=1024)
            load_pairs(sp, "in_b", 6, w_in, c0=C_FQ)
            gates_out_sync(sp)
            mlstm_sync(sp)
            fox_sync(sp)
            dec0_sync(sp)
            dec0_end(sp)
            mix_sync(sp, 0, mix)
            load_pairs(sp, "out0", 4, w_out)
            ffn_sync(sp, 0)
            shift_sync(sp)
            mixes_sync(sp)
            rwb_sync(sp)
            rwd_sync(sp)
            mix_sync(sp, 1, mix2)
            load_pairs(sp, "out1", 4, kt_of("rwkv_w_o"))
            ffn_sync(sp, 1)
            y_sync(sp)

        @block.gpsimd
        def _(pool):
            setup_gpsimd(pool)
            gates_gpsimd(pool)
            split_pairs(pool, "in_a", 4, KT)
            split_pairs(pool, "in_o", 2, KT)
            split_pairs(pool, "in_b", 6, KT)
            mlstm_gpsimd(pool)
            fox_gpsimd(pool)
            dec0_gpsimd(pool)
            split_pairs(pool, "out0", 4, KT)
            ffn_gpsimd(pool, 0)
            mixes_gpsimd(pool)
            rwb_gpsimd(pool)
            split_pairs(pool, "out1", 4, KT)
            ffn_gpsimd(pool, 1)

        @block.tensor
        def _(pe):
            load_x_tensor(pe)
            stats_tensor(pe, 0)
            gates_tensor(pe, 0)
            gemm_tensor(pe, "in_a", 4, 0)
            gemm_tensor(pe, "in_o", 2, 0)
            gemm_tensor(pe, "in_b", 6, 0)
            gates_cols_tensor(pe)
            mlstm_tensor(pe)
            fox_tensor(pe)
            dec0_tensor(pe)
            gemm_tensor(pe, "out0", 4, 1)
            stats_tensor(pe, 1)
            stats_tensor(pe, 2)
            ffn_tensor(pe, 0, 2)
            stats_tensor(pe, 3)
            stats_tensor(pe, 4)
            shift_tensor(pe)
            mixes_tensor(pe)
            rwb_tensor(pe)
            rwd_tensor(pe)
            gemm_tensor(pe, "out1", 4, 9)
            stats_tensor(pe, 5)
            stats_tensor(pe, 6)
            ffn_tensor(pe, 1, 10)
            stats_tensor(pe, 7)
            y_tensor(pe)

        @block.scalar
        def _(act):
            load_x_scalar(act)
            stats_scalar(act, 0, xT, x_sem)
            split_scalar(act, 0)
            gates_scalar(act)
            store_scalar(act, "in_a", 4, proj, 0, 0)
            store_scalar(act, "in_o", 2, proj, 1024, 4, func=ACT.Sigmoid)
            store_scalar(act, "in_b", 6, proj, 12 * P, 6)
            gates_exp_scalar(act)
            mlstm_scalar(act)
            fox_scalar(act)
            dec0_scalar(act)
            split_scalar(act, 1)
            keep_scalar(act, "out0")
            stats_scalar(act, 1, oT, after("ffn0"))
            stats_scalar(act, 2, xT, lambda eng: eng.wait_ge(x_ready, KT))
            split_scalar(act, 2)
            ffn_scalar(act, 0)
            stats_scalar(act, 3, oT, after("a_w"))
            stats_scalar(act, 4, xT, lambda eng: eng.wait_ge(x_ready, 2 * KT))
            shift_scalar(act)
            mixes_scalar(act)
            rwb_scalar(act)
            rwd_scalar(act)
            split_scalar(act, 9)
            keep_scalar(act, "out1")
            stats_scalar(act, 5, oT, after("ffn1"))
            stats_scalar(act, 6, xT, lambda eng: eng.wait_ge(x_ready, 3 * KT))
            split_scalar(act, 10)
            ffn_scalar(act, 1)
            stats_scalar(act, 7, oT, after("end"))
            y_copy(act, 0, nc.scalar.copy)

        @block.vector
        def _(dve):
            load_x_vector(dve)
            stats_vector(dve, 0)
            split_vector(dve, 0, normed(dve, 0))
            gates_vector(dve)
            gates_cols_vector(dve)
            mlstm_vector(dve)
            fox_vector(dve)
            dec0_vector(dve)
            mix_split_vector(dve, 1, 0)
            stats_vector(dve, 1)
            add_normed_vector(dve, 1, 0)
            stats_vector(dve, 2)
            split_vector(dve, 2, normed(dve, 2))
            ffn_vector(dve, 0, 2)
            stats_vector(dve, 3)
            add_normed_vector(dve, 3, 1)
            stats_vector(dve, 4)
            shift_vector(dve)
            mixes_vector(dve)
            rwb_vector(dve)
            rwd_vector(dve)
            mix_split_vector(dve, 9, 1)
            stats_vector(dve, 5)
            add_normed_vector(dve, 5, 2)
            stats_vector(dve, 6)
            split_vector(dve, 10, normed(dve, 6))
            ffn_vector(dve, 1, 10)
            stats_vector(dve, 7)
            add_normed_vector(dve, 7, 3)
            y_copy(dve, 1, nc.vector.tensor_copy)


_INS = ['x_prompt', 'x_sample', 'cache_fox_k', 'cache_fox_v', 'cache_fox_lf', 'state_mlstm_c', 'state_mlstm_n',
    'state_mlstm_m', 'state_rwkv_s', 'state_rwkv_shift', 'page_table', 'norm_g', 'hyb_w_in', 'mlstm_i_bias',
    'mlstm_f_bias', 'mlstm_out_g', 'fox_f_bias', 'hyb_w_out', 'rwkv_mix', 'rwkv_w_r', 'rwkv_w_k', 'rwkv_w_v',
    'rwkv_w_o', 'rwkv_w0', 'rwkv_w1', 'rwkv_w2', 'rwkv_a0', 'rwkv_a1', 'rwkv_a2', 'rwkv_g1', 'rwkv_g2',
    'rwkv_k_k', 'rwkv_k_a', 'rwkv_r_k', 'rwkv_ln_w', 'rwkv_ln_b', 'ffn_w_gate', 'ffn_w_up', 'ffn_w_down']
_OUTS = [('y_prompt', (1, 1024, 1024)), ('y_sample', (8, 1, 1024)), ('p_fox_k', (1, 1, 1024, 8, 64)),
    ('p_fox_v', (1, 1, 1024, 8, 64)), ('p_fox_lf', (1, 1, 1024, 8)), ('p_mlstm_c', (1, 1, 4, 64, 128)),
    ('p_mlstm_n', (1, 1, 4, 64)), ('p_mlstm_m', (1, 1, 4)), ('p_rwkv_s', (1, 1, 16, 64, 64)),
    ('p_rwkv_shift', (1, 1, 1024)), ('s_fox_k', (1, 8, 1, 8, 64)), ('s_fox_v', (1, 8, 1, 8, 64)),
    ('s_fox_lf', (1, 8, 1, 8)), ('s_mlstm_c', (1, 8, 4, 64, 128)), ('s_mlstm_n', (1, 8, 4, 64)),
    ('s_mlstm_m', (1, 8, 4)), ('s_rwkv_s', (1, 8, 16, 64, 64)), ('s_rwkv_shift', (1, 8, 1024))]


def kernel(**inputs):
    import numpy as _np
    import concourse.bacc as _bacc
    from concourse import mybir as _mybir
    from concourse.bass_utils import run_bass_kernel_spmd as _run

    nc = _bacc.Bacc("TRN2", target_bir_lowering=False, num_devices=1)
    arrays, io = {}, {}
    for name in _INS:
        a = _np.ascontiguousarray(inputs[name])
        arrays[f"in_{name}_dram"] = a
        io[name] = nc.dram_tensor(f"in_{name}_dram", a.shape, _mybir.dt.from_np(a.dtype), kind="ExternalInput").ap()
    for i, (name, shape) in enumerate(_OUTS):
        io[name] = nc.dram_tensor(f"out_{i}_dram", shape, _mybir.dt.float32, kind="ExternalOutput").ap()
    decoder_step(nc, io)
    r = _run(nc, [arrays], core_ids=[0])
    return tuple(r.results[0][f"out_{i}_dram"] for i in range(len(_OUTS)))
```

```python
import math
from contextlib import ExitStack

import numpy as np

import concourse.bass as bass
from concourse import mybir

F32 = mybir.dt.float32
F32R = mybir.dt.float32r
I32 = mybir.dt.int32
ALU = mybir.AluOpType
ACT = mybir.ActivationFunctionType
AX = mybir.AxisListType

P = 128
D = 1024
TP = 1024
NS = 8
T = TP + NS
KT = D // P
NCH = 3
CH = T // NCH
NT = TP // P
EPS = 1e-6
GN_EPS = 64e-5
HID = 2816
HT = HID // P
HG = 4
HGROUPS = HT // HG
HREST = HT - HG * HGROUPS
MH, DK, DV = 4, 64, 128
FH, DH = 8, 64
RH = 16
NPAGES, PAGE = 2, 128
BIG = 1.0e30
START = 1
LN2 = math.log(2.0)


class Steps:

    def __init__(self, sem, names):
        self.sem, self.names = sem, list(names)

    def __getitem__(self, name):
        return self.names.index(name) + 1

    def of(self, name, n):
        return n * len(self.names) + self[name]

    def chain(self, eng, ins, name, n=None):
        ins.then_inc(self.sem, 1)
        eng.wait_ge(self.sem, (self[name] if n is None else self.of(name, n)) + START)


def decoder_step(nc, io):
    with ExitStack() as ctx:
        cursor = [(nc.sbuf_base + 31) // 32 * 32]

        def take(n_bytes):
            a = cursor[0]
            cursor[0] += (n_bytes + 31) // 32 * 32
            assert cursor[0] <= nc.sbuf_usable_end, ("SBUF is full", cursor[0])
            return a

        def sb(name, shape, dt=F32):
            return nc.alloc_sbuf_tensor_at(name, shape, dt, offset=take(4 * int(np.prod(shape[1:]))))

        sems = []

        def sem(name):
            sems.append(ctx.enter_context(nc.semaphore(name)))
            return sems[-1]

        def start(eng, part):
            for s in sems[part::5]:
                eng.sem_inc(s, START)

        def dram(name, shape):
            return nc.dram_tensor(name, shape, F32, kind="Internal").ap()

        ident = sb("ident", [P, P])
        ones = sb("ones", [P, P])
        xT = sb("xT", [P, KT, T])
        slots = {"w_raw": take(2 * KT * P * 4)}
        w_raw = nc.alloc_sbuf_tensor_at("w_raw", [P, 2, KT, P], F32, offset=slots["w_raw"])
        slots["w_hi"] = take(2 * KT * P * 4)
        slots["w_lo"] = take(2 * KT * P * 4)
        w_hi, w_lo = (nc.alloc_sbuf_tensor_at(n, [P, 2, KT, P], F32R, offset=slots[n]) for n in ("w_hi", "w_lo"))
        vecs = sb("vecs", [P, 172])
        cst = sb("cst", [P, 4])
        EPS_C, ONE_C, SHIFT_C, GN_C = (cst[:, i:i + 1] for i in range(4))

        SIZE = {"hl": 2 * KT * T * 4, "o": KT * T * 4, "h": KT * T * 4, "s": 5 * T * 4}
        base = {r: take(n) for r, n in SIZE.items()}
        small = [take(544), 544]

        def at(region, name, shape, offset, dt=F32):
            n = 4 * int(np.prod(shape[1:]))
            assert offset % 32 == 0 and offset + n <= SIZE[region], (name, offset, n, SIZE[region])
            return nc.alloc_sbuf_tensor_at(name, shape, dt, offset=base[region] + offset)

        def tiny(name, shape, dt=F32):
            n = (4 * int(np.prod(shape[1:])) + 31) // 32 * 32
            assert n <= small[1], name
            small[0] += n
            small[1] -= n
            return nc.alloc_sbuf_tensor_at(name, shape, dt, offset=small[0] - n)

        VEC, column = {}, 0
        for name, n in (("norm_g", 64), ("rwkv_mix", 48), ("rwkv_w0", 8), ("rwkv_a0", 8), ("rwkv_k_k", 8),
                        ("rwkv_k_a", 8), ("rwkv_r_k", 8), ("rwkv_ln_w", 8), ("rwkv_ln_b", 8), ("mlstm_out_g", 4)):
            VEC[name] = column
            column += n
        gains = vecs[:, 0:64].rearrange("p (n k) -> p n k", k=KT)

        def vec(name, k):
            return vecs[:, VEC[name] + k:VEC[name] + k + 1]

        ROW = T * 4
        act_hi = at("hl", "act_hi", [P, KT, T], 0, F32R)
        act_lo = at("hl", "act_lo", [P, KT, T], KT * ROW, F32R)
        oT = at("o", "oT", [P, KT, T], 0)
        hid_hi = at("h", "hid_hi", [P, HG, T], 0, F32R)
        hid_lo = at("h", "hid_lo", [P, HG, T], HG * ROW, F32R)
        sq = at("s", "sq", [P, 2, T], 0)
        hf = at("s", "hf", [P, 2, T], 0)
        acc = at("s", "acc", [P, T], 2 * ROW)
        sg = at("s", "sg", [P, T], 2 * ROW)
        rstd = at("s", "rstd", [P, T], 3 * ROW)
        lnv = at("s", "lnv", [P, T], 4 * ROW)
        stage = at("s", "stage", [P, 2, T], 3 * ROW)
        PS = ctx.enter_context(nc.psum_tensor("PS", [P, 8, 512], F32))

        def chunks(ap):
            return ap.rearrange("p (c n) -> p c n", c=NCH)

        def banks(u):
            return PS[:, 3 * u:3 * u + 3, 0:CH]

        proj = dram("proj", [24 * P, T])

        w_loaded = [sem("w_loaded0"), sem("w_loaded1")]
        w_hi_done = sem("w_hi_done")
        w_turn = sem("w_turn")
        w_split = [sem("w_split0"), sem("w_split1")]
        psum_full = [sem("psum_full0"), sem("psum_full1")]
        psum_free = [sem("psum_free0"), sem("psum_free1")]
        act_ready = sem("act_ready")
        hf_ready, hi_ready = sem("hf_ready"), sem("hi_ready")
        sq_ready, sq_used, ss_ready, ln_ready, rstd_ready = (
            sem(s) for s in ("sq_ready", "sq_used", "ss_ready", "ln_ready", "rstd_ready"))
        x_ready = sem("x_ready")
        o_ready = sem("o_ready")
        stored = [sem("stored0"), sem("stored1")]
        setup_done, gain_in = sem("setup_done"), sem("gain_in")
        hid_hi_ready, hid_ready = sem("hid_hi_ready"), sem("hid_ready")
        sg_ready = sem("sg_ready")
        o_zero = sem("o_zero")
        const_in = sem("const_in")

        used = [0, 0]
        plan = {}

        def step(name, n0, n1):
            plan[name] = tuple(used)
            used[0] += n0
            used[1] += n1

        step("gates", 1, 0)
        step("in_a", 4, 4)
        step("in_o", 2, 2)
        step("in_b", 6, 6)
        step("out0", 4, 4)
        step("ffn0", 8 * HGROUPS + HREST + 4, 8 * HGROUPS + HREST + 4)

        for m in "wag":
            step(f"a_{m}", 1, 0)
        for m in "rkv":
            step(f"a_{m}", 4, 4)
        step("out1", 4, 4)
        step("ffn1", 8 * HGROUPS + HREST + 4, 8 * HGROUPS + HREST + 4)
        step("end", 0, 0)

        w_in = io["hyb_w_in"][0].rearrange("(k p) n -> p k n", p=P)
        w_out = io["hyb_w_out"][0].rearrange("(k p) n -> p k n", p=P)
        C_MI, C_MF, C_FQ, C_FF = 1536, 1540, 1544, 3080

        def setup_gpsimd(pool):
            pool.memset(w_raw[:, :, :, :], 0.0).then_inc(setup_done, 1)
            pool.memset(ident[:, :], 0.0).then_inc(setup_done, 1)
            pool.memset(ones[:, :], 1.0).then_inc(setup_done, 1)
            for col, value in ((EPS_C, EPS), (ONE_C, 1.0), (SHIFT_C, 10 * LN2), (GN_C, GN_EPS)):
                pool.memset(col, value).then_inc(setup_done, 1)
            pool.wait_ge(setup_done, 7 + START)
            pool.affine_select(out=ident[:, :], in_=ident[:, :], compare_op=ALU.not_equal, fill=1.0,
                               base=0, pattern=[[-1, P]], channel_multiplier=1).then_inc(setup_done, 1)

        x_in = at("o", "x_in", [P, NT, D], 0)
        xs_in = at("s", "xs_in", [NS, D], 0)
        vec_in = at("s", "vec_in", [P, 2, P], ROW)
        vec_loaded, vec_full = sem("vec_loaded"), sem("vec_full")
        x_loaded = [sem("x_loaded0"), sem("x_loaded1")]
        xt_full, xt_free = [sem("xt_full0"), sem("xt_full1")], [sem("xt_free0"), sem("xt_free1")]

        def load_x_sync(sp):
            xp = io["x_prompt"][0].rearrange("(t p) d -> p t d", p=P)
            for half in range(2):
                sp.dma_start(x_in[:, 4 * half:4 * half + 4, :], xp[:, 4 * half:4 * half + 4, :]).then_inc(x_loaded[half], 16)
            sp.dma_start(xs_in[:, :], io["x_sample"][:, 0, :]).then_inc(x_loaded[1], 16)
            for name, shape in (("norm_g", "l i (k p) -> (l i k) p"), ("rwkv_mix", "o i (k p) -> (o i k) p"),
                                ("rwkv_w0", ""), ("rwkv_a0", ""), ("rwkv_k_k", ""), ("rwkv_k_a", ""),
                                ("rwkv_r_k", "o (k h) d -> (o k) (h d)"), ("rwkv_ln_w", ""), ("rwkv_ln_b", ""),
                                ("mlstm_out_g", "")):
                src = io[name].rearrange(shape or "o (k p) -> (o k) p", **({"h": 2} if "h d" in shape else {"p": P}))
                c, n = VEC[name], src.shape[0]
                sp.dma_start(vec_in[c % P:c % P + n, c // P, :], src).then_inc(vec_loaded, 16)

        def load_x_tensor(pe):
            pe.wait_ge(setup_done, 8 + START)
            pe.wait_ge(vec_loaded, 160 + START)
            nc.tensor.transpose(PS[:, 2, 0:P], vec_in[:, 0, :], ident[:, :])
            nc.tensor.transpose(PS[:, 2, P:172], vec_in[0:44, 1, :], ident[0:44, 0:44]).then_inc(vec_full, 1)
            for t in range(NT):
                pe.wait_ge(x_loaded[t // 4], (16 if t < 4 else 32) + START)
                for half in range(2):
                    if t >= 1:
                        pe.wait_ge(xt_free[half], t + START)
                    for k in range(4):
                        mm = nc.tensor.transpose(PS[:, half, P * k:P * k + P],
                                                 x_in[:, t, P * (4 * half + k):P * (4 * half + k) + P], ident[:, :])
                    mm.then_inc(xt_full[half], 1)
            pe.wait_ge(xt_free[0], NT + START)
            for k in range(KT):
                mm = nc.tensor.transpose(PS[:, 0, NS * k:NS * k + NS], xs_in[:, P * k:P * k + P], ident[0:NS, 0:NS])
            mm.then_inc(xt_full[0], 1)

        def x_copy(eng_copy, half, t):
            src = PS[:, half, :].rearrange("p (k n) -> p k n", k=4)
            return eng_copy(xT[:, 4 * half:4 * half + 4, P * t:P * t + P], src)

        def load_x_scalar(act):
            for t in range(NT):
                act.wait_ge(xt_full[0], t + 1 + START)
                x_copy(nc.scalar.copy, 0, t).then_inc(xt_free[0], 1)
            act.wait_ge(xt_full[0], NT + 1 + START)
            nc.scalar.copy(xT[:, :, TP:T], PS[:, 0, 0:KT * NS].rearrange("p (k n) -> p k n", k=KT)).then_inc(xt_free[0], 1)

        def load_x_vector(dve):
            dve.wait_ge(vec_full, 1 + START)
            nc.vector.tensor_copy(vecs[:, :], PS[:, 2, 0:172]).then_inc(gain_in, 1)
            for t in range(NT):
                dve.wait_ge(xt_full[1], t + 1 + START)
                x_copy(nc.vector.tensor_copy, 1, t).then_inc(xt_free[1], 1)

        def stats_scalar(act, n, src, wait_source):
            wait_source(act)
            for k in range(KT):
                g = KT * n + k
                if g >= 2:
                    act.wait_ge(sq_used, g - 1 + START)
                nc.scalar.activation(sq[:, k % 2, :], src[:, k, :], ACT.Square).then_inc(sq_ready, 1)
            if n == 0:
                act.wait_ge(gain_in, 1 + START)
            act.wait_ge(ss_ready, n + 1 + START)
            nc.scalar.activation(chunks(lnv[:, :]), banks(0), ACT.Ln, bias=EPS_C, scale=1.0 / D).then_inc(ln_ready, 1)
            act.wait_ge(ln_ready, n + 1 + START)
            nc.scalar.activation(rstd[:, :], lnv[:, :], ACT.Exp, scale=-0.5).then_inc(rstd_ready, 1)

        def stats_vector(dve, n):
            for k in range(KT):
                g = KT * n + k
                dve.wait_ge(sq_ready, g + 1 + START)
                if k == 0:
                    nc.vector.tensor_copy(acc[:, :], sq[:, k % 2, :]).then_inc(sq_used, 1)
                else:
                    dve.wait_ge(sq_used, g + START)
                    nc.vector.tensor_tensor(acc[:, :], acc[:, :], sq[:, k % 2, :], ALU.add).then_inc(sq_used, 1)

        def stats_tensor(pe, n):
            pe.wait_ge(sq_used, KT * (n + 1) + START)
            for c in range(NCH):
                mm = nc.tensor.matmul(PS[:, c, 0:CH], ones[:, :], acc[:, CH * c:CH * c + CH], start=True, stop=True)
            mm.then_inc(ss_ready, 1)

        def split_vector(dve, r, make):
            for k in range(KT + 1):
                if k < KT:
                    if k >= 2:
                        dve.wait_ge(act_ready, KT * r + k - 1 + START)
                    make(k).then_inc(hf_ready, 1)
                if k >= 1:
                    dve.wait_ge(hf_ready, KT * r + k + START)
                    dve.wait_ge(hi_ready, KT * r + k + START)
                    nc.vector.tensor_tensor(act_lo[:, k - 1, :], hf[:, (k - 1) % 2, :],
                                            act_hi[:, k - 1, :].bitcast(F32), ALU.subtract).then_inc(act_ready, 1)

        def split_scalar(act, r):
            for k in range(KT):
                act.wait_ge(hf_ready, KT * r + k + 1 + START)
                nc.scalar.copy(act_hi[:, k, :], hf[:, k % 2, :]).then_inc(hi_ready, 1)

        def normed(dve, n):
            dve.wait_ge(rstd_ready, n + 1 + START)
            dve.wait_ge(gain_in, 1 + START)
            return lambda k: nc.vector.scalar_tensor_tensor(hf[:, k % 2, :], xT[:, k, :], gains[:, n, k:k + 1],
                                                            rstd[:, :], ALU.mult, ALU.mult)

        add_t = sem("add_t")

        def add_normed_vector(dve, n, m):
            dve.wait_ge(rstd_ready, n + 1 + START)
            for k in range(KT + 1):
                if k < KT:
                    if k >= 2:
                        dve.wait_ge(x_ready, KT * m + k - 1 + START)
                    nc.vector.scalar_tensor_tensor(hf[:, k % 2, :], oT[:, k, :], gains[:, n, k:k + 1], rstd[:, :],
                                                   ALU.mult, ALU.mult).then_inc(add_t, 1)
                if k >= 1:
                    dve.wait_ge(add_t, KT * m + k + START)
                    nc.vector.tensor_tensor(xT[:, k - 1, :], xT[:, k - 1, :], hf[:, (k - 1) % 2, :],
                                            ALU.add).then_inc(x_ready, 1)

        def load_w(sp, u, k, src, dst=None):
            sp.wait_ge(w_split[u], k + START)
            sp.dma_start(w_raw[:, u, 0:src.shape[1], :] if dst is None else dst, src).then_inc(w_loaded[u], 16)

        def split_w(pool, u, k, kts, hi_count):
            pool.wait_ge(w_loaded[u], 16 * (k + 1) + START)
            pool.wait_ge(psum_full[u], k + START)
            pool.sem_inc(w_turn, 1)
            nc.gpsimd.tensor_copy(w_hi[:, u, 0:kts, :], w_raw[:, u, 0:kts, :]).then_inc(w_hi_done, 1)
            pool.wait_ge(w_hi_done, hi_count + START)
            nc.gpsimd.tensor_tensor(w_lo[:, u, 0:kts, :], w_raw[:, u, 0:kts, :],
                                    w_hi[:, u, 0:kts, :].bitcast(F32), ALU.subtract).then_inc(w_split[u], 1)

        def split_pairs(pool, name, pairs, kts, k_off=0):
            k0, k1 = plan[name][0] + k_off, plan[name][1] + k_off
            with pool.Fori(0, pairs) as i:
                split_w(pool, 0, k0 + i, kts, k0 + k1 + 2 * i + 1)
                split_w(pool, 1, k1 + i, kts, k0 + k1 + 2 * i + 2)

        def tile_products(pe, u, k, hi, lo, kts, ready, ready_base):
            pe.wait_ge(w_split[u], k + 1 + START)
            pe.wait_ge(psum_free[u], k + START)
            for kt in range(kts):
                pe.wait_ge(ready, ready_base + kt + 1 + START)
                for part, (w, x) in enumerate(((w_hi, hi), (w_hi, lo), (w_lo, hi))):
                    for c in range(NCH):
                        mm = nc.tensor.matmul(PS[:, 3 * u + c, 0:CH], w[:, u, kt, :], x[:, kt, CH * c:CH * c + CH],
                                              start=(kt == 0 and part == 0), stop=(kt == kts - 1 and part == 2))
            mm.then_inc(psum_full[u], 1)

        def gemm_tensor(pe, name, pairs, r, k_off=0):
            k0, k1 = plan[name][0] + k_off, plan[name][1] + k_off
            with pe.Fori(0, pairs) as i:
                tile_products(pe, 0, k0 + i, act_hi, act_lo, KT, act_ready, KT * r)
                tile_products(pe, 1, k1 + i, act_hi, act_lo, KT, act_ready, KT * r)

        def load_pairs(sp, name, pairs, w, c0=0, k_off=0):
            k0, k1 = plan[name][0] + k_off, plan[name][1] + k_off
            with sp.Fori(0, pairs) as i:
                load_w(sp, 0, k0 + i, w[:, :, bass.ds(i * (2 * P) + c0, P)])
                load_w(sp, 1, k1 + i, w[:, :, bass.ds(i * (2 * P) + (c0 + P), P)])

        def store_scalar(act, name, pairs, dst, row0, s0, func=ACT.Copy, k_off=0):
            k0, k1 = plan[name][0] + k_off, plan[name][1] + k_off
            with act.Fori(0, pairs) as i:
                for u, k in ((0, k0), (1, k1)):
                    act.wait_ge(psum_full[u], k + i + 1 + START)
                    act.wait_ge(stored[u], (i + s0) * 16 + START)
                    nc.scalar.activation(chunks(stage[:, u, :]), banks(u), func).then_inc(psum_free[u], 1)
                    act.wait_ge(psum_free[u], k + i + 1 + START)
                    act.dma_start(dst[bass.ds(i * (2 * P) + (row0 + P * u), P), :], stage[:, u, :]).then_inc(stored[u], 16)

        def keep_scalar(act, name):
            k0, k1 = plan[name]
            with act.Fori(0, KT // 2) as i:
                for u, k in ((0, k0), (1, k1)):
                    act.wait_ge(psum_full[u], k + i + 1 + START)
                    nc.scalar.copy(oT[:, bass.ds(2 * i + u, 1), :].rearrange("p o (c n) -> p (o c) n", c=NCH), banks(u)).then_inc(psum_free[u], 1)

        def ffn_weights(l):
            wg, wu = (io[n][l].rearrange("(k p) n -> p k n", p=P) for n in ("ffn_w_gate", "ffn_w_up"))
            return wg, wu, io["ffn_w_down"][l].rearrange("(k p) n -> p k n", p=P)

        def ffn_groups(eng, body):
            with eng.Fori(0, HGROUPS) as g:
                body(g, HG)
            body(HGROUPS, HREST)

        def ffn_sync(sp, l):
            name = f"ffn{l}"
            k0, k1 = plan[name]
            wg, wu, wd = ffn_weights(l)

            def body(g, n):
                with sp.Fori(0, n) as i:
                    load_w(sp, 0, g * 8 + (i + k0), wg[:, :, bass.ds(g * (HG * P) + i * P, P)])
                    load_w(sp, 1, g * 8 + (i + k1), wu[:, :, bass.ds(g * (HG * P) + i * P, P)])
                with sp.Fori(0, KT // 2) as i:
                    for u, k in ((0, k0), (1, k1)):
                        load_w(sp, u, g * 8 + (i + (k + n)), wd[:, bass.ds(g * HG, n), bass.ds(i * (2 * P) + P * u, P)])
            ffn_groups(sp, body)

        def ffn_gpsimd(pool, l):
            k0, k1 = plan[f"ffn{l}"]

            def body(g, n):
                for count, kts, off in ((n, KT, 0), (KT // 2, n, n)):
                    with pool.Fori(0, count) as i:
                        for u, k in ((0, k0), (1, k1)):
                            split_w(pool, u, g * 8 + (i + (k + off)), kts, g * 16 + (2 * i + (k0 + k1 + 2 * off + u + 1)))
            ffn_groups(pool, body)

        def ffn_tensor(pe, l, r):
            k0, k1 = plan[f"ffn{l}"]

            def body(g, n):
                with pe.Fori(0, n) as i:
                    for u, k in ((0, k0), (1, k1)):
                        tile_products(pe, u, g * 8 + (i + k), act_hi, act_lo, KT, act_ready, KT * r)
                with pe.Fori(0, KT // 2) as i:
                    for u, k in ((0, k0), (1, k1)):
                        tile_products(pe, u, g * 8 + (i + (k + n)), hid_hi, hid_lo, n, hid_ready, g * HG + l * HT)
            ffn_groups(pe, body)

        def ffn_scalar(act, l):
            k0, k1 = plan[f"ffn{l}"]
            h0 = l * HT

            def body(g, n):
                with act.Fori(0, n) as i:
                    act.wait_ge(psum_full[0], g * 8 + (i + (k0 + 1)) + START)
                    act.wait_ge(hid_ready, g * HG + (i + h0) + START)
                    nc.scalar.activation(chunks(sg[:, :]), banks(0), ACT.Silu).then_inc(psum_free[0], 1)
                    act.wait_ge(psum_free[1], g * 8 + (i + (k1 + 1)) + START)
                    nc.scalar.copy(hid_hi[:, bass.ds(i, 1), :], hf[:, 0:1, :]).then_inc(hid_hi_ready, 1)
            ffn_groups(act, body)

        def ffn_vector(dve, l, m):
            k0, k1 = plan[f"ffn{l}"]
            h0 = l * HT
            dve.wait_ge(act_ready, KT * (m + 1) + START)
            nc.vector.memset(oT[:, :, :], 0.0).then_inc(o_zero, 1)
            dve.wait_ge(o_zero, l + 1 + START)

            def body(g, n):
                with dve.Fori(0, n) as i:
                    dve.wait_ge(psum_free[0], g * 8 + (i + (k0 + 1)) + START)
                    dve.wait_ge(psum_full[1], g * 8 + (i + (k1 + 1)) + START)
                    nc.vector.tensor_tensor(chunks(hf[:, 0, :]), banks(1), chunks(sg[:, :]), ALU.mult).then_inc(psum_free[1], 1)
                    dve.wait_ge(hid_hi_ready, g * HG + (i + (h0 + 1)) + START)
                    nc.vector.tensor_tensor(hid_lo[:, bass.ds(i, 1), :], hf[:, 0:1, :],
                                            hid_hi[:, bass.ds(i, 1), :].bitcast(F32), ALU.subtract).then_inc(hid_ready, 1)
                with dve.Fori(0, KT // 2) as i:
                    for u, k in ((0, k0), (1, k1)):
                        dve.wait_ge(psum_full[u], g * 8 + (i + (k + n + 1)) + START)
                        tile = oT[:, bass.ds(2 * i + u, 1), :].rearrange("p o (c n) -> p (o c) n", c=NCH)
                        nc.vector.tensor_tensor(tile, banks(u), tile, ALU.add).then_inc(psum_free[u], 1)
            ffn_groups(dve, body)

        mix = dram("mix", [D, T])
        mrow = dram("mrow", [2, MH, TP])
        frow = dram("frow", [FH, TP])
        lfs = dram("lfs", [2, MH, NS])
        g_ig, g_lf, g_ff, g_t0, g_t1, g_b, g_M, g_wi = (
            at("h", n, [FH, T], i * ROW) for i, n in enumerate(("g_ig", "g_lf", "g_ff", "g_t0", "g_t1", "g_b", "g_M", "g_wi")))
        pack = at("o", "pack", [96, TP], 0)
        cols = at("o", "cols", [P, NT, 96], 4096)
        fresh = at("o", "fresh", [FH, TP], 7168)
        mask_st = at("o", "mask_st", [P, P], 11264)
        mask_ts = at("o", "mask_ts", [P, P], 11776)
        bias_i, bias_f, bias_x = tiny("bias_i", [MH, 1]), tiny("bias_f", [MH, 1]), tiny("bias_x", [FH, 1])
        m_in = tiny("m_in", [MH, NT + 1])
        lf_tok = at("o", "lf_tok", [P, NT, FH], 12288)
        lf_sam = at("o", "lf_sam", [NS, FH], 12544)
        gate_w_in, bias_in = sem("gate_w_in"), sem("bias_in")
        gp = sem("gp")
        GA = Steps(sem("ga"), "ig mf fx fabs fexp fln xx xabs xexp xln wi wk em".split())
        GV = Steps(sem("gv"), "fresh minit lf lff F starts b g".split()
                   + [f"{x}{c}" for c in range(NT) for x in ("M", "m")] + "wi wk bM".split())
        rows_out, cols_full, cols_done = sem("rows_out"), sem("cols_full"), sem("cols_done")

        def gates_sync(sp):
            sp.wait_ge(setup_done, 8 + START)
            sp.dma_start(w_raw[:, 0, :, 0:4], w_in[:, :, C_MI:C_MI + 4], allow_slow_non_contiguous=True).then_inc(gate_w_in, 16)
            sp.dma_start(w_raw[:, 0, :, 32:36], w_in[:, :, C_MF:C_MF + 4], allow_slow_non_contiguous=True).then_inc(gate_w_in, 16)
            sp.dma_start(w_raw[:, 0, :, 64:72], w_in[:, :, C_FF:C_FF + 8], allow_slow_non_contiguous=True).then_inc(w_loaded[0], 16)
            for dst, name in ((bias_i, "mlstm_i_bias"), (bias_f, "mlstm_f_bias"), (bias_x, "fox_f_bias")):
                sp.dma_start(dst[:, :], io[name].rearrange("o h -> h o")).then_inc(bias_in, 16)

        def gates_out_sync(sp):
            sp.wait_ge(GA.sem, GA["em"] + START)
            sp.wait_ge(GV.sem, GV["bM"] + START)
            sp.dma_start(mrow[0], g_M[0:MH, 0:TP]).then_inc(rows_out, 16)
            sp.dma_start(mrow[1], g_wi[0:MH, 0:TP]).then_inc(rows_out, 16)
            sp.dma_start(frow, g_t1[:, 0:TP]).then_inc(rows_out, 16)
            sp.dma_start(lfs[0], g_ig[0:MH, TP:T]).then_inc(rows_out, 16)
            sp.dma_start(lfs[1], g_lf[0:MH, TP:T]).then_inc(rows_out, 16)
            sp.dma_start(io["p_mlstm_m"].rearrange("o b h -> (o h) b"), m_in[:, NT:NT + 1]).then_inc(rows_out, 16)
            sp.wait_ge(cols_done, 3 + START)
            sp.dma_start(io["p_fox_lf"][0, 0].rearrange("(c p) h -> p c h", p=P), lf_tok[:, :, :]).then_inc(rows_out, 16)
            sp.dma_start(io["s_fox_lf"][0, :, 0, :], lf_sam[:, :]).then_inc(rows_out, 16)

        def gates_gpsimd(pool):
            pool.wait_ge(gate_w_in, 32 + START)
            split_w(pool, 0, 0, KT, 1)
            pool.wait_ge(xt_full[0], NT + 1 + START)
            pool.memset(pack[:, :], 0.0).then_inc(gp, 1)
            pool.memset(mask_st[:, :], 0.0).then_inc(gp, 1)
            pool.memset(mask_ts[:, :], 0.0).then_inc(gp, 1)
            pool.wait_ge(gp, 3 + START)
            pool.affine_select(out=mask_st[:, :], in_=mask_st[:, :], compare_op=ALU.is_ge, fill=BIG,
                               base=0, pattern=[[1, P]], channel_multiplier=-1).then_inc(gp, 1)
            pool.affine_select(out=mask_ts[:, :], in_=mask_ts[:, :], compare_op=ALU.is_ge, fill=-BIG,
                               base=0, pattern=[[-1, P]], channel_multiplier=1).then_inc(gp, 1)

        def gates_tensor(pe, r):
            tile_products(pe, 0, 0, act_hi, act_lo, KT, act_ready, KT * r)

        def gates_cols_tensor(pe):
            pe.wait_ge(GA.sem, GA["em"] + START)
            pe.wait_ge(GV.sem, GV["bM"] + START)
            pe.wait_ge(psum_free[0], plan["out0"][0] + START)
            pe.wait_ge(psum_free[1], plan["out0"][1] + START)
            for c in range(NT):
                nc.tensor.transpose(PS[:, c // 4, P * (c % 4):P * (c % 4) + 96], pack[:, P * c:P * c + P], ident[0:96, 0:96])
            for c in range(NT):
                nc.tensor.transpose(PS[:, 2, FH * c:FH * c + FH], g_ff[:, P * c:P * c + P], ident[0:FH, 0:FH])
            nc.tensor.transpose(PS[0:NS, 2, P:P + FH], g_ff[:, TP:T], ident[0:FH, 0:FH]).then_inc(cols_full, 1)

        def gates_scalar(act):
            row = lambda ap: ap.rearrange("p (c n) -> p c n", c=NCH)
            act.wait_ge(bias_in, 48 + START)
            act.wait_ge(psum_full[0], 1 + START)
            GA.chain(act, nc.scalar.activation(row(g_ig[0:MH, :]), PS[0:MH, 0:3, 0:CH], ACT.Identity, bias=bias_i[:, :]), "ig")
            GA.chain(act, nc.scalar.copy(row(g_t0[0:MH, :]), PS[32:32 + MH, 0:3, 0:CH]), "mf")
            nc.scalar.copy(row(g_ff[:, :]), PS[64:64 + FH, 0:3, 0:CH]).then_inc(psum_free[0], 1)
            act.wait_ge(psum_free[0], 1 + START)
            for s, x, dst, n, bias in (("f", g_t0, g_t1, MH, bias_f), ("x", g_ff, g_M, FH, bias_x)):
                GA.chain(act, nc.scalar.activation(x[0:n, :], x[0:n, :], ACT.Identity, bias=bias[:, :]), s + "x")
                GA.chain(act, nc.scalar.activation(dst[0:n, :], x[0:n, :], ACT.Abs), s + "abs")
                GA.chain(act, nc.scalar.activation(dst[0:n, :], dst[0:n, :], ACT.Exp, scale=-1.0), s + "exp")
                GA.chain(act, nc.scalar.activation(dst[0:n, :], dst[0:n, :], ACT.Ln, bias=ONE_C[0:n, :]), s + "ln")

        def gates_exp_scalar(act):
            act.wait_ge(gp, 1 + START)
            act.wait_ge(GV.sem, GV["bM"] + START)
            nc.scalar.activation(g_wi[0:MH, 0:TP], g_wi[0:MH, 0:TP], ACT.Exp).then_inc(GA.sem, 1)
            nc.scalar.activation(pack[32:32 + MH, :], g_t0[0:MH, 0:TP], ACT.Exp).then_inc(GA.sem, 1)
            nc.scalar.activation(pack[64:64 + MH, :], g_b[0:MH, 0:TP], ACT.Exp, scale=-1.0).then_inc(GA.sem, 1)

        def gates_vector(dve):
            by_chunk = lambda ap: ap.rearrange("p (c n) -> p c n", c=NT)
            last = lambda ap, c: ap[0:MH, P * c + P - 1:P * c + P]
            dve.wait_ge(xt_full[0], NT + 1 + START)
            GV.chain(dve, nc.vector.memset(fresh[:, :], 1.0), "fresh")
            GV.chain(dve, nc.vector.memset(m_in[:, :], 0.0), "minit")
            dve.wait_ge(GA.sem, GA["fln"] + START)
            GV.chain(dve, nc.vector.scalar_tensor_tensor(g_lf[0:MH, :], g_t0[0:MH, :], 0.0, g_t1[0:MH, :], ALU.min, ALU.subtract), "lf")
            dve.wait_ge(GA.sem, GA["xln"] + START)
            GV.chain(dve, nc.vector.scalar_tensor_tensor(g_ff[:, :], g_ff[:, :], 0.0, g_M[:, :], ALU.min, ALU.subtract), "lff")
            GV.chain(dve, nc.vector.tensor_tensor_scan(g_t1[:, 0:TP], fresh[:, :], g_ff[:, 0:TP], 0.0, ALU.mult, ALU.subtract), "F")
            GV.chain(dve, nc.vector.memset(by_chunk(fresh[:, :])[:, :, 0:1], 0.0), "starts")
            GV.chain(dve, nc.vector.tensor_tensor_scan(g_b[0:MH, 0:TP], fresh[0:MH, :], g_lf[0:MH, 0:TP], 0.0, ALU.mult, ALU.add), "b")
            dve.wait_ge(gp, 1 + START)
            GV.chain(dve, nc.vector.tensor_tensor(pack[0:MH, :], g_ig[0:MH, 0:TP], g_b[0:MH, 0:TP], ALU.subtract), "g")
            for c in range(NT):
                s = slice(P * c, P * c + P)
                GV.chain(dve, nc.vector.tensor_tensor_scan(g_M[0:MH, s], pack[0:MH, s], pack[0:MH, s], m_in[:, c:c + 1], ALU.max, ALU.max), f"M{c}")
                GV.chain(dve, nc.vector.tensor_tensor(m_in[:, c + 1:c + 2], last(g_b, c), last(g_M, c), ALU.add), f"m{c}")
            M3 = by_chunk(g_M[0:MH, 0:TP])
            m3 = m_in[:, 0:NT].rearrange("p (c o) -> p c o", o=1).broadcast_to([MH, NT, P])
            GV.chain(dve, nc.vector.tensor_tensor(by_chunk(g_wi[0:MH, 0:TP]), m3, M3, ALU.subtract), "wi")
            GV.chain(dve, nc.vector.tensor_tensor(by_chunk(g_t0[0:MH, 0:TP]), by_chunk(pack[0:MH, :]),
                                                  M3[:, :, P - 1:P].broadcast_to([MH, NT, P]), ALU.subtract), "wk")
            GV.chain(dve, nc.vector.tensor_tensor(g_b[0:MH, 0:TP], g_b[0:MH, 0:TP], g_M[0:MH, 0:TP], ALU.add), "bM")

        def gates_cols_vector(dve):
            dve.wait_ge(cols_full, 1 + START)
            nc.vector.tensor_copy(cols[:, :, :].rearrange("p (b c) n -> p b c n", b=2),
                                  PS[:, 0:2, :].rearrange("p b (c n) -> p b c n", c=4)[:, :, :, 0:96]).then_inc(cols_done, 1)
            nc.vector.tensor_copy(lf_tok[:, :, :], PS[:, 2, 0:NT * FH].rearrange("p (c h) -> p c h", h=FH)).then_inc(cols_done, 1)
            nc.vector.tensor_copy(lf_sam[:, :], PS[0:NS, 2, P:P + FH]).then_inc(cols_done, 1)

        HB = 4 * ROW + 2 * 4096
        ml_q, ml_k, ml_v, ml_o, ml_M, ml_wi = ([at("hl", f"{n}{e}", [p, w], e * HB + off) for e in range(2)] for n, p, w, off in (
            ("ml_q", DK, T, 0), ("ml_k", DK, T, ROW), ("ml_v", P, T, 2 * ROW), ("ml_o", P, T, 3 * ROW),
            ("ml_M", P, TP, 4 * ROW), ("ml_wi", DK, TP, 4 * ROW + 4096)))
        AV = DV + 1
        ml_va = at("o", "ml_va", [P, NT, 132], 12608)
        ml_se = at("o", "ml_se", [P, NT, P], 16832)
        ml_qw = at("o", "ml_qw", [DK, TP], 20928)
        ml_num = at("o", "ml_num", [P, NT, AV], 25024)
        ml_kw = at("s", "ml_kw", [P, NT, DK], 0)
        ml_e = at("s", "ml_e", [P, NT, P], 2048)
        ml_hn = at("s", "ml_hn", [P, NT, P], 2048)
        ml_c = at("s", "ml_c", [DK, NT + 1, 132], 6144)
        ml_sq = at("s", "ml_sq", [P, NT, P], 10912)
        ml_out = at("s", "ml_out", [P, TP], 15008)
        ml_den, ml_r, ml_r2, ml_ss, ml_t, ml_ln, ml_rs, ml_fac, ml_abs = (
            at("s", n, [P, NT], 19104 + 32 * i) for i, n in enumerate("ml_den ml_r ml_r2 ml_ss ml_t ml_ln ml_rs ml_fac ml_abs".split()))
        ml_in = [sem("ml_in0"), sem("ml_in1")]
        MT = Steps(sem("ml_pe"), "tr st kv num ht".split())
        MA = Steps(sem("ml_act"), "va e num sq abs ln rs".split())
        MV = Steps(sem("ml_dve"), "kw zg se".split() + [f"c{c}" for c in range(NT)] + "den r r2 ss t fac hn out".split())
        MP = Steps(sem("ml_pool"), "z qw".split())
        ml_ones, ml_stored = sem("ml_ones"), sem("ml_stored")
        bank3 = lambda c: PS[:, 5 + c // 3, AV * (c % 3):AV * (c % 3) + AV]

        def heads_of(eng, body):
            with eng.Fori(0, MH // 2) as i:
                for e in range(2):
                    body(2 * i + e, e, i)

        def mlstm_sync(sp):
            sp.wait_ge(stored[0], 16 * plan["out0"][0] - 16 + START)
            sp.wait_ge(stored[1], 16 * plan["out0"][1] + START)
            sp.wait_ge(rows_out, 16 * 8 + START)

            def body(n, e, i):
                sp.wait_ge(MV.sem, (i * (2 * len(MV.names)) + (e - 1) * len(MV.names) if e == 1 else i * (2 * len(MV.names))) + START)
                src = lambda row, p: proj[bass.ds(n * p + row, p), :]
                sp.dma_start(ml_q[e][:, :], src(0, DK)).then_inc(ml_in[e], 16)
                sp.dma_start(ml_k[e][:, :], src(256, DK)).then_inc(ml_in[e], 16)
                sp.dma_start(ml_v[e][:, :], src(512, P)).then_inc(ml_in[e], 16)
                sp.dma_start(ml_o[e][:, :], src(1024, P)).then_inc(ml_in[e], 16)
                sp.dma_start(ml_M[e][:, :], mrow[0, bass.ds(n, 1), :].broadcast_to([P, TP])).then_inc(ml_in[e], 16)
                sp.dma_start(ml_wi[e][:, :], mrow[1, bass.ds(n, 1), :].broadcast_to([DK, TP])).then_inc(ml_in[e], 16)
            heads_of(sp, body)

        def mlstm_store_scalar(act, n, e, i):
            act.wait_ge(MV.sem, MV.of("out", n) + START)
            act.dma_start(mix[bass.ds(n * P, P), 0:TP], ml_out[:, :]).then_inc(ml_stored, 16)
            act.dma_start(io["p_mlstm_c"][0, 0, bass.ds(n, 1)].rearrange("o k v -> (o k) v"), ml_c[:, NT, 0:DV]).then_inc(ml_stored, 16)
            act.dma_start(io["p_mlstm_n"][0, 0, bass.ds(n, 1)].rearrange("o (k x) -> (o k) x", x=1), ml_c[:, NT, DV:AV], allow_slow_non_contiguous=True).then_inc(ml_stored, 16)

        def mlstm_tensor(pe):
            pe.wait_ge(cols_done, 3 + START)

            def body(n, e, i):
                pe.wait_ge(ml_in[e], i * 96 + 96 + START)
                for c in range(NT):
                    nc.tensor.transpose(PS[:, 1 + c // 4, P * (c % 4):P * (c % 4) + P], ml_v[e][:, P * c:P * c + P], ident[:, :])
                for c in range(NT):
                    mm = nc.tensor.transpose(PS[:, 0, DK * c:DK * c + DK], ml_k[e][:, P * c:P * c + P], ident[0:DK, 0:DK])
                mm.then_inc(MT.sem, 1)
                pe.wait_ge(MV.sem, n * len(MV.names) + START)
                for c in range(NT):
                    s = slice(P * c, P * c + P)
                    mm = nc.tensor.matmul(PS[:, 3 + c // 4, P * (c % 4):P * (c % 4) + P], ml_k[e][:, s], ml_q[e][:, s], start=True, stop=True)
                mm.then_inc(MT.sem, 1)
                pe.wait_ge(MV.sem, MV.of("kw", n) + START)
                pe.wait_ge(MA.sem, MA.of("va", n) + START)
                for c in range(NT):
                    mm = nc.tensor.matmul(bank3(c)[0:DK], ml_kw[:, c, :], ml_va[:, c, 0:AV], start=True, stop=True)
                mm.then_inc(MT.sem, 1)
                pe.wait_ge(MP.sem, MP.of("qw", n) + START)
                pe.wait_ge(MV.sem, MV.of("c7", n) + START)
                for c in range(NT):
                    nc.tensor.matmul(bank3(c), ml_se[:, c, :], ml_va[:, c, 0:AV], start=True, stop=False)
                    mm = nc.tensor.matmul(bank3(c), ml_qw[:, P * c:P * c + P], ml_c[:, c, 0:AV], start=False, stop=True)
                mm.then_inc(MT.sem, 1)
                pe.wait_ge(MV.sem, MV.of("hn", n) + START)
                for c in range(NT):
                    mm = nc.tensor.transpose(PS[:, 3 + c // 4, P * (c % 4):P * (c % 4) + P], ml_hn[:, c, :], ident[:, :])
                mm.then_inc(MT.sem, 1)
            heads_of(pe, body)

        def mlstm_scalar(act):
            def body(n, e, i):
                act.wait_ge(MT.sem, MT.of("tr", n) + START)
                nc.scalar.copy(ml_va[:, :, 0:DV].rearrange("p (b c) n -> p b c n", b=2),
                               PS[:, 1:3, :].rearrange("p b (c n) -> p b c n", c=4)).then_inc(MA.sem, 1)
                act.wait_ge(MV.sem, MV.of("zg", n) + START)
                nc.scalar.activation(ml_e[:, :, :], ml_e[:, :, :], ACT.Exp, scale=-1.0).then_inc(MA.sem, 1)
                act.wait_ge(MT.sem, MT.of("num", n) + START)
                nc.scalar.copy(ml_num[:, 0:6, :].rearrange("p (b c) n -> p b (c n)", b=2), PS[:, 5:7, 0:3 * AV])
                nc.scalar.copy(ml_num[:, 6:8, :].rearrange("p c n -> p (c n)"), PS[:, 7, 0:2 * AV]).then_inc(MA.sem, 1)
                act.wait_ge(MA.sem, MA.of("num", n) + START)
                nc.scalar.activation(ml_sq[:, :, :], ml_num[:, :, 0:DV], ACT.Square).then_inc(MA.sem, 1)
                nc.scalar.activation(ml_abs[:, :].rearrange("p (c o) -> p c o", o=1), ml_num[:, :, DV:AV], ACT.Abs).then_inc(MA.sem, 1)
                act.wait_ge(MV.sem, MV.of("t", n) + START)
                nc.scalar.activation(ml_ln[:, :], ml_t[:, :], ACT.Ln, bias=EPS_C, scale=1.0 / DV).then_inc(MA.sem, 1)
                act.wait_ge(MA.sem, MA.of("ln", n) + START)
                nc.scalar.activation(ml_rs[:, :], ml_ln[:, :], ACT.Exp, scale=-0.5).then_inc(MA.sem, 1)
                mlstm_store_scalar(act, n, e, i)
            heads_of(act, body)

        def mlstm_gpsimd(pool):
            def body(n, e, i):
                pool.wait_ge(ml_in[e], i * 96 + 96 + START)
                pool.wait_ge(MV.sem, n * len(MV.names) + START)
                by = lambda ap: ap.rearrange("p (c n) -> p c n", c=NT)
                nc.gpsimd.tensor_tensor(ml_e[:, :, :], by(ml_M[e][:, :]), mask_st[:, :].rearrange("p (o n) -> p o n", o=1).broadcast_to([P, NT, P]),
                                        ALU.add).then_inc(MP.sem, 1)
                nc.gpsimd.tensor_tensor(ml_qw[:, :], ml_q[e][:, 0:TP], ml_wi[e][:, :], ALU.mult).then_inc(MP.sem, 1)
            pool.memset(ml_va[:, :, DV:AV], 1.0).then_inc(ml_ones, 1)
            pool.memset(ml_c[:, 0, :], 0.0).then_inc(ml_ones, 1)
            pool.wait_ge(rows_out, 128 + START)
            heads_of(pool, body)

        def mlstm_vector(dve):
            dve.wait_ge(ml_ones, 2 + START)
            b4 = lambda ap: ap.rearrange("p (b c) n -> p b c n", b=2)

            def column(row, n):
                return cols[:, :, bass.ds(n + row, 1)]

            def body(n, e, i):
                N = len(MV.names)
                dve.wait_ge(MT.sem, MT.of("tr", n) + START)
                nc.vector.scalar_tensor_tensor(ml_kw[:, :, :], PS[:, 0, :].rearrange("p (c k) -> p c k", c=NT), DK ** -0.5,
                                               column(32, n).broadcast_to([P, NT, DK]), ALU.mult, ALU.mult).then_inc(MV.sem, 1)
                dve.wait_ge(MP.sem, MP.of("z", n) + START)
                nc.vector.tensor_tensor(ml_e[:, :, :], ml_e[:, :, :], column(0, n).broadcast_to([P, NT, P]), ALU.subtract).then_inc(MV.sem, 1)
                dve.wait_ge(MA.sem, MA.of("e", n) + START)
                dve.wait_ge(MT.sem, MT.of("st", n) + START)
                nc.vector.scalar_tensor_tensor(b4(ml_se[:, :, :]), PS[:, 3:5, :].rearrange("p b (c n) -> p b c n", c=4), DK ** -0.5,
                                               b4(ml_e[:, :, :]), ALU.mult, ALU.mult).then_inc(MV.sem, 1)
                dve.wait_ge(MT.sem, MT.of("kv", n) + START)
                dve.wait_ge(ml_stored, n * 48 + START)
                for c in range(NT):
                    dst = ml_c[:, c + 1, 0:AV]
                    if c:
                        dve.wait_ge(MV.sem, MV.of(f"c{c - 1}", n) + START)
                    nc.vector.scalar_tensor_tensor(dst, ml_c[:, c, 0:AV], ml_wi[e][:, P * c + P - 1:P * c + P], bank3(c)[0:DK],
                                                   ALU.mult, ALU.add).then_inc(MV.sem, 1)
                dve.wait_ge(MA.sem, MA.of("abs", n) + START)
                den = ml_den[:, :].rearrange("p (c o) -> p c o", o=1)
                MV.chain(dve, nc.vector.tensor_tensor(den, ml_abs[:, :].rearrange("p (c o) -> p c o", o=1), column(64, n), ALU.max), "den", n)
                MV.chain(dve, nc.vector.reciprocal(ml_r[:, :], ml_den[:, :]), "r", n)
                MV.chain(dve, nc.vector.tensor_tensor(ml_r2[:, :], ml_r[:, :], ml_r[:, :], ALU.mult), "r2", n)
                MV.chain(dve, nc.vector.tensor_reduce(ml_ss[:, :], ml_sq[:, :, :], AX.X, ALU.add), "ss", n)
                MV.chain(dve, nc.vector.tensor_tensor(ml_t[:, :], ml_ss[:, :], ml_r2[:, :], ALU.mult), "t", n)
                dve.wait_ge(MA.sem, MA.of("rs", n) + START)
                MV.chain(dve, nc.vector.tensor_tensor(ml_fac[:, :], ml_r[:, :], ml_rs[:, :], ALU.mult), "fac", n)
                MV.chain(dve, nc.vector.tensor_tensor(ml_hn[:, :, :], ml_num[:, :, 0:DV],
                                                      ml_fac[:, :].rearrange("p (c o) -> p c o", o=1).broadcast_to([P, NT, DV]), ALU.mult), "hn", n)
                dve.wait_ge(MT.sem, MT.of("ht", n) + START)
                out_g = vecs[:, bass.ds(n + VEC["mlstm_out_g"], 1)]
                nc.vector.scalar_tensor_tensor(ml_out[:, :].rearrange("p (b n) -> p b n", b=2), PS[:, 3:5, :], out_g,
                                               ml_o[e][:, 0:TP].rearrange("p (b n) -> p b n", b=2), ALU.mult, ALU.mult).then_inc(MV.sem, 1)
            heads_of(dve, body)

        FB = 3 * ROW + 4096
        fx_q, fx_k, fx_v, fx_F = ([at("hl", f"{n}{e}", [p, w], e * FB + off) for e in range(2)] for n, p, w, off in (
            ("fx_q", DH, T, 0), ("fx_k", DH, T, ROW), ("fx_v", DH, T, 2 * ROW), ("fx_F", P, TP, 3 * ROW)))
        fx_s = [at("hl", f"fx_s{e}", [P, TP], 2 * FB + 4096 * e) for e in range(2)]
        fx_p = [at("hl", f"fx_p{e}", [P, TP], 2 * FB + 8192 + 4096 * e) for e in range(2)]
        fx_pt = [at("o", f"fx_pt{e}", [P, NT, P], 12608 + 4096 * e) for e in range(2)]
        fx_Fd = at("o", "fx_Fd", [P, NT, P], 20800)
        fx_qs = at("o", "fx_qs", [DH, TP], 24896)
        fx_on = at("s", "fx_on", [P, NT, DH], 0)
        fx_vt = at("s", "fx_vt", [P, NT, DH], 2048)
        fx_kt = at("s", "fx_kt", [P, NT, DH], 4096)
        fx_of = at("s", "fx_of", [DH, TP], 6144)
        fx_mx = at("s", "fx_mx", [P, 2, NT], 10240)
        fx_nm, fx_rs, fx_ri = (at("s", n, [P, NT], 10304 + 32 * i) for i, n in enumerate(("fx_nm", "fx_rs", "fx_ri")))
        fx_in = [sem("fx_in0"), sem("fx_in1")]
        FQ, FT, FV, FO = sem("fx_scores"), sem("fx_turned"), sem("fx_pv"), sem("fx_out_turned")
        fx_kv_turned = sem("fx_kv_turned")
        fx_kv_kept = sem("fx_kv_kept")
        fx_scaled, fx_prob = sem("fx_scaled"), sem("fx_prob")
        fx_part, fx_max, fx_neg = sem("fx_part"), sem("fx_max"), sem("fx_neg")
        fx_ptk = sem("fx_ptk")
        fx_inv, fx_norm = sem("fx_inv"), sem("fx_norm")
        fx_diag = sem("fx_diag")
        fx_kept = sem("fx_kept")
        fx_stored, fx_turn = sem("fx_stored"), sem("fx_turn")

        def fox_heads(eng, body):
            with eng.Fori(0, FH // 2) as i:
                for e in range(2):
                    body(2 * i + e, e, i)

        def fox_sync(sp):
            sp.wait_ge(ml_stored, 48 * MH + START)
            sp.wait_ge(stored[0], 16 * plan["out0"][0] - 16 + START)

            def body(n, e, i):
                sp.wait_ge(fx_norm, ((i * 2 + e) * NT - (NT if e else 0) if e else i * (2 * NT)) + START)
                src = lambda row: proj[bass.ds(n * DH + row, DH), :]
                sp.dma_start(fx_q[e][:, :], src(1536)).then_inc(fx_in[e], 16)
                sp.dma_start(fx_k[e][:, :], src(2048)).then_inc(fx_in[e], 16)
                sp.dma_start(fx_v[e][:, :], src(2560)).then_inc(fx_in[e], 16)
                sp.dma_start(fx_F[e][:, :], frow[bass.ds(n, 1), :].broadcast_to([P, TP])).then_inc(fx_in[e], 16)
            fox_heads(sp, body)

        def fox_end(sp):
            sp.wait_ge(fx_stored, 48 * FH + START)

        def fox_gpsimd(pool):
            def body(n, e, i):
                pool.wait_ge(fx_in[e], i * 64 + 64 + START)
                pool.wait_ge(fx_max, n * NT + START)
                nc.gpsimd.tensor_tensor(fx_Fd[:, :, :], fx_F[e][:, :].rearrange("p (c n) -> p c n", c=NT),
                                        mask_ts[:, :].rearrange("p (o n) -> p o n", o=1).broadcast_to([P, NT, P]), ALU.add).then_inc(fx_diag, 1)
            fox_heads(pool, body)

        def fox_tensor(pe):
            pe.wait_ge(MV.sem, MV.of("out", MH - 1) + START)

            def scores(n, e, b):
                j = b % 2
                w = P * (b + 1)
                if b >= 2:
                    pe.wait_ge(fx_max, n * NT + (b - 1) + START)
                else:
                    pe.wait_ge(fx_max, n * NT + START)
                for x in range(0, w, 512):
                    m = min(512, w - x)
                    mm = nc.tensor.matmul(PS[:, 2 * j + x // 512, 0:m], fx_qs[:, P * b:P * b + P], fx_k[e][:, x:x + m], start=True, stop=True)
                mm.then_inc(FQ, 1)

            def weights(n, b):
                pe.wait_ge(fx_prob, n * NT + (b + 1) + START)
                pe.wait_ge(fx_ptk, n * NT + b + START)
                for c in range(b + 1):
                    mm = nc.tensor.transpose(PS[:, 4 + c // 4, P * (c % 4):P * (c % 4) + P], fx_p[b % 2][:, P * c:P * c + P], ident[:, :])
                mm.then_inc(FT, 1)

            def product(n, b):
                pe.wait_ge(fx_ptk, n * NT + (b + 1) + START)
                pe.wait_ge(fx_norm, n * NT + b + START)
                for c in range(b + 1):
                    mm = nc.tensor.matmul(PS[:, 6, 0:DH], fx_pt[b % 2][:, c, :], fx_vt[:, c, :], start=(c == 0), stop=(c == b))
                mm.then_inc(FV, 1)

            def body(n, e, i):
                pe.wait_ge(fx_in[e], i * 64 + 64 + START)
                pe.wait_ge(fx_kept, n + START)
                for r, src in enumerate((fx_v[e], fx_k[e])):
                    if r:
                        pe.wait_ge(fx_kv_kept, n * 2 + 1 + START)
                    pe.sem_inc(fx_turn, 1)
                    for c in range(NT):
                        mm = nc.tensor.transpose(PS[:, 7, DH * c:DH * c + DH], src[:, P * c:P * c + P], ident[0:DH, 0:DH])
                    mm.then_inc(fx_kv_turned, 1)
                pe.wait_ge(fx_scaled, n + 1 + START)
                pe.wait_ge(fx_kv_kept, n * 2 + 2 + START)
                scores(n, e, 0)
                for b in range(NT):
                    if b + 1 < NT:
                        scores(n, e, b + 1)
                    weights(n, b)
                    product(n, b)
                pe.wait_ge(fx_norm, n * NT + NT + START)
                pe.sem_inc(fx_turn, 1)
                for c in range(NT):
                    mm = nc.tensor.transpose(PS[0:DH, 6 + c // 4, P * (c % 4):P * (c % 4) + P], fx_on[:, c, :], ident[:, :])
                mm.then_inc(FO, 1)
            fox_heads(pe, body)

        def fox_scalar(act):
            def body(n, e, i):
                act.wait_ge(fx_in[e], i * 64 + 64 + START)
                act.wait_ge(FQ, n * NT + START)
                nc.scalar.mul(fx_qs[:, :], fx_q[e][:, 0:TP], DH ** -0.5).then_inc(fx_scaled, 1)
                act.wait_ge(FV, n * NT + START)
                act.wait_ge(fx_stored, n * 48 + START)
                for r, dst in enumerate((fx_vt, fx_kt)):
                    act.wait_ge(fx_kv_turned, n * 2 + (r + 1) + START)
                    nc.scalar.copy(dst[:, :, :].rearrange("p c d -> p (c d)"), PS[:, 7, :]).then_inc(fx_kv_kept, 1)
                for r, (src, name) in enumerate(((fx_vt, "p_fox_v"), (fx_kt, "p_fox_k"))):
                    act.wait_ge(fx_kv_kept, n * 2 + 2 + START)
                    act.dma_start(io[name][0, 0, :, bass.ds(n, 1), :].rearrange("(c p) o d -> p c (o d)", p=P), src[:, :, :]).then_inc(fx_stored, 16)
                for b in range(NT):
                    act.wait_ge(fx_neg, n * NT + (b + 1) + START)
                    act.wait_ge(FT, (n * NT + b - 1 if b >= 1 else n * NT) + START)
                    nc.scalar.activation(fx_p[b % 2][:, 0:P * (b + 1)], fx_s[b % 2][:, 0:P * (b + 1)], ACT.Exp,
                                         bias=fx_nm[:, b:b + 1], accum_out=fx_rs[:, b:b + 1]).then_inc(fx_prob, 1)
                act.wait_ge(FO, n + 1 + START)
                nc.scalar.copy(fx_of[:, :].rearrange("p (b n) -> p b n", b=2), PS[0:DH, 6:8, :]).then_inc(fx_kept, 1)
                act.wait_ge(fx_kept, n + 1 + START)
                act.dma_start(mix[bass.ds(n * DH + 512, DH), 0:TP], fx_of[:, :]).then_inc(fx_stored, 16)
            fox_heads(act, body)

        def fox_vector(dve):
            def soft(n, e, b):
                j = b % 2
                dve.wait_ge(FQ, n * NT + (b + 1) + START)
                if b >= 1:
                    dve.wait_ge(fx_prob, n * NT + b - 1 + START)
                else:
                    dve.wait_ge(fx_prob, n * NT + START)
                both = PS[:, 2 * j:2 * j + 2, :].rearrange("p b n -> p (b n)")
                dve.sem_inc(fx_turn, 1)
                first = -3.0e38
                if b:
                    nc.vector.tensor_tensor_reduce(fx_s[j][:, 0:P * b], both[:, 0:P * b], fx_F[e][:, 0:P * b], 1.0, -3.0e38,
                                                   ALU.add, ALU.max, fx_mx[:, 0, b:b + 1]).then_inc(fx_part, 1)
                    dve.wait_ge(fx_part, n * (NT - 1) + b + START)
                    dve.sem_inc(fx_turn, 1)
                    first = fx_mx[:, 0, b:b + 1]
                nc.vector.tensor_tensor_reduce(fx_s[j][:, P * b:P * b + P], both[:, P * b:P * b + P], fx_Fd[:, b, :], 1.0, first,
                                               ALU.add, ALU.max, fx_mx[:, 1, b:b + 1]).then_inc(fx_max, 1)
                dve.wait_ge(fx_max, n * NT + (b + 1) + START)
                nc.vector.tensor_scalar(fx_nm[:, b:b + 1], fx_mx[:, 1, b:b + 1], -1.0, None, ALU.mult).then_inc(fx_neg, 1)

            def turned(n, b):
                dve.wait_ge(FT, n * NT + (b + 1) + START)
                dve.wait_ge(FV, (n * NT + b - 1 if b >= 1 else n * NT) + START)
                k = min(4, b + 1)
                m = b + 1 - k
                if m:
                    nc.vector.tensor_copy(fx_pt[b % 2][:, 0:4, :].rearrange("p c n -> p (c n)"), PS[:, 4, :])
                    nc.vector.tensor_copy(fx_pt[b % 2][:, 4:4 + m, :].rearrange("p c n -> p (c n)"), PS[:, 5, 0:P * m]).then_inc(fx_ptk, 1)
                else:
                    nc.vector.tensor_copy(fx_pt[b % 2][:, 0:k, :].rearrange("p c n -> p (c n)"), PS[:, 4, 0:P * k]).then_inc(fx_ptk, 1)

            def out(n, b):
                nc.vector.reciprocal(fx_ri[:, b:b + 1], fx_rs[:, b:b + 1]).then_inc(fx_inv, 1)
                dve.wait_ge(fx_inv, n * NT + (b + 1) + START)
                dve.wait_ge(FV, n * NT + (b + 1) + START)
                nc.vector.tensor_scalar(fx_on[:, b, :], PS[:, 6, 0:DH], fx_ri[:, b:b + 1], None, ALU.mult).then_inc(fx_norm, 1)

            def body(n, e, i):
                dve.wait_ge(fx_diag, n + 1 + START)
                dve.wait_ge(FO, n + START)
                soft(n, e, 0)
                for b in range(NT):
                    if b + 1 < NT:
                        soft(n, e, b + 1)
                    turned(n, b)
                    out(n, b)
            fox_heads(dve, body)

        places = {}

        def packer(region, start=0):
            off = [start]

            def put(name, shape, dt=F32):
                a = off[0]
                off[0] += (4 * int(np.prod(shape[1:])) + 31) // 32 * 32
                places[name] = (region, a)
                return at(region, name, shape, a, dt)
            return put

        BH = NS * MH
        BF = NS * FH
        NP = NS * NPAGES
        R4 = 4
        put = packer("hl")
        d_v = put("d_v", [P, NP, FH * DH])
        d_k = [put(f"d_k{e}", [P, FH * DH]) for e in range(2)]
        d_qb = [put(f"d_qb{e}", [P, FH * DH]) for e in range(2)]
        d_kq = put("d_kq", [P, FH * DH])
        d_C = put("d_C", [P, DK // R4, DV])
        d_Ct = put("d_Ct", [P, DK // R4, DV])
        put = packer("o")
        d_fm = put("d_fm", [P, 24, NS])
        d_tm = put("d_tm", [NS, 24 * P])
        d_sc = put("d_sc", [P, NPAGES, BF])
        d_lf = put("d_lf", [P, NPAGES, BF])
        d_st = put("d_st", [BF, 2 * PAGE + 1])
        d_pr = put("d_pr", [BF, 2 * PAGE + 1])
        d_pt = put("d_pt", [P, NPAGES, BF])
        d_self, d_wself = put("d_self", [NS, FH]), put("d_wself", [NS, FH])
        d_w2 = put("d_w2", [NS, 4, NS, 2])
        d_qk = put("d_qk", [NS, FH * DH])
        d_ld = put("d_ld", [FH, NS, FH])
        d_tri = put("d_tri", [P, P])
        d_of = put("d_of", [P, 4, NS])
        put = packer("s")
        d_spread = put("d_spread", [BH, P])
        d_gather = put("d_gather", [P, BH])
        d_row = put("d_row", [BH, DV + 3])
        d_rep = put("d_rep", [P, DV + 3])
        d_q4, d_k4, d_n4, d_t4 = (put(n, [P, DK // R4]) for n in ("d_q4", "d_k4", "d_n4", "d_t4"))
        d_par = put("d_par", [P, DV + 3])
        d_sum = put("d_sum", [BH, DV + 3])
        d_h, d_hn = put("d_h", [BH, DV]), put("d_hn", [BH, DV])
        d_sq = put("d_sq", [BH, DV])
        d_hm = put("d_hm", [P, MH, NS])
        d_c = put("d_c", [P, 16])
        d_max, d_sumw, d_inv = (put(n, [BF, 1]) for n in ("d_max", "d_sumw", "d_inv"))
        d_pg = put("d_pg", [1, NP], I32)
        sam = dram("sam", [NS, 24 * P])
        d_fm_in, d_state_in, d_rows_in, d_lf_in, d_pg_in, d_self_in, d_wself_in, d_out, d_sam_out = (
            sem(s) for s in ("d_fm_in", "d_state_in", "d_rows_in", "d_lf_in", "d_pg_in", "d_self_in", "d_wself_in", "d_out", "d_sam_out"))
        d_k_in, d_v_in, d_q_in = [sem("d_k_in0"), sem("d_k_in1")], sem("d_v_in"), [sem("d_q_in0"), sem("d_q_in1")]
        d_kq_done, d_sc_done = sem("d_kq_done"), sem("d_sc_done")
        EP = Steps(sem("d_pool"), "z1 z2 tri s1 s2 g1 g2".split())
        ET = Steps(sem("d_pe"), "turn rep bias st pt pv sum hm".split())
        EA = Steps(sem("d_act"), "tm rep winter wintra em exp pt of0 of1 sq ln rs".split())
        EV = Steps(sem("d_dve"), ("lfm m di da kw nt n ct c cq cs nq ns e4 m4 qk self ld bias st self8 max neg inv pr "
                                  "w0 w1 w2 w3 dsum dneg dabs dmax dinv h hn hm0 hm1 hm2 hm3").split())

        def dec0_sync(sp):
            sp.wait_ge(fx_stored, 48 * FH + START)
            sp.wait_ge(stored[0], 16 * (plan["out0"][0] - 1) + START)
            sp.wait_ge(stored[1], 16 * plan["out0"][1] + START)
            sp.wait_ge(rows_out, 128 + START)
            sp.dma_start(d_fm[:, :, :], proj.rearrange("(k p) t -> p k t", p=P)[:, :, TP:T]).then_inc(d_fm_in, 16)
            sp.dma_start(d_C[:, :, :], io["state_mlstm_c"][0].rearrange("b h (r d) v -> (b h r) d v", r=R4)).then_inc(d_state_in, 16)
            sp.dma_start(d_n4[:, :], io["state_mlstm_n"][0].rearrange("b h (r d) -> (b h r) d", r=R4)).then_inc(d_state_in, 16)
            sp.dma_start(d_row[:, DV + 2:DV + 3], io["state_mlstm_m"][0].rearrange("b (h o) -> (b h) o", o=1), allow_slow_non_contiguous=True).then_inc(d_rows_in, 16)
            for j in range(2):
                for h in range(MH):
                    sp.dma_start(d_row[h:BH:MH, DV + j:DV + j + 1], lfs[j, h:h + 1, :].rearrange("h b -> b h"), allow_slow_non_contiguous=True).then_inc(d_rows_in, 16)
            sp.dma_start(d_pg[:, :], io["page_table"].rearrange("(o b) n -> o (b n)", o=1)).then_inc(d_pg_in, 16)
            sp.wait_ge(EA.sem, EA["tm"] + START)
            sp.dma_start(sam, d_tm[:, :]).then_inc(d_sam_out, 16)
            sp.dma_start(io["s_fox_k"][0].rearrange("b o h d -> b (o h d)"), d_tm[:, 2048:2560]).then_inc(d_out, 16)
            sp.dma_start(io["s_fox_v"][0].rearrange("b o h d -> b (o h d)"), d_tm[:, 2560:3072]).then_inc(d_out, 16)
            sp.dma_start(d_q4[:, :], d_tm[:, 0:256]).then_inc(d_state_in, 16)
            sp.dma_start(d_k4[:, :], d_tm[:, 256:512]).then_inc(d_state_in, 16)
            sp.dma_start(d_row[:, 0:DV], d_tm[:, 512:1024]).then_inc(d_rows_in, 16)
            sp.wait_ge(d_sam_out, 16 + START)
            sp.wait_ge(d_pg_in, 16 + START)
            for b in range(NS):
                if b >= 2:
                    sp.wait_ge(d_kq_done, 2 * b - 2 + START)
                sp.dma_start(d_qb[b % 2][:, :], sam[b:b + 1, 1536:2048].broadcast_to([P, FH * DH])).then_inc(d_q_in[b % 2], 16)
                for p in range(NPAGES):
                    i = NPAGES * b + p
                    page = sp.value_load(d_pg[0:1, i:i + 1], min_val=0, max_val=io["cache_fox_k"].shape[1] - 1)
                    if i >= 2:
                        sp.wait_ge(d_kq_done, i - 1 + START)
                    sp.dma_start(d_k[i % 2][:, :], io["cache_fox_k"][0, bass.ds(page, 1)].rearrange("o t h d -> (o t) (h d)")).then_inc(d_k_in[i % 2], 16)
                    sp.dma_start(d_v[:, i, :], io["cache_fox_v"][0, bass.ds(page, 1)].rearrange("o t h d -> (o t) (h d)")).then_inc(d_v_in, 16)
                    sp.dma_start(d_lf[:, p, FH * b:FH * b + FH], io["cache_fox_lf"][0, bass.ds(page, 1)].rearrange("o t h -> (o t) h")).then_inc(d_lf_in, 16)
            sp.wait_ge(EV.sem, EV["c"] + START)
            sp.dma_start(io["s_mlstm_c"][0].rearrange("b h (r d) v -> (b h r) d v", r=R4), d_C[:, :, :]).then_inc(d_out, 16)
            sp.dma_start(io["s_mlstm_n"][0].rearrange("b h (r d) -> (b h r) d", r=R4), d_n4[:, :]).then_inc(d_out, 16)
            sp.wait_ge(EV.sem, EV["self"] + START)
            sp.dma_start(d_st[:, 2 * PAGE:2 * PAGE + 1], d_self[:, :], allow_slow_non_contiguous=True).then_inc(d_self_in, 16)
            sp.wait_ge(EV.sem, EV["pr"] + START)
            sp.dma_start(d_wself[:, :], d_pr[:, 2 * PAGE:2 * PAGE + 1], allow_slow_non_contiguous=True).then_inc(d_wself_in, 16)
            sp.wait_ge(EA.sem, EA["of1"] + START)
            sp.dma_start(mix[512:1024, TP:T].rearrange("(j p) t -> p j t", p=P), d_of[:, :, :]).then_inc(d_out, 16)
            sp.wait_ge(EV.sem, EV["hm3"] + START)
            sp.dma_start(io["s_mlstm_m"][0].rearrange("b (h o) -> (b h) o", o=1), d_sum[:, DV + 2:DV + 3], allow_slow_non_contiguous=True).then_inc(d_out, 16)
            sp.dma_start(mix[0:512, TP:T].rearrange("(j p) t -> p j t", p=P), d_hm[:, :, :]).then_inc(d_out, 16)

        def dec0_end(sp):
            sp.wait_ge(d_out, 16 * 7 + START)

        def dec0_gpsimd(pool):
            pool.wait_ge(fx_stored, 48 * FH + START)
            EP.chain(pool, pool.memset(d_spread[:, :], 1.0), "z1")
            EP.chain(pool, pool.memset(d_gather[:, :], 1.0), "z2")
            EP.chain(pool, pool.affine_select(out=d_tri[:, :], in_=ones[:, :], compare_op=ALU.is_ge, fill=0.0,
                                              base=-1, pattern=[[-1, P]], channel_multiplier=1), "tri")
            for name, base, m in (("s1", 0, 1), ("s2", R4 - 1, -1)):
                EP.chain(pool, pool.affine_select(out=d_spread[:, :], in_=d_spread[:, :], compare_op=ALU.is_ge, fill=0.0,
                                                  base=base, pattern=[[m, P]], channel_multiplier=-m * R4), name)
            for name, base, m in (("g1", 0, 1), ("g2", R4 - 1, -1)):
                EP.chain(pool, pool.affine_select(out=d_gather[:, :], in_=d_gather[:, :], compare_op=ALU.is_ge, fill=0.0,
                                                  base=base, pattern=[[-m * R4, BH]], channel_multiplier=m), name)

        def dec0_tensor(pe):
            pe.wait_ge(fx_kept, FH + START)
            pe.wait_ge(d_fm_in, 16 + START)
            for k in range(24):
                mm = nc.tensor.transpose(PS[0:NS, k // 4, P * (k % 4):P * (k % 4) + P], d_fm[:, k, :], ident[:, :])
            mm.then_inc(ET.sem, 1)
            pe.wait_ge(EP.sem, EP["g2"] + START)
            pe.wait_ge(d_rows_in, 16 * (2 + 2 * MH) + START)
            nc.tensor.matmul(PS[:, 6, 0:DV + 3], d_spread[:, :], d_row[:, :], start=True, stop=True).then_inc(ET.sem, 1)
            pe.wait_ge(d_lf_in, 16 * NP + START)
            pe.wait_ge(EV.sem, EV["ld"] + START)
            nc.tensor.matmul(PS[:, 7, BF:2 * BF], d_tri[:, :], d_lf[:, 1, :], start=True, stop=False)
            nc.tensor.matmul(PS[:, 7, BF:2 * BF], ones[0:FH, :], d_ld[:, :, :].rearrange("p b h -> p (b h)"), start=False, stop=True)
            nc.tensor.matmul(PS[:, 7, 0:BF], d_tri[:, :], d_lf[:, 0, :], start=True, stop=False)
            nc.tensor.matmul(PS[:, 7, 0:BF], ones[:, :], d_lf[:, 1, :], start=False, stop=False)
            nc.tensor.matmul(PS[:, 7, 0:BF], ones[0:FH, :], d_ld[:, :, :].rearrange("p b h -> p (b h)"), start=False, stop=True).then_inc(ET.sem, 1)
            pe.wait_ge(EV.sem, EV["bias"] + START)
            pe.wait_ge(EA.sem, EA["tm"] + START)
            for p in range(NPAGES):
                mm = nc.tensor.transpose(PS[0:BF, 0, P * p:P * p + P], d_sc[:, p, :], ident[:, :])
            mm.then_inc(ET.sem, 1)
            pe.wait_ge(EV.sem, EV["pr"] + START)
            for p in range(NPAGES):
                mm = nc.tensor.transpose(PS[:, 1, BF * p:BF * p + BF], d_pr[:, P * p:P * p + P], ident[0:BF, 0:BF])
            mm.then_inc(ET.sem, 1)
            pe.wait_ge(d_v_in, 16 * NP + START)
            pe.wait_ge(EV.sem, EV["w3"] + START)
            pe.wait_ge(EA.sem, EA["pt"] + START)
            for j in range(4):
                out = lambda b: PS[:, 2, 2 * (NS * j + b):2 * (NS * j + b) + 2]
                nc.tensor.matmul(PS[:, 2, 2 * NS * j:2 * NS * (j + 1)], d_tm[:, 2560 + P * j:2560 + P * j + P],
                                 d_w2[:, j, :, :].rearrange("p b e -> p (b e)"), start=True, stop=False, skip_group_check=True)
                for i in range(NP):
                    b, p = i // NPAGES, i % NPAGES
                    mm = nc.tensor.matmul(out(b), d_v[:, i, P * j:P * j + P], d_pt[:, p, FH * b + 2 * j:FH * b + 2 * j + 2],
                                          start=False, stop=(i == NP - 1), skip_group_check=True)
            mm.then_inc(ET.sem, 1)
            pe.wait_ge(EV.sem, EV["m4"] + START)
            nc.tensor.matmul(PS[0:BH, 3, 0:DV + 3], d_gather[:, :], d_par[:, :], start=True, stop=True).then_inc(ET.sem, 1)
            pe.wait_ge(EV.sem, EV["hn"] + START)
            nc.tensor.transpose(PS[:, 4, 0:BH], d_hn[:, :], ident[0:BH, 0:BH]).then_inc(ET.sem, 1)

        d_col = lambda i: d_c[:, i:i + 1]
        LFM, MN, DI, DA, WI, WA = (d_col(i) for i in range(6))
        DN, DX, RI, LN_, RS, SS = (d_c[0:BH, 6 + i:7 + i] for i in range(6))

        def dec0_scalar(act):
            act.wait_ge(ET.sem, ET["turn"] + START)
            EA.chain(act, nc.scalar.copy(d_tm[:, :].rearrange("p (b n) -> p b n", b=6), PS[0:NS, 0:6, :]), "tm")
            act.wait_ge(ET.sem, ET["rep"] + START)
            EA.chain(act, nc.scalar.copy(d_rep[:, :], PS[:, 6, 0:DV + 3]), "rep")
            act.wait_ge(EV.sem, EV["da"] + START)
            EA.chain(act, nc.scalar.activation(WI, DI, ACT.Exp), "winter")
            EA.chain(act, nc.scalar.activation(WA, DA, ACT.Exp), "wintra")
            EA.chain(act, nc.scalar.activation(d_par[:, DV + 1:DV + 2], MN, ACT.Exp, scale=-1.0), "em")
            act.wait_ge(EV.sem, EV["neg"] + START)
            EA.chain(act, nc.scalar.activation(d_pr[:, :], d_st[:, :], ACT.Exp, bias=d_max[:, :], accum_out=d_sumw[:, :]), "exp")
            act.wait_ge(ET.sem, ET["pt"] + START)
            EA.chain(act, nc.scalar.copy(d_pt[:, :, :].rearrange("p n b -> p (n b)"), PS[:, 1, 0:2 * BF]), "pt")
            act.wait_ge(ET.sem, ET["pv"] + START)
            out = PS[:, 2, 0:2 * NS * 4].rearrange("p (j b e) -> p j b e", j=4, e=2)
            for e in range(2):
                EA.chain(act, nc.scalar.copy(d_of[64 * e:64 * e + 64, :, :], out[64 * e:64 * e + 64, :, :, e]), f"of{e}")
            act.wait_ge(EV.sem, EV["h"] + START)
            EA.chain(act, nc.scalar.activation(d_sq[:, :], d_h[:, :], ACT.Square, accum_out=SS), "sq")
            EA.chain(act, nc.scalar.activation(LN_, SS, ACT.Ln, bias=EPS_C[0:BH, :], scale=1.0 / DV), "ln")
            EA.chain(act, nc.scalar.activation(RS, LN_, ACT.Exp, scale=-0.5), "rs")

        def dec0_vector(dve):
            c = lambda ins, name: EV.chain(dve, ins, name)
            tt, ts, stt = nc.vector.tensor_tensor, nc.vector.tensor_scalar, nc.vector.scalar_tensor_tensor
            IG, LF, M0 = (d_rep[:, DV + j:DV + j + 1] for j in range(3))
            cut = lambda ap, o: ap.rearrange("p (d o) -> p d o", o=1).broadcast_to([P, DK // R4, DV])
            dve.wait_ge(EA.sem, EA["rep"] + START)
            c(tt(LFM, LF, M0, ALU.add), "lfm")
            c(tt(MN, LFM, IG, ALU.max), "m")
            c(tt(DI, LFM, MN, ALU.subtract), "di")
            c(tt(DA, IG, MN, ALU.subtract), "da")
            dve.wait_ge(EA.sem, EA["wintra"] + START)
            dve.wait_ge(d_state_in, 64 + START)
            c(ts(d_k4[:, :], d_k4[:, :], WA, DK ** -0.5, ALU.mult, ALU.mult), "kw")
            c(ts(d_n4[:, :], d_n4[:, :], WI, None, ALU.mult), "nt")
            c(tt(d_n4[:, :], d_n4[:, :], d_k4[:, :], ALU.add), "n")
            vrep = d_rep[:, 0:DV].rearrange("p (o v) -> p o v", o=1).broadcast_to([P, DK // R4, DV])
            c(tt(d_Ct[:, :, :], cut(d_k4[:, :], 1), vrep, ALU.mult), "ct")
            c(stt(d_C[:, :, :], d_C[:, :, :], WI, d_Ct[:, :, :], ALU.mult, ALU.add), "c")
            c(tt(d_Ct[:, :, :], d_C[:, :, :], cut(d_q4[:, :], 1), ALU.mult), "cq")
            c(nc.vector.tensor_reduce(d_par[:, 0:DV], d_Ct[:, :, :].rearrange("p d v -> p v d"), AX.X, ALU.add), "cs")
            c(tt(d_t4[:, :], d_n4[:, :], d_q4[:, :], ALU.mult), "nq")
            c(nc.vector.tensor_reduce(d_par[:, DV:DV + 1], d_t4[:, :], AX.X, ALU.add), "ns")
            dve.wait_ge(EA.sem, EA["em"] + START)
            c(ts(d_par[:, DV + 1:DV + 2], d_par[:, DV + 1:DV + 2], 1.0 / R4, None, ALU.mult), "e4")
            c(ts(d_par[:, DV + 2:DV + 3], MN, 1.0 / R4, None, ALU.mult), "m4")
            c(tt(d_qk[:, :], d_tm[:, 1536:2048], d_tm[:, 2048:2560], ALU.mult), "qk")
            c(nc.vector.tensor_reduce(d_self[:, :], d_qk[:, :].rearrange("p (h d) -> p h d", h=FH), AX.X, ALU.add), "self")
            c(tt(d_ld[:, :, :], ident[0:FH, 0:FH].rearrange("p (o h) -> p o h", o=1).broadcast_to([FH, NS, FH]),
                 g_ff[:, TP:T].rearrange("p (b o) -> p b o", o=1).broadcast_to([FH, NS, FH]), ALU.mult), "ld")
            for i in range(NP):
                b, p = i // NPAGES, i % NPAGES
                dve.wait_ge(d_q_in[b % 2], 16 * (b // 2 + 1) + START)
                dve.wait_ge(d_k_in[i % 2], 16 * (i // 2 + 1) + START)
                if i:
                    dve.wait_ge(d_sc_done, i + START)
                tt(d_kq[:, :], d_k[i % 2][:, :], d_qb[b % 2][:, :], ALU.mult).then_inc(d_kq_done, 1)
                dve.wait_ge(d_kq_done, i + 1 + START)
                nc.vector.tensor_reduce(d_sc[:, p, FH * b:FH * b + FH], d_kq[:, :].rearrange("p (h d) -> p h d", h=FH), AX.X, ALU.add).then_inc(d_sc_done, 1)
            dve.wait_ge(d_sc_done, NP + START)
            dve.wait_ge(ET.sem, ET["bias"] + START)
            c(stt(d_sc[:, :, :], d_sc[:, :, :], DH ** -0.5, PS[:, 7, 0:2 * BF].rearrange("p (n b) -> p n b", n=NPAGES), ALU.mult, ALU.add), "bias")
            dve.wait_ge(ET.sem, ET["st"] + START)
            dve.wait_ge(d_self_in, 16 + START)
            c(nc.vector.tensor_copy(d_st[:, 0:2 * PAGE], PS[0:BF, 0, 0:2 * PAGE]), "st")
            c(ts(d_st[:, 2 * PAGE:2 * PAGE + 1], d_st[:, 2 * PAGE:2 * PAGE + 1], DH ** -0.5, None, ALU.mult), "self8")
            c(nc.vector.tensor_reduce(d_inv[:, :], d_st[:, :], AX.X, ALU.max), "max")
            c(ts(d_max[:, :], d_inv[:, :], -1.0, None, ALU.mult), "neg")
            dve.wait_ge(EA.sem, EA["exp"] + START)
            c(nc.vector.reciprocal(d_inv[:, :], d_sumw[:, :]), "inv")
            c(ts(d_pr[:, :], d_pr[:, :], d_inv[:, :], None, ALU.mult), "pr")
            dve.wait_ge(d_wself_in, 16 + START)
            for j in range(4):
                c(tt(d_w2[:, j, :, :], ident[0:NS, 0:NS].rearrange("p (b o) -> p b o", o=1).broadcast_to([NS, NS, 2]),
                     d_wself[:, 2 * j:2 * j + 2].rearrange("p (o e) -> p o e", o=1).broadcast_to([NS, NS, 2]), ALU.mult), f"w{j}")
            dve.wait_ge(ET.sem, ET["sum"] + START)
            c(nc.vector.tensor_copy(d_sum[:, :], PS[0:BH, 3, 0:DV + 3]), "dsum")
            c(ts(DN, d_sum[:, DV:DV + 1], -1.0, None, ALU.mult), "dneg")
            c(tt(DN, DN, d_sum[:, DV:DV + 1], ALU.max), "dabs")
            c(tt(DX, DN, d_sum[:, DV + 1:DV + 2], ALU.max), "dmax")
            c(nc.vector.reciprocal(RI, DX), "dinv")
            c(ts(d_h[:, :], d_sum[:, 0:DV], RI, None, ALU.mult), "h")
            dve.wait_ge(EA.sem, EA["rs"] + START)
            c(ts(d_hn[:, :], d_h[:, :], RS, None, ALU.mult), "hn")
            dve.wait_ge(ET.sem, ET["hm"] + START)
            for h in range(MH):
                c(stt(d_hm[:, h, :], PS[:, 4, 0:BH].rearrange("p (b h) -> p b h", h=MH)[:, :, h], vec("mlstm_out_g", h),
                      d_fm[:, 8 + h, :], ALU.mult, ALU.mult), f"hm{h}")

        mix_in = [sem("mix_in0"), sem("mix_in1")]

        def mix_sync(sp, n, src):
            for half in range(2):
                sp.dma_start(oT[:, 4 * half:4 * half + 4, :], src.rearrange("(k p) t -> p k t", p=P)[:, 4 * half:4 * half + 4, :]).then_inc(mix_in[half], 16)

        def mix_split_vector(dve, r, n):
            def make(k):
                if k % 4 == 0:
                    dve.wait_ge(mix_in[k // 4], 16 * n + 16 + START)
                return nc.vector.tensor_copy(hf[:, k % 2, :], oT[:, k, :])
            split_vector(dve, r, make)

        def after(name):
            return lambda eng: [eng.wait_ge(psum_free[u], plan[name][u] + START) for u in range(2)]

        xx = at("h", "xx", [P, KT, T], 0)
        sh_in = at("hl", "sh_in", [NS, D], 0)
        sh_out = at("s", "sh_out", [NS + 1, D], 2 * ROW)
        lora = at("s", "lora", [P, T], 2 * ROW)
        rw = dram("rw", [6 * D, T])
        RW = {n: i * D for i, n in enumerate("rkvsag")}
        mix2 = dram("mix2", [D, T])
        sh_loaded, sh_turned, h_ready, xx_ready, sh_full, sh_kept, sh_stored = (
            sem(s) for s in ("sh_loaded", "sh_turned", "h_ready", "xx_ready", "sh_full", "sh_kept", "sh_stored"))
        w2_loaded, lora_ready = sem("w2_loaded"), sem("lora_ready")
        z_full, z_free = [sem("z_full0"), sem("z_full1")], [sem("z_free0"), sem("z_free1")]
        w2_in = at("s", "w2_in", [P, D], 0)
        MIXES = (("w", 1), ("a", 4), ("g", 5), ("r", 0), ("k", 2), ("v", 3))
        LORA = {"w": ("rwkv_w1", "rwkv_w2", 64, ACT.Tanh, "s"), "a": ("rwkv_a1", "rwkv_a2", 64, ACT.Copy, "a"),
                "g": ("rwkv_g1", "rwkv_g2", 128, ACT.Sigmoid, "g")}
        R0 = 3
        S0 = 12
        kt_of = lambda name: io[name][0].rearrange("(k p) n -> p k n", p=P)

        def shift_sync(sp):
            sp.wait_ge(psum_full[1], plan["a_w"][1] + START)
            sp.dma_start(sh_in[:, :], io["state_rwkv_shift"][0]).then_inc(sh_loaded, 16)

        def shift_tensor(pe):
            pe.wait_ge(sh_loaded, 16 + START)
            for k in range(KT):
                mm = nc.tensor.transpose(PS[:, 6, NS * k:NS * k + NS], sh_in[:, P * k:P * k + P], ident[0:NS, 0:NS])
            mm.then_inc(sh_turned, 1)
            pe.wait_ge(xx_ready, 3 + START)
            for k in range(KT):
                mm = nc.tensor.transpose(PS[0:NS + 1, 6 + k // 4, P * (k % 4):P * (k % 4) + P], oT[:, k, TP - 1:T], ident[:, :])
            mm.then_inc(sh_full, 1)

        def shift_vector(dve):
            dve.wait_ge(rstd_ready, 5 + START)
            for k in range(KT):
                mm = nc.vector.scalar_tensor_tensor(oT[:, k, :], xT[:, k, :], gains[:, 4, k:k + 1], rstd[:, :], ALU.mult, ALU.mult)
                mm.then_inc(h_ready, 1)
            dve.wait_ge(h_ready, KT + START)
            dve.wait_ge(psum_free[1], plan["a_w"][1] + START)
            nc.vector.tensor_tensor(xx[:, :, 1:TP], oT[:, :, 0:TP - 1], oT[:, :, 1:TP], ALU.subtract).then_inc(xx_ready, 1)
            nc.vector.tensor_scalar(xx[:, :, 0:1], oT[:, :, 0:1], -1.0, None, ALU.mult).then_inc(xx_ready, 1)
            dve.wait_ge(sh_turned, 1 + START)
            nc.vector.tensor_tensor(xx[:, :, TP:T], PS[:, 6, 0:KT * NS].rearrange("p (k n) -> p k n", k=KT),
                                    oT[:, :, TP:T], ALU.subtract).then_inc(xx_ready, 1)
            dve.wait_ge(xx_ready, 3 + START)

        def shift_scalar(act):
            act.wait_ge(sh_full, 1 + START)
            act.wait_ge(sq_used, KT * 5 + START)
            act.wait_ge(ss_ready, 5 + START)
            nc.scalar.copy(sh_out[:, :].rearrange("p (b n) -> p b n", b=2), PS[0:NS + 1, 6:8, :]).then_inc(sh_kept, 1)
            act.wait_ge(sh_kept, 1 + START)
            act.dma_start(io["p_rwkv_shift"][0], sh_out[0:1, :]).then_inc(sh_stored, 16)
            act.dma_start(io["s_rwkv_shift"][0], sh_out[1:NS + 1, :]).then_inc(sh_stored, 16)

        def mixes_sync(sp):
            nl = 0
            for n, (m, _) in enumerate(MIXES):
                if m in LORA:
                    w1, w2, rank = LORA[m][:3]
                    load_w(sp, 0, plan[f"a_{m}"][0], kt_of(w1), w_raw[:, 0, :, 0:rank])
                    sp.wait_ge(act_ready, KT * (R0 + n + 1) + START)
                    sp.dma_start(w2_in[0:rank, :], io[w2][0]).then_inc(w2_loaded, 16)
                else:
                    load_pairs(sp, f"a_{m}", 4, kt_of("rwkv_w_" + m))

        def mixes_gpsimd(pool):
            for m, _ in MIXES:
                k0, k1 = plan[f"a_{m}"]
                if m in LORA:
                    split_w(pool, 0, k0, KT, k0 + k1 + 1)
                else:
                    split_pairs(pool, f"a_{m}", 4, KT)

        def mixes_tensor(pe):
            for n, (m, _) in enumerate(MIXES):
                r = R0 + n
                if m not in LORA:
                    gemm_tensor(pe, f"a_{m}", 4, r)
                    continue
                rank = LORA[m][2]
                tile_products(pe, 0, plan[f"a_{m}"][0], act_hi, act_lo, KT, act_ready, KT * r)
                pe.wait_ge(lora_ready, n + 1 + START)
                pe.wait_ge(w2_loaded, 16 * n + 16 + START)
                for j in range(KT):
                    u = j % 2
                    if 4 * n + j // 2:
                        pe.wait_ge(z_free[u], 4 * n + j // 2 + START)
                    for c in range(NCH):
                        mm = nc.tensor.matmul(PS[:, 3 * u + c, 0:CH], w2_in[0:rank, P * j:P * j + P], lora[0:rank, CH * c:CH * c + CH],
                                              start=True, stop=True)
                    mm.then_inc(z_full[u], 1)
                for u in range(2):
                    pe.wait_ge(z_free[u], 4 * n + 4 + START)

        def mixes_scalar(act):
            stores = S0
            for n, (m, _) in enumerate(MIXES):
                r = R0 + n
                if n:
                    for u in range(2):
                        act.wait_ge(psum_full[u], plan[f"a_{m}"][u] + START)
                split_scalar(act, r)
                if m not in LORA:
                    store_scalar(act, f"a_{m}", 4, rw, RW[m], stores)
                    stores += 4
                    continue
                _, _, rank, func, out = LORA[m]
                k0 = plan[f"a_{m}"][0]
                act.wait_ge(psum_full[0], k0 + 1 + START)
                if n == 0:
                    act.wait_ge(sh_stored, 32 + START)
                else:
                    act.wait_ge(z_full[1], 4 * n + START)
                nc.scalar.activation(chunks(lora[:, :])[0:rank], PS[0:rank, 0:3, 0:CH], func).then_inc(psum_free[0], 1)
                act.wait_ge(psum_free[0], k0 + 1 + START)
                act.sem_inc(lora_ready, 1)
                for j in range(KT):
                    u = j % 2
                    act.wait_ge(z_full[u], 4 * n + j // 2 + 1 + START)
                    act.wait_ge(stored[u], 16 * (stores + j // 2) + START)
                    dst = chunks(stage[:, u, :])
                    if m == "g":
                        ins = nc.scalar.copy(dst, banks(u))
                    else:
                        ins = nc.scalar.activation(dst, banks(u), ACT.Sigmoid, bias=vec(f"rwkv_{m}0", j))
                    ins.then_inc(z_free[u], 1)
                    act.wait_ge(z_free[u], 4 * n + j // 2 + 1 + START)
                    act.dma_start(rw[RW[out] + P * j:RW[out] + P * j + P, :], stage[:, u, :]).then_inc(stored[u], 16)
                stores += 4

        def mixes_vector(dve):
            for n, (m, i) in enumerate(MIXES):
                if n:
                    for u in range(2):
                        dve.wait_ge(psum_full[u], plan[f"a_{m}"][u] + START)
                    if n <= 3:
                        dve.wait_ge(z_full[0], 4 * n + START)
                        dve.wait_ge(z_full[1], 4 * n + START)
                split_vector(dve, R0 + n, lambda k: nc.vector.scalar_tensor_tensor(
                    hf[:, k % 2, :], xx[:, k, :], vec("rwkv_mix", KT * i + k), oT[:, k, :], ALU.mult, ALU.add))

        C0 = math.exp(-0.5)
        PAIRS = RH // 2
        L2 = 2 * P
        put = packer("hl")
        b_in = {n: put(f"b_{n}", [P, T]) for n in "rksavg"}
        b_AR = put("b_AR", [P, NT, L2])
        b_B, b_K = put("b_B", [P, TP]), put("b_K", [P, TP])
        b_bv = put("b_bv", [P, T])
        b_cs, b_P, b_iP, b_Pm = (put(n, [P, T]) for n in ("b_cs", "b_P", "b_iP", "b_Pm"))
        b_kkn = put("b_kkn", [P, T])
        put = packer("o")
        b_kp, b_b = put("b_kp", [P, T]), put("b_b", [P, T])
        b_y = put("b_y", [P, NT, P])
        b_ysq = put("b_ysq", [P, NT, P])
        b_Z, b_CZ, b_W = (put(n, [P, 8, P]) for n in ("b_Z", "b_CZ", "b_W"))
        b_GT = put("b_GT", [DH, 8, P])
        put = packer("h")
        tm = {n: put(f"tm_{n}", [P, NT, P]) for n in "VBK"}
        b_ab = [put(f"b_ab{l}", [P, 4, L2]) for l in range(2)]
        b_ak = [put(f"b_ak{l}", [P, 4, L2]) for l in range(2)]
        put = packer("s")
        b_X, b_XTc, b_T1 = ([put(f"{n}{l}", [P, 4, 32]) for l in range(2)] for n in ("b_X", "b_XTc", "b_T1"))
        b_XT = [put(f"b_XT{l}", [P, 4, P]) for l in range(2)]
        b_T = put("b_T", [DH, NT + 1, 2, DH])
        b_MT = put("b_MT", [DH, 8, DH])
        b_so = put("b_so", [DH, 2, DH])
        b_pc, b_mid, b_dm, b_dx = (put(n, [P, 8]) for n in ("b_pc", "b_mid", "b_dm", "b_dx"))
        b_D = put("b_D", [DH, 2, NT])
        b_gm, b_gv, b_gl, b_gr = (put(n, [P, 16]) for n in ("b_gm", "b_gv", "b_gl", "b_gr"))
        over = lambda buf, name, shape, off: nc.alloc_sbuf_tensor_at(name, shape, F32, offset=slots[buf] + off)
        b_AV = over("w_raw", "b_AV", [P, NT, 2, P], 0)
        LEVELS = (1, 2, 4, 8, 16, 32, 64)
        b_C = [over("w_hi", f"b_C{k}", [P, 8, P], 4096 * k) for k in range(2)]
        b_lev = {m: over("w_lo", f"b_lev{m}", [P, P], 512 * i) for i, m in enumerate(LEVELS)}
        b_bd32, b_bd64 = over("w_lo", "b_bd32", [P, P], 3584), over("w_lo", "b_bd64", [P, P], 4096)
        b_mask = over("w_lo", "b_mask", [P, L2], 4608)
        b_ic = over("w_lo", "b_ic", [P, 32], 5632)
        bd_tmp = {m: at("h", f"bd_tmp{m}", [P, P], 512 * i) for i, m in enumerate((2, 4, 8, 16))}
        bd_tmp[32], bd_tmp[64] = b_bd32, b_bd64
        bd_tmp[1], bd_tmp[128] = ident, ones
        rsam = dram("rsam", [4, D, NS])
        rk_in, rv_in, b_in_free, b_stored, b_turn = (sem(s) for s in ("rk_in", "rv_in", "b_in_free", "b_stored", "b_turn"))
        pe_names, act_names, dve_names, pool_names = "ss tV tA tB tK bon dcol".split(), "P iP Pm dx sq ln rs eV eA eB eK eD".split(), \
            "pc cs mid cc dm dl ccm kk0 ssm kkn b k1 kp A B K R rk bv".split(), []
        for h in range(2):
            two = lambda n: [f"{n}_{h}{l}" for l in range(2)]
            pe_names += two("s") + two("AV") + [x for m in LEVELS[1:6] for x in two(f"T{m}") + two(f"X{m}")]
            pe_names += two("Z") + two("CZ") + two("XZ") + two("G") + two("M")
            pe_names += [x for c in range(4 * h, 4 * h + 4) for x in (f"c{c}", f"y{c}")]
            act_names += two("av") + [x for m in LEVELS[1:5] for x in two(f"t{m}")] + two("zc") + two("cz") + two("gc")
            act_names += [f"yc{c}" for c in range(4 * h, 4 * h + 4)]
            dve_names += two("mak") + two("mab") + [f"xr_{h}{l}" for l in range(2)] + [f"{x}{m}_{h}{l}" for m in LEVELS[0:5] for l in range(2) for x in ("xa", "xt", "xb")]
            dve_names += two("t32") + [f"{x}_{h}{l}" for l in range(2) for x in ("xp", "xq")] + two("w") + two("mt")
            dve_names += [f"ch{c}" for c in range(4 * h, 4 * h + 4)]
            pool_names += [x for m in LEVELS for x in two(f"cm{m}")]
        pe_names += ["yt"]
        act_names += "gsq gln grs so".split()
        dve_names += "g1 g2 g3 g4 g5 o1 o2 o3".split()
        BP, BA, BV, BG = Steps(sem("b_pe"), pe_names), Steps(sem("b_act"), act_names), Steps(sem("b_dve"), dve_names), Steps(sem("b_pool"), pool_names)
        GM = Steps(sem("b_masks"), [f"bd{m}{x}" for m in (2, 4, 8, 16, 32, 64) for x in "ab"] + [f"lev{m}" for m in LEVELS] + "m0 m1".split())
        VM = Steps(sem("b_ic_done"), "0 1 2 3".split())

        def rwb_sync(sp):
            sp.wait_ge(BG_ready, 1 + START)
            with sp.Fori(0, PAIRS) as j:
                sp.wait_ge(b_in_free, j + START)
                for n in "rksa":
                    sp.dma_start(b_in[n][:, :], rw[bass.ds(j * P + RW[n], P), :]).then_inc(rk_in, 16)
                sp.wait_ge(BV.sem, j * len(BV.names) + START)
                for n in "vg":
                    sp.dma_start(b_in[n][:, :], rw[bass.ds(j * P + RW[n], P), :]).then_inc(rv_in, 16)

        BG_ready = sem("b_region_free")

        def rwb_gpsimd(pool):
            for u in range(2):
                pool.wait_ge(psum_free[u], plan["out1"][u] + START)
                pool.wait_ge(stored[u], 16 * 36 + START)
            pool.sem_inc(BG_ready, 1)
            for m in (2, 4, 8, 16, 32, 64):
                view = bd_tmp[m][:, :].rearrange("p (q i) -> p q i", i=m)
                GM.chain(pool, pool.affine_select(out=view, in_=ones[:, :].rearrange("p (q i) -> p q i", i=m), compare_op=ALU.is_ge, fill=0.0,
                                                  base=0, pattern=[[-m, P // m], [0, m]], channel_multiplier=1), f"bd{m}a")
                GM.chain(pool, pool.affine_select(out=view, in_=view, compare_op=ALU.is_ge, fill=0.0,
                                                  base=m - 1, pattern=[[m, P // m], [0, m]], channel_multiplier=-1), f"bd{m}b")
            for m in LEVELS:
                GM.chain(pool, nc.gpsimd.tensor_tensor(b_lev[m][:, :], bd_tmp[2 * m][:, :], bd_tmp[m][:, :], ALU.subtract), f"lev{m}")
            GM.chain(pool, pool.affine_select(out=b_mask[:, 0:P], in_=ones[:, :], compare_op=ALU.is_ge, fill=0.0,
                                              base=-1, pattern=[[1, P]], channel_multiplier=-1), "m0")
            GM.chain(pool, pool.affine_select(out=b_mask[:, P:L2], in_=ones[:, :], compare_op=ALU.is_ge, fill=0.0,
                                              base=0, pattern=[[1, P]], channel_multiplier=-1), "m1")
            with pool.Fori(0, PAIRS) as j:
                for h in range(2):
                    for i, m in enumerate(LEVELS):
                        for l in range(2):
                            if i < 2:
                                pool.wait_ge(BV.sem, BV.of(f"mab_{h}{l}", j) + START)
                            if i == 2:
                                pool.wait_ge(BV.sem, BV.of(f"xr_{h}{l}", j) + START)
                            elif i > 2:
                                pool.wait_ge(BP.sem, BP.of(f"T{LEVELS[i - 2]}_{h}{l}", j) + START)
                            elif i < 2 and h:
                                pool.wait_ge(BP.sem, (BP.of(f"{'T32' if i else 'CZ'}_0{l}", j)) + START)
                            pool.sem_inc(b_turn_pool, 1)
                            nc.gpsimd.tensor_tensor(b_C[i % 2][:, 4 * l:4 * l + 4, :], b_ab[l][:, :, 0:P],
                                                    b_lev[m][:, :].rearrange("p (o n) -> p o n", o=1).broadcast_to([P, 4, P]), ALU.mult).then_inc(BG.sem, 1)
            pool.wait_ge(BP.sem, PAIRS * len(BP.names) + START)

        b_turn_pool = sem("b_turn_pool")

        def rwb_tensor(pe):
            heads = lambda e: slice(DH * e, DH * e + DH)
            def done(mm):
                mm.then_inc(BP.sem, 1)

            def body(j):
                v = lambda n: pe.wait_ge(BV.sem, BV.of(n, j) + START)
                a = lambda n: pe.wait_ge(BA.sem, BA.of(n, j) + START)
                g = lambda n: pe.wait_ge(BG.sem, BG.of(n, j) + START)

                def go():
                    pe.sem_inc(b_turn, 1)
                a("sq")
                go()
                for c in range(NCH):
                    mm = nc.tensor.matmul(PS[:, c, 0:CH], b_bd64[:, :], b_b[:, CH * c:CH * c + CH], start=True, stop=True)
                done(mm)

                def turn(src, bank):
                    go()
                    for c in range(NT):
                        mm = nc.tensor.transpose(PS[:, bank + c // 4, P * (c % 4):P * (c % 4) + P], src(c), ident[:, :])
                    done(mm)
                pe.wait_ge(rv_in, j * 32 + 32 + START)
                turn(lambda c: b_in["v"][:, P * c:P * c + P], 6)
                v("A")
                turn(lambda c: b_AR[:, c, 0:P], 0)
                v("B")
                a("eV")
                turn(lambda c: b_B[:, P * c:P * c + P], 6)
                v("K")
                a("eA")
                turn(lambda c: b_K[:, P * c:P * c + P], 0)
                v("rk")
                go()
                for c in range(NCH):
                    mm = nc.tensor.matmul(PS[:, 3 + c, 0:CH], b_bd64[:, :], b_cs[:, CH * c:CH * c + CH], start=True, stop=True)
                done(mm)
                for e in range(2):
                    mm = nc.tensor.matmul(PS[0:DH, 2, NT * e:NT * e + NT], ident[:, heads(e)], b_dx[:, :], start=True, stop=True)
                done(mm)
                a("eD")
                v("bv")
                for h in range(2):
                    us = lambda l: [(u, 4 * h + 2 * l + u % 2, u // 2) for u in range(4)]
                    for l in range(2):
                        if h:
                            v("ch3")
                            a("yc3")
                        go()
                        for u, c, e in us(l):
                            for x, (lhs, bank) in enumerate(((b_B, 4 * l), (b_K, 4 * l + 2))):
                                mm = nc.tensor.matmul(PS[:, bank + u // 2, L2 * (u % 2):L2 * (u % 2) + L2], lhs[heads(e), P * c:P * c + P],
                                                      b_AR[heads(e), c, :], start=True, stop=True)
                        done(mm)
                    for l in range(2):
                        v(f"mak_{h}{l}")
                        go()
                        for u, c, e in us(l):
                            mm = nc.tensor.matmul(PS[:, 4 * l + 2, DH * u:DH * u + DH], b_ak[l][:, u, 0:P], tm["V"][:, c, heads(e)], start=True, stop=True)
                        done(mm)
                    small = lambda l, bank, u: PS[:, 4 * l + bank, 32 * u:32 * u + 32]
                    for i, m in enumerate(LEVELS[1:6], 1):
                        for l in range(2):
                            g(f"cm{m}_{h}{l}")
                            v(f"xb{m // 2}_{h}{l}")
                            go()
                            for u in range(4):
                                mm = nc.tensor.matmul(small(l, 0, u), b_C[i % 2][:, 4 * l + u, :], b_X[l][:, u, :], start=True, stop=True)
                            done(mm)
                        for l in range(2):
                            if m < 32:
                                a(f"t{m}_{h}{l}")
                            else:
                                v(f"t32_{h}{l}")
                            go()
                            for u in range(4):
                                lhs, rhs = (b_XT[l][:, u, :], b_T1[l][:, u, :]) if m < 32 else (b_Z[:, 4 * l + u, :], b_XTc[l][:, u, :])
                                mm = nc.tensor.matmul(small(l, 1, u), lhs, rhs, start=True, stop=True)
                            done(mm)
                    full = lambda l, bank, u: PS[:, 4 * l + bank, P * u:P * u + P]
                    for l in range(2):
                        v(f"xq_{h}{l}")
                        a(f"av_{h}{l}")
                        go()
                        for u, c, e in us(l):
                            mm = nc.tensor.matmul(full(l, 3, u), b_XT[l][:, u, :], b_AV[:, c, e, :], start=True, stop=True)
                        done(mm)
                    for l in range(2):
                        g(f"cm64_{h}{l}")
                        a(f"zc_{h}{l}")
                        go()
                        for u in range(4):
                            mm = nc.tensor.matmul(full(l, 0, u), b_C[0][:, 4 * l + u, :], b_Z[:, 4 * l + u, :], start=True, stop=True)
                        done(mm)
                    for l in range(2):
                        a(f"cz_{h}{l}")
                        go()
                        for u in range(4):
                            mm = nc.tensor.matmul(full(l, 1, u), b_XT[l][:, u, :], b_CZ[:, 4 * l + u, :], start=True, stop=True)
                        done(mm)
                    for l in range(2):
                        v(f"w_{h}{l}")
                        go()
                        for u, c, e in us(l):
                            out = PS[0:DH, 4 * l + 2, P * u:P * u + P]
                            nc.tensor.matmul(out, b_W[:, 4 * l + u, 0:DH], b_ab[l][:, u, P:L2], start=True, stop=False)
                            mm = nc.tensor.matmul(out, ident[:, heads(e)], b_AR[:, c, P:L2], start=False, stop=True)
                        done(mm)
                    for l in range(2):
                        go()
                        for u, c, e in us(l):
                            mm = nc.tensor.matmul(PS[0:DH, 4 * l + 3, DH * u:DH * u + DH], b_W[:, 4 * l + u, 0:DH], tm["B"][:, c, heads(e)], start=True, stop=True)
                        done(mm)
                    for c in range(4 * h, 4 * h + 4):
                        l = (c % 4) // 2
                        at_ = lambda bank, p, e: PS[0:p, 4 * l + bank + 2 * (c % 2), DH * e:DH * e + DH]
                        v(f"ch{c - 1}" if c % 4 else f"mt_{h}1")
                        go()
                        for e in range(2):
                            u = 2 * e + c % 2
                            nc.tensor.matmul(at_(0, DH, e), tm["B"][:, c, heads(e)], b_W[:, 4 * l + u, DH:P], start=True, stop=False)
                            mm = nc.tensor.matmul(at_(0, DH, e), tm["K"][:, c, heads(e)], tm["V"][:, c, heads(e)], start=False, stop=(c == 0))
                            if c:
                                mm = nc.tensor.matmul(at_(0, DH, e), b_MT[:, 4 * l + u, :], b_T[:, c, e, :], start=False, stop=True)
                        done(mm)
                        a(f"gc_{h}{l}")
                        go()
                        for e in range(2):
                            u = 2 * e + c % 2
                            nc.tensor.matmul(at_(1, P, e), b_ab[l][:, u, P:L2], b_W[:, 4 * l + u, DH:P], start=True, stop=False)
                            mm = nc.tensor.matmul(at_(1, P, e), b_ak[l][:, u, P:L2], tm["V"][:, c, heads(e)], start=False, stop=(c == 0))
                            if c:
                                mm = nc.tensor.matmul(at_(1, P, e), b_GT[:, 4 * l + u, :], b_T[:, c, e, :], start=False, stop=True)
                        done(mm)
                v("g5")
                go()
                for c in range(NT):
                    nc.tensor.transpose(PS[:, c // 4, P * (c % 4):P * (c % 4) + P], b_y[:, c, :], ident[:, :])
                for e in range(2):
                    mm = nc.tensor.transpose(PS[0:DH, 2, DH * e:DH * e + DH], b_T[:, NT, e, :], ident[0:DH, 0:DH])
                done(mm)
            with pe.Fori(0, PAIRS) as j:
                body(j)

        def rwb_scalar(act):
            def body(j):
                v = lambda n: act.wait_ge(BV.sem, BV.of(n, j) + START)
                p = lambda n: act.wait_ge(BP.sem, BP.of(n, j) + START)
                done = lambda ins: ins.then_inc(BA.sem, 1)
                own = lambda n: act.wait_ge(BA.sem, BA.of(n, j) + START)
                v("cc")
                done(nc.scalar.activation(b_P[:, 0:TP], b_cs[:, 0:TP], ACT.Exp, scale=-C0))
                done(nc.scalar.activation(b_iP[:, 0:TP], b_cs[:, 0:TP], ACT.Exp, scale=C0))
                v("ccm")
                done(nc.scalar.activation(b_Pm[:, 0:TP], b_Pm[:, 0:TP], ACT.Exp, scale=-C0))
                done(nc.scalar.activation(b_dx[:, :], b_dm[:, :], ACT.Exp, scale=-C0))
                v("kk0")
                act.wait_ge(b_stored, j * (16 * 6) + START)
                done(nc.scalar.activation(b_b[:, :], b_kkn[:, :], ACT.Square))
                v("ssm")
                done(nc.scalar.activation(b_b[:, :], b_b[:, :], ACT.Ln, scale=2.0 ** 20))
                own("ln")
                done(nc.scalar.activation(b_b[:, :], b_b[:, :], ACT.Exp, scale=-0.5, bias=SHIFT_C))
                for n, bank in (("V", 6), ("A", 0), ("B", 6), ("K", 0)):
                    p(f"t{n}")
                    if n == "A":
                        done(nc.scalar.copy(b_AV[:, :, :, 0:DH], PS[:, 0:2, :].rearrange("p b (c e n) -> p (b c) e n", e=2, n=DH)))
                        continue
                    done(nc.scalar.copy(tm[n][:, :, :].rearrange("p (b c) n -> p b (c n)", b=2), PS[:, bank:bank + 2, :]))
                p("dcol")
                done(nc.scalar.copy(b_D[:, :, :].rearrange("p e c -> p (e c)"), PS[0:DH, 2, 0:2 * NT]))
                v("bv")
                for i, src in enumerate((b_kp, b_kkn, b_b, b_bv)):
                    act.dma_start(rsam[i, bass.ds(j * P, P), :], src[:, TP:T]).then_inc(b_stored, 16)
                for h in range(2):
                    flat = lambda ap: ap.rearrange("p u n -> p (u n)")
                    for l in range(2):
                        p(f"AV_{h}{l}")
                        c = 4 * h + 2 * l
                        done(nc.scalar.copy(b_AV[:, c:c + 2, :, DH:P].rearrange("p c e n -> p e c n"),
                                            PS[:, 4 * l + 2, 0:4 * DH].rearrange("p (e c n) -> p e c n", e=2, n=DH)))
                    for m in LEVELS[1:5]:
                        for l in range(2):
                            p(f"T{m}_{h}{l}")
                            done(nc.scalar.copy(flat(b_T1[l][:, :, :]), PS[:, 4 * l, 0:P]))
                    for l in range(2):
                        p(f"Z_{h}{l}")
                        done(nc.scalar.copy(flat(b_Z[:, 4 * l:4 * l + 4, :]), PS[:, 4 * l + 3, :]))
                    for l in range(2):
                        p(f"CZ_{h}{l}")
                        done(nc.scalar.copy(flat(b_CZ[:, 4 * l:4 * l + 4, :]), PS[:, 4 * l, :]))
                    for l in range(2):
                        p(f"G_{h}{l}")
                        done(nc.scalar.copy(flat(b_GT[:, 4 * l:4 * l + 4, :]), PS[0:DH, 4 * l + 2, :]))
                    for c in range(4 * h, 4 * h + 4):
                        l = (c % 4) // 2
                        p(f"y{c}")
                        done(nc.scalar.copy(b_y[:, c, :], PS[:, 4 * l + 1 + 2 * (c % 2), 0:P]))
                v("g3")
                done(nc.scalar.activation(b_ysq[:, :, :], b_y[:, :, :], ACT.Square))
                v("g4")
                done(nc.scalar.activation(b_gl[:, :], b_gv[:, :], ACT.Ln, scale=1.0 / DH, bias=GN_C))
                own("gln")
                done(nc.scalar.activation(b_gr[:, :], b_gl[:, :], ACT.Exp, scale=-0.5))
                p("yt")
                done(nc.scalar.copy(b_so[:, :, :].rearrange("p e n -> p (e n)"), PS[0:DH, 2, 0:P]))
                own("so")
                act.dma_start(io["p_rwkv_s"][0, 0, bass.ds(2 * j, 2)].rearrange("e v k -> v e k"), b_so[:, :, :]).then_inc(b_stored, 16)
                v("o3")
                act.dma_start(mix2[bass.ds(j * P, P), 0:TP], b_kp[:, 0:TP]).then_inc(b_stored, 16)
            with act.Fori(0, PAIRS) as j:
                body(j)

        def rwb_vector(dve):
            tt, ts, stt = nc.vector.tensor_tensor, nc.vector.tensor_scalar, nc.vector.scalar_tensor_tensor
            dve.wait_ge(BG_ready, 1 + START)
            for i in range(4):
                VM.chain(dve, nc.vector.tensor_copy(b_ic[32 * i:32 * i + 32, :], ident[32 * i:32 * i + 32, 32 * i:32 * i + 32]), str(i))
            dve.wait_ge(GM.sem, len(GM.names) + START)
            by = lambda ap: ap.rearrange("p (c n) -> p c n", c=NT)
            spread = lambda ap, n: ap.rearrange("p (o n) -> p o n", o=1).broadcast_to([P, n, ap.shape[1]])

            def body(j):
                def done(ins, name):
                    BV.chain(dve, ins, name, j)
                p = lambda n: dve.wait_ge(BP.sem, BP.of(n, j) + START)
                a = lambda n: dve.wait_ge(BA.sem, BA.of(n, j) + START)
                col = lambda i: b_pc[:, i:i + 1]
                r, k, s, aa, vv, gg = (b_in[n] for n in "rksavg")
                pars = vecs[:, VEC["rwkv_k_k"]:VEC["rwkv_k_k"] + 40].rearrange("p (n k) -> p n k", k=KT)
                done(nc.vector.tensor_copy(b_pc[:, 0:5].rearrange("p (n o) -> p n o", o=1), pars[:, :, bass.ds(j, 1)]), "pc")
                dve.wait_ge(rk_in, j * 64 + 64 + START)
                dve.sem_inc(b_turn_dve, 1)
                for c in range(NT):
                    x = slice(P * c, P * c + P)
                    ins = nc.vector.tensor_tensor_scan(b_cs[:, x], ones[:, :], s[:, x], 0.0, ALU.mult, ALU.add)
                done(ins, "cs")
                done(ts(b_mid[:, :].rearrange("p (c o) -> p c o", o=1), by(b_cs[:, 0:TP])[:, :, P - 1:P], 0.5, None, ALU.mult), "mid")
                done(tt(by(b_cs[:, 0:TP]), by(b_cs[:, 0:TP]), b_mid[:, :].rearrange("p (c o) -> p c o", o=1).broadcast_to([P, NT, P]), ALU.subtract), "cc")
                done(tt(b_dm[:, 0:NT - 1], b_mid[:, 0:NT - 1], b_mid[:, 1:NT], ALU.add), "dm")
                done(nc.vector.tensor_copy(b_dm[:, NT - 1:NT], b_mid[:, NT - 1:NT]), "dl")
                done(tt(b_Pm[:, 0:TP], b_cs[:, 0:TP], s[:, 0:TP], ALU.subtract), "ccm")
                dve.wait_ge(b_stored, j * (16 * 6) + START)
                dve.sem_inc(b_turn_dve, 1)
                done(ts(b_kkn[:, :], k[:, :], col(0), None, ALU.mult), "kk0")
                p("ss")
                done(ts(chunks(b_b[:, :]), banks(0), 1e-24, None, ALU.max), "ssm")
                a("rs")
                done(tt(b_kkn[:, :], b_kkn[:, :], b_b[:, :], ALU.mult), "kkn")
                done(tt(b_b[:, :], b_kkn[:, :], aa[:, :], ALU.mult), "b")
                done(ts(b_kp[:, :], aa[:, :], 1.0, col(1), ALU.subtract, ALU.mult), "k1")
                done(stt(b_kp[:, :], b_kp[:, :], 1.0, k[:, :], ALU.add, ALU.mult), "kp")
                done(stt(b_AR[:, :, 0:P], by(b_kkn[:, 0:TP]), -1.0, by(b_Pm[:, 0:TP]), ALU.mult, ALU.mult), "A")
                done(tt(b_B[:, :], b_b[:, 0:TP], b_iP[:, 0:TP], ALU.mult), "B")
                done(tt(b_K[:, :], b_kp[:, 0:TP], b_iP[:, 0:TP], ALU.mult), "K")
                done(tt(b_AR[:, :, P:L2], by(r[:, 0:TP]), by(b_P[:, 0:TP]), ALU.mult), "R")
                done(stt(b_cs[:, :], r[:, :], col(2), b_kp[:, :], ALU.mult, ALU.mult), "rk")
                dve.sem_inc(b_in_free, 1)
                p("bon")
                done(tt(chunks(b_bv[:, :]), banks(1), chunks(vv[:, :]), ALU.mult), "bv")
                for h in range(2):
                    two = lambda l, bank: PS[:, 4 * l + bank:4 * l + bank + 2, :].rearrange("p b (u n) -> p (b u) n", u=2)
                    for dst, bank, name in ((b_ak, 2, "mak"), (b_ab, 0, "mab")):
                        for l in range(2):
                            p(f"s_{h}{l}")
                            done(tt(dst[l][:, :, :], two(l, bank), spread(b_mask[:, :], 4), ALU.mult), f"{name}_{h}{l}")
                    small = lambda l, bank: PS[:, 4 * l + bank, 0:P].rearrange("p (u n) -> p u n", u=4)
                    blocks = lambda ap: ap.rearrange("p u (o n) -> p u o n", o=1).broadcast_to([P, 4, 4, 32])
                    wide = lambda ap: ap.rearrange("p u (q n) -> p u q n", q=4)
                    bmask = lambda m: m[:, :].rearrange("p (o q n) -> p o q n", o=1, q=4).broadcast_to([P, 4, 4, 32])

                    def widen(dst, src, mask, name):
                        done(tt(wide(dst), blocks(src), bmask(mask), ALU.mult), name)
                    for l in range(2):
                        dve.wait_ge(BG.sem, BG.of(f"cm1_{h}{l}", j) + START)
                        dve.sem_inc(b_turn_dve, 1)
                        done(nc.vector.tensor_reduce(b_XTc[l][:, :, :], b_C[0][:, 4 * l:4 * l + 4, :].rearrange("p u (q n) -> p u n q", q=4), AX.X, ALU.add), f"xr_{h}{l}")
                    flat = lambda ap: ap.rearrange("p u n -> p (u n)")
                    for m in LEVELS[0:5]:
                        for l in range(2):
                            if m == 1:
                                done(tt(b_XTc[l][:, :, :], b_XTc[l][:, :, :], spread(b_ic[:, :], 4), ALU.add), f"xa1_{h}{l}")
                                done(nc.vector.transpose(flat(b_X[l][:, :, :]), flat(b_XTc[l][:, :, :])), f"xt1_{h}{l}")
                            else:
                                p(f"X{m}_{h}{l}")
                                done(tt(b_X[l][:, :, :], small(l, 1), b_X[l][:, :, :], ALU.add), f"xa{m}_{h}{l}")
                                done(nc.vector.transpose(flat(b_XTc[l][:, :, :]), flat(b_X[l][:, :, :])), f"xt{m}_{h}{l}")
                            widen(b_XT[l][:, :, :], b_XTc[l][:, :, :], b_bd32, f"xb{m}_{h}{l}")
                    for l in range(2):
                        p(f"T32_{h}{l}")
                        widen(b_Z[:, 4 * l:4 * l + 4, :], small(l, 0), b_lev[32], f"t32_{h}{l}")
                    for l in range(2):
                        p(f"X32_{h}{l}")
                        widen(b_Z[:, 4 * l:4 * l + 4, :], small(l, 1), b_lev[32], f"xp_{h}{l}")
                        done(tt(b_XT[l][:, :, :], b_XT[l][:, :, :], b_Z[:, 4 * l:4 * l + 4, :], ALU.add), f"xq_{h}{l}")
                    for l in range(2):
                        p(f"XZ_{h}{l}")
                        done(tt(b_W[:, 4 * l:4 * l + 4, :], b_Z[:, 4 * l:4 * l + 4, :], PS[:, 4 * l + 1, :].rearrange("p (u n) -> p u n", u=4), ALU.add), f"w_{h}{l}")
                    for l in range(2):
                        p(f"M_{h}{l}")
                        done(tt(b_MT[:, 4 * l:4 * l + 4, :], PS[0:DH, 4 * l + 3, 0:4 * DH].rearrange("p (u n) -> p u n", u=4),
                                ident[0:DH, 0:DH].rearrange("p (o n) -> p o n", o=1).broadcast_to([DH, 4, DH]), ALU.add), f"mt_{h}{l}")
                    for c in range(4 * h, 4 * h + 4):
                        l = (c % 4) // 2
                        p(f"c{c}")
                        done(tt(b_T[:, c + 1, :, :], PS[0:DH, 4 * l + 2 * (c % 2), 0:P].rearrange("p (e n) -> p e n", e=2),
                                b_D[:, :, c:c + 1].broadcast_to([DH, 2, DH]), ALU.mult), f"ch{c}")
                groups = lambda ap: ap.rearrange("p c (e n) -> p (c e) n", e=2)
                each = lambda ap: ap.rearrange("p (g o) -> p g o", o=1).broadcast_to([P, 16, DH])
                a("yc7")
                done(nc.vector.tensor_reduce(b_gm[:, :], groups(b_y[:, :, :]), AX.X, ALU.add), "g1")
                done(ts(b_gm[:, :], b_gm[:, :], 1.0 / DH, None, ALU.mult), "g2")
                done(tt(groups(b_y[:, :, :]), groups(b_y[:, :, :]), each(b_gm[:, :]), ALU.subtract), "g3")
                a("gsq")
                done(nc.vector.tensor_reduce(b_gv[:, :], groups(b_ysq[:, :, :]), AX.X, ALU.add), "g4")
                a("grs")
                done(tt(groups(b_y[:, :, :]), groups(b_y[:, :, :]), each(b_gr[:, :]), ALU.mult), "g5")
                p("yt")
                yo = b_kp[:, 0:TP]
                done(ts(yo.rearrange("p (b n) -> p b n", b=2), PS[:, 0:2, :], col(3), col(4), ALU.mult, ALU.add), "o1")
                done(tt(yo, yo, b_bv[:, 0:TP], ALU.add), "o2")
                done(tt(yo, yo, gg[:, 0:TP], ALU.mult), "o3")
            with dve.Fori(0, PAIRS) as j:
                body(j)

        b_turn_dve = sem("b_turn_dve")

        QN = "srvgpkbe"
        HD = RH * NS
        put = packer("h")
        e_S, e_t = put("e_S", [HD, DH, DH]), put("e_t", [HD, DH, DH])
        put = packer("hl")
        e_fm = put("e_fm", [P, 8, KT, NS])
        e_tm = put("e_tm", [NS, 8, D])
        e_rows = {n: put(f"e_{n}", [HD, DH]) for n in QN}
        e_w, e_sa, e_y, e_sq, e_lnw, e_lnb = (put(n, [HD, DH]) for n in ("e_w", "e_sa", "e_y", "e_sq", "e_lnw", "e_lnb"))
        e_mu, e_var, e_ln, e_rs = (put(n, [HD, 1]) for n in ("e_mu", "e_var", "e_ln", "e_rs"))
        e_yT = put("e_yT", [DH, RH, NS])
        e_fm_in, e_S_in, e_par_in, e_rows_in, e_out = (sem(s) for s in ("e_fm_in", "e_S_in", "e_par_in", "e_rows_in", "e_out"))
        QT = Steps(sem("e_pe"), "t0 t1 yt".split())
        QA = Steps(sem("e_act"), "k0 k1 w sq ln rs yk".split())
        QV = Steps(sem("e_dve"), "ta sa sw sb s1 vk s2 tr y mu1 mu2 yc yw yb ye yg".split())

        def rwd_sync(sp):
            sp.wait_ge(b_stored, 16 * 6 * PAIRS + START)
            sp.wait_ge(BV.sem, PAIRS * len(BV.names) + START)
            tile = lambda ap: ap.rearrange("(k p) t -> p k t", p=P)
            for i, n in enumerate(QN[0:4]):
                sp.dma_start(e_fm[:, i, :, :], tile(rw[RW[n]:RW[n] + D, TP:T])).then_inc(e_fm_in, 16)
            for i in range(4):
                sp.dma_start(e_fm[:, 4 + i, :, :], tile(rsam[i])).then_inc(e_fm_in, 16)
            sp.dma_start(e_S[:, :, :], io["state_rwkv_s"][0].rearrange("b h v k -> (b h) v k")).then_inc(e_S_in, 16)
            for dst, name in ((e_lnw, "rwkv_ln_w"), (e_lnb, "rwkv_ln_b")):
                for b in range(NS):
                    sp.dma_start(dst[RH * b:RH * b + RH, :], io[name].rearrange("o (h d) -> (o h) d", d=DH)).then_inc(e_par_in, 16)
            for r in range(2):
                sp.wait_ge(QA.sem, QA[f"k{r}"] + START)
                for i, n in enumerate(QN[4 * r:4 * r + 4]):
                    sp.dma_start(e_rows[n][:, :], e_tm[:, 4 * r + i, :]).then_inc(e_rows_in, 16)
            sp.wait_ge(QV.sem, QV["s2"] + START)
            sp.dma_start(io["s_rwkv_s"][0].rearrange("b h v k -> (b h) v k"), e_S[:, :, :]).then_inc(e_out, 16)
            sp.wait_ge(QA.sem, QA["yk"] + START)
            sp.dma_start(mix2[:, TP:T].rearrange("(h d) t -> d h t", d=DH), e_yT[:, :, :]).then_inc(e_out, 16)
            sp.wait_ge(e_out, 32 + START)

        def rwd_tensor(pe):
            for r in range(2):
                if r:
                    pe.wait_ge(QA.sem, QA["k0"] + START)
                pe.wait_ge(e_fm_in, 16 * 8 + START)
                for i in range(4 * KT):
                    mm = nc.tensor.transpose(PS[0:NS, i // 4, P * (i % 4):P * (i % 4) + P], e_fm[:, 4 * r + i // KT, i % KT, :], ident[:, :])
                mm.then_inc(QT.sem, 1)
            pe.wait_ge(QV.sem, QV["yg"] + START)
            pe.wait_ge(QA.sem, QA["k1"] + START)
            nc.tensor.transpose(PS[0:DH, 0, 0:HD], e_y[:, :], ident[:, :]).then_inc(QT.sem, 1)

        def rwd_scalar(act):
            for r in range(2):
                act.wait_ge(QT.sem, QT[f"t{r}"] + START)
                QA.chain(act, nc.scalar.copy(e_tm[:, 4 * r:4 * r + 4, :].rearrange("p i n -> p (i n)"), PS[0:NS, :, :].rearrange("p b n -> p (b n)")), f"k{r}")
            act.wait_ge(e_rows_in, 16 * 8 + START)
            QA.chain(act, nc.scalar.activation(e_w[:, :], e_rows["s"][:, :], ACT.Exp, scale=-C0), "w")
            act.wait_ge(QV.sem, QV["yc"] + START)
            QA.chain(act, nc.scalar.activation(e_sq[:, :], e_y[:, :], ACT.Square, accum_out=e_var[:, :]), "sq")
            QA.chain(act, nc.scalar.activation(e_ln[:, :], e_var[:, :], ACT.Ln, scale=1.0 / DH, bias=GN_C), "ln")
            QA.chain(act, nc.scalar.activation(e_rs[:, :], e_ln[:, :], ACT.Exp, scale=-0.5), "rs")
            act.wait_ge(QT.sem, QT["yt"] + START)
            QA.chain(act, nc.scalar.copy(e_yT[:, :, :], PS[0:DH, 0, 0:HD].rearrange("p (b h) -> p h b", b=NS)), "yk")

        def rwd_vector(dve):
            tt, ts, stt = nc.vector.tensor_tensor, nc.vector.tensor_scalar, nc.vector.scalar_tensor_tensor
            c = lambda ins, name: QV.chain(dve, ins, name)
            by_k = lambda ap: ap[:, :].rearrange("p (o k) -> p o k", o=1).broadcast_to([HD, DH, DH])
            by_v = lambda ap: ap[:, :].rearrange("p (v o) -> p v o", o=1).broadcast_to([HD, DH, DH])
            R = e_rows
            S, t = e_S[:, :, :], e_t[:, :, :]
            dve.wait_ge(e_S_in, 16 + START)
            dve.wait_ge(e_rows_in, 16 * 8 + START)
            c(tt(t, S, by_k(R["k"]), ALU.mult), "ta")
            c(nc.vector.tensor_reduce(e_sa[:, :], t, AX.X, ALU.add), "sa")
            dve.wait_ge(QA.sem, QA["w"] + START)
            c(tt(S, S, by_k(e_w), ALU.mult), "sw")
            c(tt(t, by_v(e_sa), by_k(R["b"]), ALU.mult), "sb")
            c(tt(S, S, t, ALU.subtract), "s1")
            c(tt(t, by_v(R["v"]), by_k(R["p"]), ALU.mult), "vk")
            c(tt(S, S, t, ALU.add), "s2")
            c(tt(t, S, by_k(R["r"]), ALU.mult), "tr")
            c(nc.vector.tensor_reduce(e_y[:, :], t, AX.X, ALU.add), "y")
            c(nc.vector.tensor_reduce(e_mu[:, :], e_y[:, :], AX.X, ALU.add), "mu1")
            c(ts(e_mu[:, :], e_mu[:, :], 1.0 / DH, None, ALU.mult), "mu2")
            c(ts(e_y[:, :], e_y[:, :], e_mu[:, :], None, ALU.subtract), "yc")
            dve.wait_ge(QA.sem, QA["sq"] + START)
            dve.wait_ge(e_par_in, 16 * 2 * NS + START)
            c(tt(e_y[:, :], e_y[:, :], e_lnw[:, :], ALU.mult), "yw")
            dve.wait_ge(QA.sem, QA["rs"] + START)
            c(stt(e_y[:, :], e_y[:, :], e_rs[:, :], e_lnb[:, :], ALU.mult, ALU.add), "yb")
            c(tt(e_y[:, :], e_y[:, :], R["e"][:, :], ALU.add), "ye")
            c(tt(e_y[:, :], e_y[:, :], R["g"][:, :], ALU.mult), "yg")

        y_out = at("h", "y_out", [P, NT, D], 0)
        ys_out = at("s", "ys_out", [NS, D], 0)
        y_full, y_free = [sem("y_full0"), sem("y_full1")], [sem("y_free0"), sem("y_free1")]
        y_stored = sem("y_stored")

        def y_tensor(pe):
            pe.wait_ge(x_ready, 4 * KT + START)
            for t in range(NT + 1):
                for half in range(2):
                    if t >= 1:
                        pe.wait_ge(y_free[half], t + START)
                    n = P if t < NT else NS
                    for k in range(4):
                        mm = nc.tensor.transpose(PS[0:n, half, P * k:P * k + P], xT[:, 4 * half + k, P * t:P * t + n], ident[:, :])
                    mm.then_inc(y_full[half], 1)

        def y_copy(eng, half, copy):
            eng.wait_ge(x_ready, 4 * KT + START)
            for t in range(NT + 1):
                eng.wait_ge(y_full[half], t + 1 + START)
                if t < NT:
                    copy(y_out[:, t, 512 * half:512 * half + 512], PS[:, half, :]).then_inc(y_free[half], 1)
                else:
                    copy(ys_out[:, 512 * half:512 * half + 512], PS[0:NS, half, :]).then_inc(y_free[half], 1)

        def y_sync(sp):
            for t in range(NT + 1):
                for half in range(2):
                    sp.wait_ge(y_free[half], t + 1 + START)
                if t < NT:
                    sp.dma_start(io["y_prompt"][0, P * t:P * t + P, :], y_out[:, t, :]).then_inc(y_stored, 16)
                else:
                    sp.dma_start(io["y_sample"][:, 0, :], ys_out[:, :]).then_inc(y_stored, 16)
            sp.wait_ge(y_stored, 16 * (NT + 1) + START)
            sp.wait_ge(sh_stored, 32 + START)

        block = ctx.enter_context(nc.Block())



        x_sem = lambda eng: [eng.wait_ge(s, (NT + (1 if i == 0 else 0)) + START) for i, s in enumerate(xt_free)]

        @block.sync
        def _(sp):
            start(sp, 0)
            load_x_sync(sp)
            gates_sync(sp)
            load_pairs(sp, "in_a", 4, w_in)
            load_pairs(sp, "in_o", 2, w_in, c0=1024)
            load_pairs(sp, "in_b", 6, w_in, c0=C_FQ)
            gates_out_sync(sp)
            mlstm_sync(sp)
            fox_sync(sp)
            dec0_sync(sp)
            dec0_end(sp)
            mix_sync(sp, 0, mix)
            load_pairs(sp, "out0", 4, w_out)
            ffn_sync(sp, 0)
            shift_sync(sp)
            mixes_sync(sp)
            rwb_sync(sp)
            rwd_sync(sp)
            mix_sync(sp, 1, mix2)
            load_pairs(sp, "out1", 4, kt_of("rwkv_w_o"))
            ffn_sync(sp, 1)
            y_sync(sp)

        @block.gpsimd
        def _(pool):
            start(pool, 1)
            setup_gpsimd(pool)
            gates_gpsimd(pool)
            split_pairs(pool, "in_a", 4, KT)
            split_pairs(pool, "in_o", 2, KT)
            split_pairs(pool, "in_b", 6, KT)
            mlstm_gpsimd(pool)
            fox_gpsimd(pool)
            dec0_gpsimd(pool)
            split_pairs(pool, "out0", 4, KT)
            ffn_gpsimd(pool, 0)
            mixes_gpsimd(pool)
            rwb_gpsimd(pool)
            split_pairs(pool, "out1", 4, KT)
            ffn_gpsimd(pool, 1)

        @block.tensor
        def _(pe):
            start(pe, 2)
            load_x_tensor(pe)
            stats_tensor(pe, 0)
            gates_tensor(pe, 0)
            gemm_tensor(pe, "in_a", 4, 0)
            gemm_tensor(pe, "in_o", 2, 0)
            gemm_tensor(pe, "in_b", 6, 0)
            gates_cols_tensor(pe)
            mlstm_tensor(pe)
            fox_tensor(pe)
            dec0_tensor(pe)
            gemm_tensor(pe, "out0", 4, 1)
            stats_tensor(pe, 1)
            stats_tensor(pe, 2)
            ffn_tensor(pe, 0, 2)
            stats_tensor(pe, 3)
            stats_tensor(pe, 4)
            shift_tensor(pe)
            mixes_tensor(pe)
            rwb_tensor(pe)
            rwd_tensor(pe)
            gemm_tensor(pe, "out1", 4, 9)
            stats_tensor(pe, 5)
            stats_tensor(pe, 6)
            ffn_tensor(pe, 1, 10)
            stats_tensor(pe, 7)
            y_tensor(pe)

        @block.scalar
        def _(act):
            start(act, 3)
            load_x_scalar(act)
            stats_scalar(act, 0, xT, x_sem)
            split_scalar(act, 0)
            gates_scalar(act)
            store_scalar(act, "in_a", 4, proj, 0, 0)
            store_scalar(act, "in_o", 2, proj, 1024, 4, func=ACT.Sigmoid)
            store_scalar(act, "in_b", 6, proj, 12 * P, 6)
            gates_exp_scalar(act)
            mlstm_scalar(act)
            fox_scalar(act)
            dec0_scalar(act)
            split_scalar(act, 1)
            keep_scalar(act, "out0")
            stats_scalar(act, 1, oT, after("ffn0"))
            stats_scalar(act, 2, xT, lambda eng: eng.wait_ge(x_ready, KT + START))
            split_scalar(act, 2)
            ffn_scalar(act, 0)
            stats_scalar(act, 3, oT, after("a_w"))
            stats_scalar(act, 4, xT, lambda eng: eng.wait_ge(x_ready, 2 * KT + START))
            shift_scalar(act)
            mixes_scalar(act)
            rwb_scalar(act)
            rwd_scalar(act)
            split_scalar(act, 9)
            keep_scalar(act, "out1")
            stats_scalar(act, 5, oT, after("ffn1"))
            stats_scalar(act, 6, xT, lambda eng: eng.wait_ge(x_ready, 3 * KT + START))
            split_scalar(act, 10)
            ffn_scalar(act, 1)
            stats_scalar(act, 7, oT, after("end"))
            y_copy(act, 0, nc.scalar.copy)

        @block.vector
        def _(dve):
            start(dve, 4)
            load_x_vector(dve)
            stats_vector(dve, 0)
            split_vector(dve, 0, normed(dve, 0))
            gates_vector(dve)
            gates_cols_vector(dve)
            mlstm_vector(dve)
            fox_vector(dve)
            dec0_vector(dve)
            mix_split_vector(dve, 1, 0)
            stats_vector(dve, 1)
            add_normed_vector(dve, 1, 0)
            stats_vector(dve, 2)
            split_vector(dve, 2, normed(dve, 2))
            ffn_vector(dve, 0, 2)
            stats_vector(dve, 3)
            add_normed_vector(dve, 3, 1)
            stats_vector(dve, 4)
            shift_vector(dve)
            mixes_vector(dve)
            rwb_vector(dve)
            rwd_vector(dve)
            mix_split_vector(dve, 9, 1)
            stats_vector(dve, 5)
            add_normed_vector(dve, 5, 2)
            stats_vector(dve, 6)
            split_vector(dve, 10, normed(dve, 6))
            ffn_vector(dve, 1, 10)
            stats_vector(dve, 7)
            add_normed_vector(dve, 7, 3)
            y_copy(dve, 1, nc.vector.tensor_copy)


_INS = ['x_prompt', 'x_sample', 'cache_fox_k', 'cache_fox_v', 'cache_fox_lf', 'state_mlstm_c', 'state_mlstm_n',
    'state_mlstm_m', 'state_rwkv_s', 'state_rwkv_shift', 'page_table', 'norm_g', 'hyb_w_in', 'mlstm_i_bias',
    'mlstm_f_bias', 'mlstm_out_g', 'fox_f_bias', 'hyb_w_out', 'rwkv_mix', 'rwkv_w_r', 'rwkv_w_k', 'rwkv_w_v',
    'rwkv_w_o', 'rwkv_w0', 'rwkv_w1', 'rwkv_w2', 'rwkv_a0', 'rwkv_a1', 'rwkv_a2', 'rwkv_g1', 'rwkv_g2',
    'rwkv_k_k', 'rwkv_k_a', 'rwkv_r_k', 'rwkv_ln_w', 'rwkv_ln_b', 'ffn_w_gate', 'ffn_w_up', 'ffn_w_down']
_OUTS = [('y_prompt', (1, 1024, 1024)), ('y_sample', (8, 1, 1024)), ('p_fox_k', (1, 1, 1024, 8, 64)),
    ('p_fox_v', (1, 1, 1024, 8, 64)), ('p_fox_lf', (1, 1, 1024, 8)), ('p_mlstm_c', (1, 1, 4, 64, 128)),
    ('p_mlstm_n', (1, 1, 4, 64)), ('p_mlstm_m', (1, 1, 4)), ('p_rwkv_s', (1, 1, 16, 64, 64)),
    ('p_rwkv_shift', (1, 1, 1024)), ('s_fox_k', (1, 8, 1, 8, 64)), ('s_fox_v', (1, 8, 1, 8, 64)),
    ('s_fox_lf', (1, 8, 1, 8)), ('s_mlstm_c', (1, 8, 4, 64, 128)), ('s_mlstm_n', (1, 8, 4, 64)),
    ('s_mlstm_m', (1, 8, 4)), ('s_rwkv_s', (1, 8, 16, 64, 64)), ('s_rwkv_shift', (1, 8, 1024))]


def kernel(**inputs):
    import numpy as _np
    import concourse.bacc as _bacc
    from concourse import mybir as _mybir
    from concourse.bass_utils import run_bass_kernel_spmd as _run

    nc = _bacc.Bacc("TRN2", target_bir_lowering=False, num_devices=1)
    arrays, io = {}, {}
    for name in _INS:
        a = _np.ascontiguousarray(inputs[name])
        arrays[f"in_{name}_dram"] = a
        io[name] = nc.dram_tensor(f"in_{name}_dram", a.shape, _mybir.dt.from_np(a.dtype), kind="ExternalInput").ap()
    for i, (name, shape) in enumerate(_OUTS):
        io[name] = nc.dram_tensor(f"out_{i}_dram", shape, _mybir.dt.float32, kind="ExternalOutput").ap()
    decoder_step(nc, io)
    r = _run(nc, [arrays], core_ids=[0])
    return tuple(r.results[0][f"out_{i}_dram"] for i in range(len(_OUTS)))
```
